# Optimizing a Trainium2 kernel written in Bass

```python
import math
import jax, jax.numpy as jnp
from jax import lax
import numpy as np

D_MODEL = 1024
BATCH = 1
SEQ = 256
DEPTH = 1

HGRN_HEADS = 4
HGRN_DK = 128
HGRN_DV = 128
HGRN_WIDTH = HGRN_HEADS * HGRN_DK
HGRN_CHUNK = 64
ATT_HEADS = 8
ATT_DH = 64
ATT_WIDTH = ATT_HEADS * ATT_DH
IDX_HEADS = 8
IDX_DH = 64
TOPK_MAX = 256
Q_BLOCK = 128
REL_BUCKETS = 32
REL_MAX_DIST = 128
N_EXPERTS = 32
TOP_K = 4
D_FF = 1024
SWIGLU_ALPHA = 1.702
SWIGLU_LIMIT = 7.0
MOE_BLOCK = 256
NORM_EPS = 1e-6
N_MOD = 6

IN_WIDTHS = (
    HGRN_WIDTH, HGRN_WIDTH, HGRN_HEADS * HGRN_DV, HGRN_HEADS * HGRN_DV,
    ATT_WIDTH, ATT_DH, ATT_DH,
    IDX_HEADS * IDX_DH, IDX_DH, IDX_HEADS,
    D_MODEL, D_MODEL,
)
IN_COLS = sum(IN_WIDTHS)

kernel_name = "hybrid_hgrn2_dsa_moe_adaln"

def rms_norm(x, w):
    xf = x.astype(jnp.float32)
    y = xf * lax.rsqrt(jnp.mean(xf * xf, axis=-1, keepdims=True) + NORM_EPS)
    return (y * w.astype(jnp.float32)).astype(x.dtype)

def split_columns(z):
    parts, off = [], 0
    for w in IN_WIDTHS:
        parts.append(z[..., off:off + w])
        off += w
    return parts

def t5_bucket(rel):
    max_exact = REL_BUCKETS // 2
    rel_f = jnp.maximum(rel, 1).astype(jnp.float32)
    large = max_exact + (jnp.log(rel_f / max_exact) / math.log(REL_MAX_DIST / max_exact)
                         * (REL_BUCKETS - max_exact)).astype(jnp.int32)
    large = jnp.minimum(large, REL_BUCKETS - 1)
    return jnp.where(rel < max_exact, rel, large)

def hgrn2_chunk_scan(q, k, v, log_f):
    b_, seq_len, heads, dk = q.shape
    dv = v.shape[-1]
    n_chunks = seq_len // HGRN_CHUNK

    def to_chunks(t):
        return t.reshape(b_, n_chunks, HGRN_CHUNK, heads, t.shape[-1]).transpose(1, 0, 3, 2, 4)

    causal = jnp.tril(jnp.ones((HGRN_CHUNK, HGRN_CHUNK), bool))

    def step(state, inp):
        qc, kc, vc, gc = inp
        b = jnp.cumsum(gc, axis=2)
        diff = b[:, :, :, None, :] - b[:, :, None, :, :]
        decay = jnp.exp(jnp.where(causal[:, :, None], diff, -jnp.inf))
        a = jnp.einsum('bhtd,bhsd,bhtsd->bhts', qc, kc, decay)
        o = (jnp.einsum('bhts,bhsv->bhtv', a, vc)
             + jnp.einsum('bhtd,bhdv->bhtv', qc * jnp.exp(b), state))
        b_last = b[:, :, -1:, :]
        state = (jnp.exp(b_last[:, :, 0, :])[..., None] * state
                 + jnp.einsum('bhsd,bhsv->bhdv', kc * jnp.exp(b_last - b), vc))
        return state, o

    state0 = jnp.zeros((b_, heads, dk, dv), jnp.float32)
    _, o = lax.scan(step, state0, (to_chunks(q), to_chunks(k), to_chunks(v), to_chunks(log_f)))
    return o.transpose(1, 0, 3, 2, 4).reshape(b_, seq_len, heads, dv)

def hgrn2_branch(qa, fa, ia, ga, lb, norm_w):
    b_, seq_len, _ = qa.shape
    shp = (b_, seq_len, HGRN_HEADS, HGRN_DK)
    q = jax.nn.silu(qa.astype(jnp.float32)).reshape(shp)
    z = fa.astype(jnp.float32).reshape(shp)
    lbh = lb.reshape(HGRN_HEADS, HGRN_DK)
    log_f = jnp.logaddexp(jnp.log(lbh), jnp.log1p(-lbh) + jax.nn.log_sigmoid(z))
    k = (1.0 - lbh) * jax.nn.sigmoid(-z)
    v = ia.astype(jnp.float32).reshape(b_, seq_len, HGRN_HEADS, HGRN_DV)
    o = hgrn2_chunk_scan(q, k, v, log_f)
    o = o * lax.rsqrt(jnp.mean(o * o, axis=-1, keepdims=True) + NORM_EPS)
    o = o.reshape(b_, seq_len, HGRN_HEADS * HGRN_DV) * norm_w.astype(jnp.float32)
    return (o * jax.nn.silu(ga.astype(jnp.float32))).astype(qa.dtype)

def dsa_branch(qb, kb, vb, iq, ik, iw, rel_bias):
    b_, seq_len, _ = qb.shape
    top_k = min(TOPK_MAX, seq_len // 4)
    n_blocks = seq_len // Q_BLOCK
    q = qb.reshape(b_, seq_len, ATT_HEADS, ATT_DH)
    iq = iq.reshape(b_, seq_len, IDX_HEADS, IDX_DH).astype(jnp.float32)
    ik = ik.astype(jnp.float32)
    iw = iw.astype(jnp.float32) * (IDX_HEADS ** -0.5 * IDX_DH ** -0.5)
    key_pos = jnp.arange(seq_len)
    gather_rows = jax.vmap(lambda kv, ix: kv[ix])

    def block(i):
        start = i * Q_BLOCK
        t = start + jnp.arange(Q_BLOCK)
        q_b = lax.dynamic_slice_in_dim(q, start, Q_BLOCK, axis=1).astype(jnp.float32)
        iq_b = lax.dynamic_slice_in_dim(iq, start, Q_BLOCK, axis=1)
        iw_b = lax.dynamic_slice_in_dim(iw, start, Q_BLOCK, axis=1)
        s = jnp.einsum('bqhd,bsd->bqhs', iq_b, ik)
        score = jnp.einsum('bqh,bqhs->bqs', iw_b, jax.nn.relu(s))
        score = jnp.where(key_pos[None, None, :] <= t[None, :, None], score, -jnp.inf)
        _, idx = lax.top_k(score, top_k)
        valid = idx <= t[None, :, None]
        k_sel = gather_rows(kb, idx).astype(jnp.float32)
        v_sel = gather_rows(vb, idx).astype(jnp.float32)
        bias = rel_bias[t5_bucket(jnp.maximum(t[None, :, None] - idx, 0))]
        logits = (jnp.einsum('bqhd,bqkd->bqhk', q_b, k_sel) * ATT_DH ** -0.5
                  + bias.transpose(0, 1, 3, 2).astype(jnp.float32))
        logits = jnp.where(valid[:, :, None, :], logits, -jnp.inf)
        p = jax.nn.softmax(logits, axis=-1)
        return jnp.einsum('bqhk,bqkd->bqhd', p, v_sel).astype(qb.dtype)

    out = lax.map(block, jnp.arange(n_blocks))
    return out.transpose(1, 0, 2, 3, 4).reshape(b_, seq_len, ATT_WIDTH)

def mixer_block(h, w_in, lb, hgrn_norm_w, rel_bias, w_proj_a, w_proj_b, w_out):
    z = h @ w_in
    qa, fa, ia, ga, qb, kb, vb, iq, ik, iw, gate_a, gate_b = split_columns(z)
    y_a = hgrn2_branch(qa, fa, ia, ga, lb, hgrn_norm_w) @ w_proj_a
    y_b = dsa_branch(qb, kb, vb, iq, ik, iw, rel_bias) @ w_proj_b
    merged = jax.nn.sigmoid(gate_a) * y_a + jax.nn.sigmoid(gate_b) * y_b
    return merged @ w_out

def moe_block(h, w_router, b_router, w1, b1, w2, b2):
    n_tok, d = h.shape
    n_assign = n_tok * TOP_K
    logits = (h @ w_router + b_router).astype(jnp.float32)
    top_val, top_idx = lax.top_k(logits, TOP_K)
    gates = jax.nn.softmax(top_val, axis=-1).astype(h.dtype)
    flat_e = top_idx.reshape(-1)
    order = jnp.argsort(flat_e)
    sorted_e = flat_e[order]
    tok = order // TOP_K
    counts = jnp.bincount(flat_e, length=N_EXPERTS)
    padded = (counts + MOE_BLOCK - 1) // MOE_BLOCK * MOE_BLOCK
    pad_end = jnp.cumsum(padded)
    pad_start = pad_end - padded
    start = jnp.cumsum(counts) - counts
    dest = pad_start[sorted_e] + (jnp.arange(n_assign) - start[sorted_e])
    n_slots = -(-n_assign // MOE_BLOCK) * MOE_BLOCK + N_EXPERTS * MOE_BLOCK
    n_blk = n_slots // MOE_BLOCK
    slot_tok = jnp.full((n_slots,), n_tok, jnp.int32).at[dest].set(tok.astype(jnp.int32))
    h_pad = jnp.concatenate([h, jnp.zeros((1, d), h.dtype)], axis=0)
    xs = h_pad[slot_tok].reshape(n_blk, MOE_BLOCK, d)
    block_expert = jnp.minimum(
        jnp.searchsorted(pad_end, jnp.arange(n_blk) * MOE_BLOCK, side='right'), N_EXPERTS - 1)

    def expert_block(args):
        xb, e = args
        hm = xb @ w1[e] + b1[e]
        glu = jnp.minimum(hm[:, :D_FF], SWIGLU_LIMIT)
        lin = jnp.clip(hm[:, D_FF:], -SWIGLU_LIMIT, SWIGLU_LIMIT)
        act = glu * jax.nn.sigmoid(SWIGLU_ALPHA * glu) * (lin + 1.0)
        return act @ w2[e] + b2[e]

    y_slots = lax.map(expert_block, (xs, block_expert)).reshape(n_slots, d)
    dest_orig = jnp.zeros((n_assign,), jnp.int32).at[order].set(dest.astype(jnp.int32))
    y_sel = y_slots[dest_orig].reshape(n_tok, TOP_K, d)
    return jnp.einsum('tk,tkd->td', gates, y_sel)

def setup_inputs(seed: int = 0) -> dict:
    key = jax.random.key(seed)
    ks = jax.random.split(key, 20)

    def nrm(k, shape, fan_in, scale=1.0):
        return jax.random.normal(k, shape, jnp.float32) * (scale * fan_in ** -0.5)

    def gain(k, shape):
        return 1.0 + 0.02 * jax.random.normal(k, shape, jnp.float32)

    return {
        "x": jax.random.normal(ks[0], (BATCH, SEQ, D_MODEL), jnp.float32),
        "c": jax.random.normal(ks[1], (BATCH, D_MODEL), jnp.float32),
        "w_ada": nrm(ks[2], (DEPTH, D_MODEL, N_MOD * D_MODEL), D_MODEL, 0.5),
        "b_ada": 0.02 * jax.random.normal(ks[3], (DEPTH, N_MOD * D_MODEL), jnp.float32),
        "norm_mix_w": gain(ks[4], (DEPTH, D_MODEL)),
        "w_in": nrm(ks[5], (DEPTH, D_MODEL, IN_COLS), D_MODEL),
        "hgrn_lb_logits": 0.5 * jax.random.normal(ks[6], (DEPTH, HGRN_WIDTH), jnp.float32),
        "hgrn_norm_w": gain(ks[7], (DEPTH, HGRN_HEADS * HGRN_DV)),
        "rel_bias": 0.5 * jax.random.normal(ks[8], (REL_BUCKETS, ATT_HEADS), jnp.float32),
        "w_proj_a": nrm(ks[9], (DEPTH, HGRN_HEADS * HGRN_DV, D_MODEL), HGRN_HEADS * HGRN_DV),
        "w_proj_b": nrm(ks[10], (DEPTH, ATT_WIDTH, D_MODEL), ATT_WIDTH),
        "w_out": nrm(ks[11], (DEPTH, D_MODEL, D_MODEL), D_MODEL),
        "norm_ffn_w": gain(ks[12], (DEPTH, D_MODEL)),
        "w_router": nrm(ks[13], (DEPTH, D_MODEL, N_EXPERTS), D_MODEL),
        "b_router": 0.01 * jax.random.normal(ks[14], (DEPTH, N_EXPERTS), jnp.float32),
        "w_mlp1": nrm(ks[15], (DEPTH, N_EXPERTS, D_MODEL, 2 * D_FF), D_MODEL),
        "b_mlp1": 0.02 * jax.random.normal(ks[16], (DEPTH, N_EXPERTS, 2 * D_FF), jnp.float32),
        "w_mlp2": nrm(ks[17], (DEPTH, N_EXPERTS, D_FF, D_MODEL), D_FF),
        "b_mlp2": 0.02 * jax.random.normal(ks[18], (DEPTH, N_EXPERTS, D_MODEL), jnp.float32),
        "final_norm_w": gain(ks[19], (D_MODEL,)),
    }

def reference(x, c, w_ada, b_ada, norm_mix_w, w_in, hgrn_lb_logits, hgrn_norm_w, rel_bias,
              w_proj_a, w_proj_b, w_out, norm_ffn_w, w_router, b_router,
              w_mlp1, b_mlp1, w_mlp2, b_mlp2, final_norm_w):
    b_, seq_len, d = x.shape
    lb_all = jnp.cumsum(jax.nn.softmax(hgrn_lb_logits.astype(jnp.float32), axis=0), axis=0)
    lb_all = lb_all - lb_all[0]
    c_act = jax.nn.silu(c)
    for l in range(DEPTH):
        mod = c_act @ w_ada[l] + b_ada[l]
        shift_m, scale_m, gate_m, shift_f, scale_f, gate_f = jnp.split(mod, N_MOD, axis=-1)
        h = rms_norm(x, norm_mix_w[l]) * (1.0 + scale_m[:, None, :]) + shift_m[:, None, :]
        y = mixer_block(h, w_in[l], lb_all[l], hgrn_norm_w[l], rel_bias,
                        w_proj_a[l], w_proj_b[l], w_out[l])
        x = x + gate_m[:, None, :] * y
        h = rms_norm(x, norm_ffn_w[l]) * (1.0 + scale_f[:, None, :]) + shift_f[:, None, :]
        y = moe_block(h.reshape(b_ * seq_len, d), w_router[l], b_router[l],
                      w_mlp1[l], b_mlp1[l], w_mlp2[l], b_mlp2[l])
        x = x + gate_f[:, None, :] * y.reshape(b_, seq_len, d)
    return rms_norm(x, final_norm_w)


_drawn_inputs = setup_inputs


def setup_inputs(seed=0):
    import zlib

    import numpy as np

    out = dict(_drawn_inputs(seed))
    spreads = {}
    factors = {'norm_mix_w': 5.454,
     'hgrn_norm_w': 8.0,
     'norm_ffn_w': 13.903,
     'b_router': 34.135,
     'b_mlp1': 25.035,
     'b_mlp2': 64.0,
     'final_norm_w': 7.822,
     'rel_bias': 4.315}
    for name, (base, spread) in spreads.items():
        noise = np.random.default_rng([zlib.crc32(name.encode()), seed]).standard_normal(out[name].shape)
        drawn = base * np.exp(spread * noise) if base else spread * noise
        out[name] = __import__('jax').numpy.asarray(drawn.astype(out[name].dtype))
    for name, factor in factors.items():
        out[name] = (out[name] * factor).astype(out[name].dtype)
    return out
```

```python
from contextlib import ExitStack

import concourse.bass as bass
from concourse import mybir

P = 128
F32 = mybir.dt.float32
F32R = mybir.dt.float32r
BF16 = mybir.dt.bfloat16
I32 = mybir.dt.int32
U8 = mybir.dt.uint8
ALU = mybir.AluOpType
ACT = mybir.ActivationFunctionType
AX_X = mybir.AxisListType.X

EPS = 1e-6
HGRN_H, HGRN_D = 4, 128
ATT_H, ATT_D = 8, 64
TOPK = 64
TOP_E = 4
LIMIT, ALPHA = 7.0, 1.702
SLOTS = 64
MAX_MORE = 15
DEAD, PICKED = -1.0e30, -3.0e38
MIX_RING = 6
RING = 12
PARTS = 4
HALVES = (64, 32, 16, 8, 4, 2, 1)

Z_BLOCKS = (
    [("T", 2688 + 256 * i, 256) for i in range(2)]
    + [("IK", 3200, 72), ("KV", 2560, 128)]
    + [("T", 2048 + 256 * i, 256) for i in range(2)]
    + [("T", 512 + 256 * i, 256) for i in range(2)]
    + [("T", 256 * i, 256) for i in range(2)]
    + [("N", 1024 + 256 * i, 256) for i in range(2)]
    + [("N", 1536 + 256 * i, 256) for i in range(2)]
    + [("GATE", 3272 + 256 * i, 256) for i in range(8)]
)
Z_IQ, Z_IK, Z_KV, Z_QB, Z_F, Z_Q, Z_V, Z_G, Z_GATE = 0, 2, 3, 4, 6, 8, 10, 12, 14


def mixer_stream():
    tiles = [("ada", n) for n in range(8)]
    for n in range(len(Z_BLOCKS)):
        tiles.append(("in", n))
        if n < 16:
            tiles.append(("ada", 8 + n))
    tiles += [("pa", 0), ("pb", 0), ("pa", 1), ("pb", 1)]
    tiles += [("out", n) for n in range(4)]
    return tiles


def build(nc, x, c, w_ada, b_ada, norm_mix_w, w_in, hgrn_lb_logits, hgrn_norm_w, rel_bias, w_proj_a,
          w_proj_b, w_out, norm_ffn_w, w_router, b_router, w_mlp1, b_mlp1, w_mlp2, b_mlp2,
          final_norm_w, k_ident, k_fold, k_bucket, k_masks, k_iota, k_upper, k_more, out):
    T, D = x.shape[1], x.shape[2]
    TT, KC = T // P, D // P
    NE, FF2 = w_mlp1.shape[1], w_mlp1.shape[3]
    FF = FF2 // 2
    assert (T, D, TT, KC, NE, FF) == (256, 1024, 2, 8, 32, 1024)

    stream = mixer_stream()
    place = {key: (n % MIX_RING, 16 * (n // MIX_RING + 1)) for n, key in enumerate(stream)}
    MIX_ROUNDS = len(stream) // MIX_RING
    assert len(stream) % MIX_RING == 0

    bias_dram = nc.dram_tensor("bias_rows", [ATT_H, P, 384], F32, kind="Internal").ap()

    ctx = ExitStack()
    with ctx:
        def sem(name):
            return ctx.enter_context(nc.semaphore(name))

        def sb(name, shape, dt, stack=ctx):
            return stack.enter_context(nc.sbuf_tensor(name, shape, dt))

        ident = sb("ident", [P, P], F32)
        fold = sb("fold", [P, P], F32)
        iota = sb("iota", [P, 256], F32)
        x_sb = sb("x_sb", [P, TT, D], F32)
        h = sb("h", [P, TT, D], F32)
        hT = sb("hT", [P, KC, T], F32)
        mod = sb("mod", [P, 3, D], F32)
        gate_f = sb("gate_f", [P, D], F32)
        norm_w = sb("norm_w", [P, D], F32)
        raw_a = sb("raw_a", [P, MIX_RING, 2048], F32)
        route = sb("route", [P, TT, 8, NE], F32)
        small = sb("small", [P, 64], F32)
        lists = sb("lists", [1, 64], F32)
        lists_i = sb("lists_i", [1, 64], I32)

        mix = ExitStack()
        with mix:
            bias = sb("bias", [P, 3, ATT_H, P], F32, mix)
            relu = sb("relu", [P, 2, 512], F32, mix)
            score = sb("score", [P, TT, T], F32, mix)
            pT = sb("pT", [P, 3, ATT_H, P], F32, mix)
            decay = sb("decay", [P, HGRN_H, T], F32, mix)
            level_e = sb("level_e", [P, HGRN_H, T], F32, mix)
            level_x = sb("level_x", [P, 2, HGRN_H, T], F32, mix)
            aT = sb("aT", [P, 2, HGRN_H, P], F32, mix)
            aT_off = sb("aT_off", [P, HGRN_H, P], F32, mix)
            z = sb("z", [P, len(Z_BLOCKS), 512], F32, mix)
            acc = sb("acc", [P, 2, D], F32, mix)
            masks = sb("masks", [P, 8, P], U8, mix)
            upper = sb("upper", [P, 2, P], F32, mix)
            onw = sb("onw", [P, 512], F32, mix)
            lb = sb("lb", [P, 4, HGRN_H], F32, mix)
            wr = sb("wr", [P, KC, NE], F32, mix)
            br = sb("br", [P, NE], F32, mix)
            cc = sb("cc", [P, 4, KC], F32, mix)
            more_c = sb("more_c", [96, 4], F32, mix)
        bucket = pT[0:32, 0, 0:3, :].rearrange("p a n -> p (a n)")
        brow = pT[0:ATT_H, 1, 0:3, :].rearrange("p a n -> p (a n)")
        relb = pT[0:32, 2, 0, 0:ATT_H]
        moe = ctx
        raw_b = sb("raw_b", [P, RING - MIX_RING, 2048], F32, moe)
        w_hi = sb("w_hi", [P, PARTS, 1024], F32R, moe)
        w_lo = sb("w_lo", [P, PARTS, 1024], F32R, moe)
        xs = sb("xs", [P, KC, P], F32R, moe)
        act = sb("act", [P, KC, P], F32R, moe)
        h_parts = sb("h_parts", [P, TT, 3, D], BF16, moe)
        b1T = sb("b1T", [P, NE * 16], F32, moe)
        st = sb("st", [P, T], F32, moe)
        pick = sb("pick", [P, TT, SLOTS], BF16, moe)
        pick_g = sb("pick_g", [P, TT, P], F32, moe)
        glu = sb("glu", [P, 4, SLOTS], F32, moe)
        lin = sb("lin", [P, 4, SLOTS], F32, moe)
        sig = sb("sig", [P, 4, SLOTS], F32, moe)
        act32 = sb("act32", [P, 4, SLOTS], F32, moe)
        hs = h[:, 0, :].rearrange("p (b n) -> p b n", b=2)
        ysb = h[:, 1, :]
        yacc = hT[:, :, :].rearrange("p k t -> p (k t)").rearrange("p (a n) -> p a n", a=TT)

        ps = ctx.enter_context(nc.psum_tensor("ps", [P, 8, 512], F32))

        ld_first = sem("ld_first")
        ld_small = sem("ld_small")
        ld_x = sem("ld_x")
        ld_bada = [sem(f"ld_bada{n}") for n in range(6)]
        ld_ffn = sem("ld_ffn")
        ld_fin = sem("ld_fin")
        ld_b = sem("ld_b")
        raw_full = [sem(f"raw_full{s}") for s in range(RING)]
        ada_used = sem("ada_used")
        dve_step = sem("dve_step")
        act_step = sem("act_step")
        pool_step = sem("pool_step")
        c_exp = sem("c_exp")
        acc_ready = sem("acc_ready")
        ada_mm = sem("ada_mm")
        mod_ready = sem("mod_ready")
        sq_done = sem("sq_done")
        ln_in = sem("ln_in")
        ln_out = sem("ln_out")
        h_ready = sem("h_ready")
        tr_mm = sem("tr_mm")
        hT_ready = sem("hT_ready")
        z_mm = sem("z_mm")
        z_ready = sem("z_ready")
        bias_mm = sem("bias_mm")
        brow_ready = sem("brow_ready")
        brow_out = sem("brow_out")
        bias_in = sem("bias_in")
        score_mm = sem("score_mm")
        relu_ready = sem("relu_ready")
        relu_used = sem("relu_used")
        score_sum = sem("score_sum")
        score_causal = sem("score_causal")
        picked = sem("picked")
        pick_causal = sem("pick_causal")
        logit_mm = sem("logit_mm")
        logit_ready = sem("logit_ready")
        max_ready = sem("max_ready")
        probs_ready = sem("probs_ready")
        pT_mm = sem("pT_mm")
        pT_ready = sem("pT_ready")
        av_mm = sem("av_mm")
        ob_ready = sem("ob_ready")
        hg_exp = sem("hg_exp")
        hg_lin = sem("hg_lin")
        lvl_d = sem("lvl_d")
        lvl_e = sem("lvl_e")
        lvl_x = sem("lvl_x")
        lvl_mm = sem("lvl_mm")
        lvl_at = sem("lvl_at")
        o_mm = sem("o_mm")
        o_sq = sem("o_sq")
        oa_ready = sem("oa_ready")
        br_mm = sem("br_mm")
        brT_ready = sem("brT_ready")
        gates_ready = sem("gates_ready")
        proj_mm = sem("proj_mm")
        merged = sem("merged")
        mT_mm = sem("mT_mm")
        mT_ready = sem("mT_ready")
        out_mm = sem("out_mm")
        out_used = sem("out_used")
        h2_ready = sem("h2_ready")
        h2_mm = sem("h2_mm")
        h2T_ready = sem("h2T_ready")
        rt_mm = sem("rt_mm")
        rt_max = sem("rt_max")
        rt_exp = sem("rt_exp")
        rt_sel = sem("rt_sel")
        pos_mm = sem("pos_mm")
        cnt_ready = sem("cnt_ready")
        flag_ready = sem("flag_ready")
        flag_mm = sem("flag_mm")
        hot_ready = sem("hot_ready")
        list_mm = sem("list_mm")
        list_ready = sem("list_ready")
        b1_mm = sem("b1_mm")
        b1_ready = sem("b1_ready")
        gT_mm = sem("gT_mm")
        gT_ready = sem("gT_ready")
        b2_mm = sem("b2_mm")
        y_start = sem("y_start")
        parts_ready = sem("parts_ready")
        hi_ready = sem("hi_ready")
        lo_ready = sem("lo_ready")
        w_free = sem("w_free")
        pick_ready = sem("pick_ready")
        pickg_ready = sem("pickg_ready")
        gather_mm = sem("gather_mm")
        xhi_ready = sem("xhi_ready")
        xs_ready = sem("xs_ready")
        st_mm = sem("st_mm")
        st_ready = sem("st_ready")
        hs_ready = sem("hs_ready")
        sum_mm = sem("sum_mm")
        glu_ready = sem("glu_ready")
        sig_ready = sem("sig_ready")
        a32_ready = sem("a32_ready")
        ahi_ready = sem("ahi_ready")
        act_ready = sem("act_ready")
        t_free = sem("t_free")
        ysb_ready = sem("ysb_ready")
        sc_mm = sem("sc_mm")
        y_added = sem("y_added")
        moe_step = sem("moe_step")
        fin_sq = sem("fin_sq")
        fin_ready = sem("fin_ready")
        st_out = sem("st_out")

        N_FIRST, N_SMALL = 2, 14
        bada_rows = b_ada[0].rearrange("(s n) -> s n", n=D)
        BADA_DST = [mod[:, 0, :], mod[:, 1, :], mod[:, 2, :], mod[:, 0, :], mod[:, 1, :], gate_f[:, :]]

        def raw(s):
            return raw_a[:, s, :] if s < MIX_RING else raw_b[:, s - MIX_RING, :]

        def tile_src(kind, n):
            if kind == "ada":
                return w_ada[0].rearrange("(p j) n -> p j n", j=KC)[:, :, 256 * n:256 * n + 256]
            if kind == "in":
                _, c0, w = Z_BLOCKS[n]
                return w_in[0].rearrange("(k p) n -> p k n", p=P)[:, :, c0:c0 + w]
            if kind in ("pa", "pb"):
                w = (w_proj_a if kind == "pa" else w_proj_b)[0]
                return w.rearrange("(k p) n -> p k n", p=P)[:, :, 512 * n:512 * n + 512]
            return w_out[0].rearrange("(k p) n -> p k n", p=P)[:, :, 256 * n:256 * n + 256]

        def tile_at(kind, n):
            s, full = place[(kind, n)]
            a, w = tile_src(kind, n).shape[1:]
            return raw(s)[:, 0:a * w].rearrange("p (a w) -> p a w", a=a), raw_full[s], full

        w1_v = w_mlp1[0].rearrange("e (k p) n -> p e k n", p=P)
        w2_v = w_mlp2[0].rearrange("e (k p) n -> p e k n", p=P)
        W1_COL = [0, FF, 512, FF + 512]

        block = ctx.enter_context(nc.Block())

        @block.sync
        def _(sp):
            def slot_read(kind, i):
                if kind == "ada":
                    sp.wait_ge(ada_used, i + 1)
                elif kind == "in":
                    sp.wait_ge(z_mm, i + 1)
                elif kind == "out":
                    sp.wait_ge(out_mm, i + 1)
                else:
                    sp.wait_ge(proj_mm, 2 * i + 2)

            for n, (kind, i) in enumerate(stream):
                if n >= MIX_RING:
                    slot_read(*stream[n - MIX_RING])
                dst, full, _ = tile_at(kind, i)
                sp.dma_start(dst, tile_src(kind, i)).then_inc(full, 16)

            def expert_tile(e, q):
                dst = raw(q)
                if q < 8:
                    c0 = W1_COL[q // 2]
                    src = w1_v[:, bass.ds(e, 1), 4 * (q % 2):4 * (q % 2) + 4, c0:c0 + 512]
                    dst = dst.rearrange("p (k n) -> p k n", k=4)
                else:
                    src = w2_v[:, bass.ds(e, 1), 2 * (q - 8):2 * (q - 8) + 2, :]
                    dst = dst.rearrange("p (k n) -> p k n", k=2)
                sp.dma_start(dst, src.rearrange("p e k n -> p (e k) n")).then_inc(raw_full[q], 16)

            for q in range(RING):
                if q < MIX_RING:
                    slot_read(*stream[len(stream) - MIX_RING + q])
                if q == MIX_RING:
                    sp.wait_ge(av_mm, 2)
                    sp.wait_ge(o_mm, 2)
                    sp.wait_ge(oa_ready, 2)
                    sp.wait_ge(ob_ready, 2)
                expert_tile(0, q)
            with sp.Fori(1, NE) as i:
                for q in range(RING):
                    sp.wait_ge(lo_ready, i * 24 + (2 * q + 2 - 24))
                    expert_tile(i, q)
            sp.wait_ge(list_ready, 1)
            n_more = sp.value_load(lists_i[0:1, 0:1], min_val=0, max_val=MAX_MORE)
            with sp.If(n_more > 0):
                with sp.Fori(0, n_more) as r:
                    e = sp.value_load(lists_i[0:1, bass.ds(r + 1, 1)], min_val=0, max_val=NE - 1)
                    for q in range(RING):
                        sp.wait_ge(lo_ready, r * 24 + (24 * (NE - 1) + 2 * q + 2))
                        expert_tile(e, q)
            for tt in range(TT):
                sp.wait_ge(fin_ready, tt + 1)
                sp.dma_start(out[0, tt * P:(tt + 1) * P, :], h[:, tt, :]).then_inc(st_out, 16)
            sp.wait_ge(st_out, 32)

        @block.gpsimd
        def _(pool):
            small_loads = [
                (fold[:, :], k_fold), (iota[:, :], k_iota),
                (bucket, k_bucket), (relb, rel_bias),
                (z[:, 20:22, :].rearrange("p a n -> p (a n)"), k_masks),
                (upper[:, :, :], k_upper.rearrange("p (a n) -> p a n", a=2)),
                (onw[:, :], hgrn_norm_w[0:1, :].broadcast_to([P, 512])),
                (wr[:, :, :], w_router[0].rearrange("(k p) n -> p k n", p=P)),
                (br[:, :], b_router[0:1, :].broadcast_to([P, NE])),
                (more_c[:, :], k_more),
                (norm_w[:, :], norm_mix_w[0:1, :].broadcast_to([P, D])),
            ]
            for dst, src in small_loads:
                pool.dma_start(dst, src).then_inc(ld_small, 16)
            for n in range(3):
                pool.dma_start(BADA_DST[n], bada_rows[n:n + 1, :].broadcast_to([P, D])).then_inc(ld_bada[n], 16)
            assert len(small_loads) + 3 == N_SMALL

            pool.wait_ge(brow_ready, 1)
            pool.dma_start(bias_dram, brow.rearrange("h (o j) -> h o j", o=1).broadcast_to([ATT_H, P, 384])).then_inc(brow_out, 16)
            pool.wait_ge(brow_out, 16)
            for n, (tt, st_) in enumerate(((0, 0), (1, 0), (1, 1))):
                src = bass.AP(tensor=bias_dram.tensor, offset=255 - tt * P + st_ * P,
                              ap=[[383, P], [384 * P, ATT_H], [1, P]])
                pool.dma_start(bias[:, n, :, :], src).then_inc(bias_in, 16)

            pool.wait_ge(h_ready, 2)
            for n in range(3, 6):
                pool.dma_start(BADA_DST[n], bada_rows[n:n + 1, :].broadcast_to([P, D])).then_inc(ld_bada[n], 16)
            pool.dma_start(norm_w[:, :], norm_ffn_w[0:1, :].broadcast_to([P, D])).then_inc(ld_ffn, 16)

            for tt in range(TT):
                S = (tt + 1) * P
                pool.wait_ge(score_sum, tt + 1)
                nc.gpsimd.affine_select(out=score[:, tt, 0:S], in_=score[:, tt, 0:S], compare_op=ALU.is_ge,
                                        fill=DEAD, base=tt * P, pattern=[[-1, S]],
                                        channel_multiplier=1).then_inc(score_causal, 1)
            for tt in range(TT):
                S = (tt + 1) * P
                pool.wait_ge(picked, tt + 1)
                nc.gpsimd.affine_select(out=score[:, tt, 0:S], in_=score[:, tt, 0:S], compare_op=ALU.is_ge,
                                        fill=DEAD, base=tt * P, pattern=[[-1, S]],
                                        channel_multiplier=1).then_inc(pick_causal, 1)
            pool.wait_ge(merged, 4)
            pool.dma_start(z[:, 16:17, :].rearrange("p a (m n) -> p (a m) n", m=4),
                           b_mlp1[0].rearrange("e (c n) -> (e c) n", n=P)
                           .rearrange("(m p) n -> p m n", p=P)).then_inc(ld_b, 16)
            pool.dma_start(z[0:NE, 10:12, :].rearrange("p a n -> p (a n)"), b_mlp2[0]).then_inc(ld_b, 16)
            pool.wait_ge(h2_ready, 2)
            pool.dma_start(norm_w[:, :], final_norm_w.rearrange("(a n) -> a n", a=1).broadcast_to([P, D])).then_inc(ld_fin, 16)
            for s in (ld_small,):
                pool.wait_ge(s, 16 * N_SMALL - 48)

        @block.scalar
        def _(a):
            a.dma_start(cc[:, 0, :], c[0].rearrange("(p j) -> p j", j=KC)).then_inc(ld_first, 16)
            a.dma_start(ident[:, :], k_ident).then_inc(ld_first, 16)
            a.dma_start(x_sb[:, :, :], x[0].rearrange("(t p) d -> p t d", p=P)).then_inc(ld_x, 16)
            a.dma_start(lb[:, 0, :], hgrn_lb_logits[0].rearrange("(h d) -> d h", d=P), allow_slow_non_contiguous=True).then_inc(ld_x, 16)

            count = [0]

            def step(ins):
                count[0] += 1
                ins.then_inc(act_step, 1)
                a.wait_ge(act_step, count[0])

            a.wait_ge(ld_first, 16 * N_FIRST)
            nc.scalar.activation(cc[:, 1, :], cc[:, 0, :], ACT.Exp, scale=-1.0).then_inc(c_exp, 1)
            a.wait_ge(ld_x, 32)

            def norm_square(tt):
                nc.scalar.activation(h[:, tt, :], x_sb[:, tt, :], ACT.Square,
                                     accum_out=small[:, 8 * tt:8 * tt + 1]).then_inc(sq_done, 1)

            def rsqrt_guess(n, lo, w):
                a.wait_ge(ln_in, n)
                step(nc.scalar.activation(small[:, lo + w:lo + 2 * w], small[:, lo:lo + w], ACT.Ln))
                nc.scalar.activation(small[:, lo + 2 * w:lo + 3 * w], small[:, lo + w:lo + 2 * w], ACT.Exp,
                                     scale=-0.5).then_inc(ln_out, 1)

            def copy_T(src_banks, dst, tt, sig):
                for g in range(2):
                    nc.scalar.activation(dst[:, 4 * g:4 * g + 4, tt * P:(tt + 1) * P],
                                         ps[:, src_banks + g, :].rearrange("p (k t) -> p k t", k=4),
                                         ACT.Copy).then_inc(sig, 1)

            for tt in range(TT):
                norm_square(tt)
            for tt in range(TT):
                rsqrt_guess(tt + 1, 8 * tt + 1, 1)
            for tt in range(TT):
                a.wait_ge(tr_mm, tt + 1)
                copy_T(2 * tt, hT, tt, hT_ready)

            a.wait_ge(bias_mm, 1)
            nc.scalar.activation(brow, ps[0:ATT_H, 6, 0:384], ACT.Copy).then_inc(brow_ready, 1)

            def evac_z(n):
                a.wait_ge(z_mm, n + 1)
                bank = ps[:, n % 2, :]
                kind = Z_BLOCKS[n][0]
                if kind == "IK":
                    nc.scalar.activation(z[0:64, n, 0:T], bank[0:64, 0:T], ACT.Copy)
                    nc.scalar.activation(z[64:128, n, 0:T], bank[0:64, 0:T], ACT.Copy)
                    nc.scalar.activation(z[:, n, T:T + 16], bank[:, T:T + 16], ACT.Copy,
                                         scale=ATT_H ** -0.5 * ATT_D ** -0.5).then_inc(z_ready, 1)
                elif kind == "KV":
                    nc.scalar.activation(z[0:64, n, 0:T], bank[0:64, 0:T], ACT.Copy)
                    nc.scalar.activation(z[64:128, n, 0:T], bank[0:64, 0:T], ACT.Copy)
                    nc.scalar.activation(z[:, n, T:T + 128], bank[:, T:T + 128], ACT.Copy).then_inc(z_ready, 1)
                elif kind == "GATE":
                    nc.scalar.activation(z[:, n, :], bank, ACT.Exp, scale=-1.0).then_inc(z_ready, 1)
                else:
                    nc.scalar.activation(z[:, n, :], bank, ACT.Copy).then_inc(z_ready, 1)

            for n in range(6):
                evac_z(n)
            for u in range(8):
                S = (u // 4 + 1) * P
                a.wait_ge(score_mm, u + 1)
                if u >= 2:
                    a.wait_ge(relu_used, u - 1)
                nc.scalar.activation(relu[:, u % 2, 0:2 * S], ps[:, 2 + u % 2, 0:2 * S], ACT.Relu).then_inc(relu_ready, 1)
            for n in range(6, 10):
                evac_z(n)
            zf = z[:, Z_F:Z_F + 2, :].rearrange("p a n -> p (a n)")
            zq = z[:, Z_Q:Z_Q + 2, :].rearrange("p a n -> p (a n)")
            le = level_e[:, :, :].rearrange("p h t -> p (h t)")
            lx0 = level_x[:, 0, :, :].rearrange("p h t -> p (h t)")
            lx1 = level_x[:, 1, :, :].rearrange("p h t -> p (h t)")
            a.wait_ge(z_ready, 10)
            step(nc.scalar.activation(le, zf, ACT.Abs))
            step(nc.scalar.activation(le, le, ACT.Exp, scale=-1.0))
            nc.scalar.activation(le, le, ACT.Ln, bias=1.0).then_inc(hg_exp, 1)
            nc.scalar.activation(lx0, zq, ACT.Exp, scale=-1.0).then_inc(hg_exp, 1)
            evac_z(10)
            evac_z(11)
            evac_z(12)
            evac_z(13)
            a.wait_ge(hg_lin, 1)
            nc.scalar.activation(lx1, lx1, ACT.Exp, scale=-1.0).then_inc(hg_exp, 1)
            for n in range(1 + len(HALVES)):
                a.wait_ge(lvl_d, n + 1)
                nc.scalar.activation(le, le, ACT.Exp).then_inc(lvl_e, 1)
            a.wait_ge(max_ready, 1)
            for tt in range(TT):
                for hd in range(ATT_H):
                    if tt == 0:
                        nc.scalar.activation(bias[:, 0, hd, :], bias[:, 0, hd, :], ACT.Exp,
                                             bias=small[:, 32 + hd:33 + hd],
                                             accum_out=small[:, 48 + hd:49 + hd]).then_inc(probs_ready, 1)
                    else:
                        nc.scalar.activation(bias[:, 1:3, hd, :], bias[:, 1:3, hd, :], ACT.Exp,
                                             bias=small[:, 40 + hd:41 + hd],
                                             accum_out=small[:, 56 + hd:57 + hd]).then_inc(probs_ready, 1)
            for n in range(14, 18):
                evac_z(n)
            a.wait_ge(brow_out, 16)
            for u in range(6):
                a.wait_ge(pT_mm, u + 1)
                nc.scalar.activation(pT[:, u // 2, 4 * (u % 2):4 * (u % 2) + 4, :],
                                     ps[:, 2 + u % 2, :].rearrange("p (h t) -> p h t", h=4),
                                     ACT.Copy).then_inc(pT_ready, 1)
            obT = acc[:, 0, :].rearrange("p (k t) -> p k t", k=4)
            oaT = acc[:, 1, :].rearrange("p (k t) -> p k t", k=4)
            a.wait_ge(mod_ready, 6)
            for tt in range(TT):
                a.wait_ge(br_mm, tt + 1)
                nc.scalar.activation(obT[:, :, tt * P:(tt + 1) * P],
                                     ps[:, 2 + tt, :].rearrange("p (k t) -> p k t", k=4), ACT.Copy).then_inc(brT_ready, 1)
            for tt in range(TT):
                a.wait_ge(o_mm, tt + 1)
                for hd in range(HGRN_H):
                    nc.scalar.activation(level_x[:, tt, hd, 0:P], ps[:, 4 + tt, hd * P:(hd + 1) * P], ACT.Square,
                                         accum_out=small[:, 16 + 4 * tt + hd:17 + 4 * tt + hd]).then_inc(o_sq, 1)
            a.wait_ge(z_ready, 14)
            nc.scalar.activation(le, z[:, Z_G:Z_G + 2, :].rearrange("p a n -> p (a n)"), ACT.Exp, scale=-1.0).then_inc(hg_exp, 1)
            rsqrt_guess(3, 16, 8)
            for tt in range(TT):
                a.wait_ge(br_mm, 2 + tt + 1)
                nc.scalar.activation(oaT[:, :, tt * P:(tt + 1) * P],
                                     ps[:, 2 + tt, :].rearrange("p (k t) -> p k t", k=4), ACT.Copy).then_inc(brT_ready, 1)
            for n in range(18, 22):
                evac_z(n)
            for tt in range(TT):
                a.wait_ge(mT_mm, tt + 1)
                copy_T(4 + 2 * tt, hT, tt, mT_ready)
            for tt in range(TT):
                a.wait_ge(out_used, 4)
                norm_square(tt)
            for tt in range(TT):
                rsqrt_guess(4 + tt, 8 * tt + 1, 1)
            for tt in range(TT):
                a.wait_ge(h2_mm, tt + 1)
                copy_T(4 + 2 * tt, hT, tt, h2T_ready)
            for tt in range(TT):
                a.wait_ge(rt_max, tt + 1)
                nc.scalar.activation(route[:, tt, 2, :], route[:, tt, 0, :], ACT.Exp,
                                     bias=small[:, 32 + tt:33 + tt]).then_inc(rt_exp, 1)
            a.wait_ge(b1_mm, 1)
            nc.scalar.activation(b1T[:, :], ps[:, 3, :], ACT.Copy).then_inc(b1_ready, 1)

            a.wait_ge(y_start, 4)
            a.wait_ge(parts_ready, 2)
            def split_hi(g24, u):
                tile_round[0](u)
                a.wait_ge(w_free, g24 + (u + 1))
                src = raw(u // 2)[:, 1024 * (u % 2):1024 * (u % 2) + 1024]
                nc.scalar.activation(w_hi[:, u % PARTS, :], src, ACT.Copy).then_inc(hi_ready, 1)

            tile_round = [None]

            def body(g):
                g24 = g * 24

                def arrived(u):
                    if u % 2 == 0:
                        q = u // 2
                        a.wait_ge(raw_full[q], g * 16 + (16 * MIX_ROUNDS + 16 if q < MIX_RING else 16))
                tile_round[0] = arrived

                def evac_h(b):
                    a.wait_ge(w_free, g24 + (PARTS + 4 * b + 4))
                    if b >= 2:
                        a.wait_ge(sum_mm, g * 4 + (b - 1))
                    nc.scalar.activation(hs[:, b % 2, :], ps[:, b % 2, :], ACT.Copy).then_inc(hs_ready, 1)

                def sigmoid(half):
                    a.wait_ge(glu_ready, g * 2 + (half + 1))
                    nc.scalar.activation(sig[:, :, :], glu[:, :, :], ACT.Sigmoid, scale=ALPHA).then_inc(sig_ready, 1)

                def act_hi(half):
                    a.wait_ge(a32_ready, g * 2 + (half + 1))
                    nc.scalar.activation(act[:, 4 * half:4 * half + 4, 0:SLOTS], act32[:, :, :], ACT.Copy).then_inc(ahi_ready, 1)

                a.wait_ge(gather_mm, g + 1)
                nc.scalar.activation(xs[:, :, 0:SLOTS], ps[:, 6, :].rearrange("p (k s) -> p k s", k=KC),
                                     ACT.Copy).then_inc(xhi_ready, 1)
                a.wait_ge(st_mm, g + 1)
                nc.scalar.activation(st[:, :], ps[:, 7, 0:T], ACT.Copy).then_inc(st_ready, 1)
                for u in range(24):
                    split_hi(g24, u)
                    if u in (5, 9, 13, 17):
                        evac_h((u - 5) // 4)
                    if u == 11:
                        sigmoid(0)
                    if u == 13:
                        act_hi(0)
                    if u == 19:
                        sigmoid(1)
                    if u == 21:
                        act_hi(1)
                a.wait_ge(w_free, g24 + (PARTS + 24))
                nc.scalar.activation(ysb[:, 0:512], ps[:, 4, :], ACT.Copy).then_inc(ysb_ready, 1)
                nc.scalar.activation(ysb[:, 512:1024], ps[:, 5, :], ACT.Copy).then_inc(ysb_ready, 1)

            with a.Fori(0, NE) as i:
                body(i)
            a.wait_ge(list_ready, 1)
            n_more = a.value_load(lists_i[0:1, 0:1], min_val=0, max_val=MAX_MORE)
            with a.If(n_more > 0):
                with a.Fori(0, n_more) as r:
                    body(r + NE)
            for tt in range(TT):
                a.wait_ge(fin_sq, tt + 1)
                norm_square(tt)
            for tt in range(TT):
                rsqrt_guess(6 + tt, 8 * tt + 1, 1)

        @block.vector
        def _(v):
            count = [0]

            def step(ins):
                count[0] += 1
                ins.then_inc(dve_step, 1)
                v.wait_ge(dve_step, count[0])

            def after(sem_, n, ins):
                ins.then_inc(sem_, 1)
                v.wait_ge(sem_, n)

            V = nc.vector
            v.wait_ge(c_exp, 1)
            step(V.tensor_scalar(cc[:, 2, :], cc[:, 1, :], 1.0, None, ALU.add))
            step(V.reciprocal(cc[:, 3, :], cc[:, 2, :]))
            step(V.tensor_tensor(cc[:, 1, :], cc[:, 0, :], cc[:, 3, :], ALU.mult))

            def ada_section(s):
                dst = acc[:, s % 2, :]
                if s >= 2:
                    v.wait_ge(ada_mm, s - 1)
                for n in range(4):
                    w, full, at = tile_at("ada", 4 * s + n)
                    v.wait_ge(full, at)
                    part = dst[:, 256 * n:256 * n + 256]
                    step(V.tensor_scalar(part, w[:, 0, :], cc[:, 1, 0:1], None, ALU.mult))
                    for j in range(1, KC):
                        ins = V.scalar_tensor_tensor(out=part, in0=w[:, j, :], scalar=cc[:, 1, j:j + 1], in1=part,
                                                     op0=ALU.mult, op1=ALU.add)
                        if j < KC - 1:
                            step(ins)
                        else:
                            after(ada_used, 4 * s + n + 1, ins)
                V.tensor_copy(small[:, 63:64], dst[:, 1023:1024]).then_inc(acc_ready, 1)

            def mod_section(s):
                v.wait_ge(ada_mm, s + 1)
                v.wait_ge(ld_bada[s], 16)
                for g in range(2):
                    dst = BADA_DST[s][:, 512 * g:512 * g + 512]
                    ins = V.tensor_tensor(dst, ps[:, 4 + g, :], dst, ALU.add)
                    if g == 0:
                        step(ins)
                    else:
                        after(mod_ready, s + 1, ins)

            def newton(n, lo, w, scale):
                val, guess, tmp = (small[:, lo + k * w:lo + (k + 1) * w] for k in range(3))
                step(V.tensor_scalar(val, val, scale, EPS, ALU.mult, ALU.add))
                V.tensor_copy(small[:, 62:63], val[:, 0:1]).then_inc(ln_in, 1)
                v.wait_ge(ln_out, n)
                r = tmp
                step(V.tensor_tensor(guess, r, r, ALU.mult))
                step(V.tensor_tensor(guess, guess, val, ALU.mult))
                step(V.tensor_scalar(guess, guess, -0.5, 1.5, ALU.mult, ALU.add))
                step(V.tensor_tensor(r, r, guess, ALU.mult))

            def norm(base, sq_n, shift, scale, sig):
                if scale is not None:
                    step(V.scalar_tensor_tensor(out=scale, in0=scale, scalar=1.0, in1=norm_w[:, :], op0=ALU.add, op1=ALU.mult))
                for tt in range(TT):
                    v.wait_ge(sq_done, sq_n + tt + 1)
                    step(V.tensor_copy(small[:, 8 * tt + 1:8 * tt + 2], small[:, 8 * tt:8 * tt + 1]))
                    newton(base + tt + 1, 8 * tt + 1, 1, 1.0 / D)
                    ins = V.scalar_tensor_tensor(out=h[:, tt, :], in0=x_sb[:, tt, :], scalar=small[:, 8 * tt + 3:8 * tt + 4],
                                                 in1=scale if scale is not None else norm_w[:, :],
                                                 op0=ALU.mult, op1=ALU.mult)
                    if shift is None:
                        after(sig, tt + 1, ins)
                    else:
                        step(ins)
                        after(sig, tt + 1, V.tensor_tensor(h[:, tt, :], h[:, tt, :], shift, ALU.add))

            v.wait_ge(ld_small, 16 * (N_SMALL - 3))
            step(V.tensor_copy(masks[:, :, :].rearrange("p a n -> p (a n)"), z[:, 20:22, :].rearrange("p a n -> p (a n)")))
            ada_section(0)
            ada_section(1)
            mod_section(0)
            mod_section(1)
            norm(0, 0, mod[:, 0, :], mod[:, 1, :], h_ready)
            step(V.tensor_tensor(lb[:, 1, :], lb[:, 0, :], lb[:, 0, :], ALU.subtract))
            step(V.tensor_scalar(lb[:, 2, :], lb[:, 1, :], 1.0, None, ALU.add))
            step(V.tensor_tensor(lb[:, 1, :], lb[:, 2, :], lb[:, 2, :], ALU.subtract))
            step(V.tensor_scalar(lb[:, 2, :], lb[:, 1, :], -1.0, 1.0, ALU.mult, ALU.add))
            ada_section(2)
            v.wait_ge(z_ready, 3)
            for tt in range(TT):
                S = (tt + 1) * P
                for hp in range(4):
                    u = 4 * tt + hp
                    v.wait_ge(relu_ready, u + 1)
                    for j in range(2):
                        hd = 4 * (hp // 2) + hp % 2 + 2 * j
                        iw = z[:, Z_IK, T + 8 * tt + hd:T + 8 * tt + hd + 1]
                        src = relu[:, u % 2, j * S:(j + 1) * S]
                        dst = score[:, tt, 0:S]
                        if hp == 0 and j == 0:
                            ins = V.tensor_scalar(dst, src, iw, None, ALU.mult)
                        else:
                            ins = V.scalar_tensor_tensor(out=dst, in0=src, scalar=iw, in1=dst, op0=ALU.mult, op1=ALU.add)
                        if j == 0:
                            step(ins)
                        else:
                            after(relu_used, u + 1, ins)
                V.tensor_copy(small[:, 61:62], score[:, tt, 0:1]).then_inc(score_sum, 1)
            mod_section(2)
            best = small[:, 16:24]
            for tt in range(TT):
                S = (tt + 1) * P
                v.wait_ge(score_causal, tt + 1)
                for _ in range(TOPK // 8):
                    step(V.max(out=best, in_=score[:, tt, 0:S]))
                    step(V.match_replace(out=score[:, tt, 0:S], in_to_replace=best, in_values=score[:, tt, 0:S],
                                         imm_value=PICKED))
                after(picked, tt + 1, V.tensor_scalar(score[:, tt, 0:S], score[:, tt, 0:S], PICKED / 2, DEAD, ALU.is_gt, ALU.mult))
                ada_section(3 + tt)
                mod_section(3 + tt)
            ada_section(5)
            mod_section(5)
            zf = z[:, Z_F:Z_F + 2, :].rearrange("p a n -> p (a n)")
            zq = z[:, Z_Q:Z_Q + 2, :].rearrange("p a n -> p (a n)")
            zf4 = zf.rearrange("p (h t) -> p h t", h=HGRN_H)
            zq4 = zq.rearrange("p (h t) -> p h t", h=HGRN_H)
            le = level_e[:, :, :].rearrange("p h t -> p (h t)")
            lx0 = level_x[:, 0, :, :].rearrange("p h t -> p (h t)")
            lx1 = level_x[:, 1, :, :].rearrange("p h t -> p (h t)")
            dec = decay[:, :, :].rearrange("p h t -> p (h t)")
            v.wait_ge(hg_exp, 1)
            step(V.scalar_tensor_tensor(out=dec, in0=zf, scalar=0.0, in1=le, op0=ALU.min, op1=ALU.subtract))
            after(hg_lin, 1, V.scalar_tensor_tensor(out=lx1, in0=zf, scalar=0.0, in1=le, op0=ALU.max, op1=ALU.add))
            step(V.memset(zf, 1.0))
            for hd in range(HGRN_H):
                step(V.tensor_tensor_scan(level_e[:, hd, :], zf4[:, hd, :], decay[:, hd, :], 0.0, ALU.mult, ALU.add))
            step(V.tensor_copy(dec, le))
            v.wait_ge(hg_exp, 2)
            step(V.tensor_scalar(lx0, lx0, 1.0, None, ALU.add))
            step(V.reciprocal(lx0, lx0))
            step(V.tensor_tensor(zq, zq, lx0, ALU.mult))
            v.wait_ge(hg_exp, 3)
            for hd in range(HGRN_H):
                step(V.tensor_scalar(zf4[:, hd, :], level_x[:, 1, hd, :], lb[:, 2, hd:hd + 1], None, ALU.mult))
            step(V.memset(aT[:, :, :, :], 0.0))
            for n, half in enumerate((128,) + HALVES):
                nb = T * HGRN_H // (2 * half)
                b_v = dec.rearrange("p (n w) -> p n w", w=2 * half)
                e_v = le.rearrange("p (n w) -> p n w", w=2 * half)
                x_v = level_x[:, n % 2, :, :].rearrange("p h t -> p (h t)").rearrange("p (n w) -> p n w", w=2 * half)
                k_v = zf.rearrange("p (n w) -> p n w", w=2 * half)
                q_v = zq.rearrange("p (n w) -> p n w", w=2 * half)
                mid = b_v[:, :, half - 1:half].broadcast_to([P, nb, half])
                step(V.tensor_tensor(e_v[:, :, 0:half], mid, b_v[:, :, 0:half], ALU.subtract))
                after(lvl_d, n + 1, V.tensor_tensor(e_v[:, :, half:], b_v[:, :, half:], mid, ALU.subtract))
                v.wait_ge(lvl_e, n + 1)
                if n >= 2:
                    v.wait_ge(lvl_mm, n - 1)
                step(V.tensor_tensor(x_v[:, :, 0:half], e_v[:, :, 0:half], k_v[:, :, 0:half], ALU.mult))
                after(lvl_x, n + 1, V.tensor_tensor(x_v[:, :, half:], e_v[:, :, half:], q_v[:, :, half:], ALU.mult))
                v.wait_ge(lvl_mm, n + 1)
                if n == 0:
                    after(lvl_at, 1, V.tensor_copy(aT_off[:, :, :], ps[:, 4, :].rearrange("p (h t) -> p h t", h=HGRN_H)))
                else:
                    for tt in range(TT):
                        ins = V.copy_predicated(aT[:, tt, :, :], masks[:, n - 1:n, :].broadcast_to([P, HGRN_H, P]),
                                                ps[:, 6 + tt, :].rearrange("p (h t) -> p h t", h=HGRN_H))
                        if tt == 0:
                            step(ins)
                        else:
                            after(lvl_at, n + 1, ins)
            v.wait_ge(lvl_mm, len(HALVES) + 2)
            for tt in range(TT):
                ins = V.copy_predicated(aT[:, tt, :, :], masks[:, len(HALVES):len(HALVES) + 1, :].broadcast_to([P, HGRN_H, P]),
                                        ps[:, 6 + tt, :].rearrange("p (h t) -> p h t", h=HGRN_H))
                if tt == 0:
                    step(ins)
                else:
                    after(lvl_at, len(HALVES) + 2, ins)
            v.wait_ge(bias_in, 48)
            v.wait_ge(pick_causal, 2)
            for n, (tt, s0) in enumerate(((0, 0), (1, 0), (1, 1))):
                step(V.tensor_tensor(bias[:, n, :, :], bias[:, n, :, :],
                                     score[:, tt:tt + 1, s0 * P:(s0 + 1) * P].broadcast_to([P, ATT_H, P]), ALU.add))
            for tt in range(TT):
                for hp in range(4):
                    u = 4 * tt + hp
                    v.wait_ge(logit_mm, u + 1)
                    n0, w = (0, 1) if tt == 0 else (1, 2)
                    hd = 4 * (hp // 2) + hp % 2
                    dst = bias[:, n0:n0 + w, hd:hd + 3:2, :]
                    src = ps[:, 2 + u % 2, 0:2 * w * P].rearrange("p (h n s) -> p n h s", h=2, n=w)
                    for k in range(w):
                        ins = V.scalar_tensor_tensor(out=dst[:, k], in0=src[:, k], scalar=ATT_D ** -0.5, in1=dst[:, k],
                                                     op0=ALU.mult, op1=ALU.add)
                        if k < w - 1:
                            step(ins)
                        else:
                            after(logit_ready, u + 1, ins)
            for tt in range(TT):
                if tt == 0:
                    step(V.tensor_reduce(small[:, 32:40], bias[:, 0, :, :], AX_X, ALU.max))
                else:
                    step(V.tensor_reduce(small[:, 16:32].rearrange("p (n h) -> p n h", n=2), bias[:, 1:3, :, :], AX_X, ALU.max))
                    step(V.tensor_tensor(small[:, 40:48], small[:, 16:24], small[:, 24:32], ALU.max))
            after(max_ready, 1, V.tensor_scalar(small[:, 32:48], small[:, 32:48], -1.0, None, ALU.mult))
            v.wait_ge(probs_ready, 16)
            step(V.reciprocal(small[:, 48:64], small[:, 48:64]))
            for tt in range(TT):
                v.wait_ge(av_mm, tt + 1)
                after(ob_ready, tt + 1, V.tensor_tensor(
                    relu[:, tt, :].rearrange("p (h d) -> p h d", h=ATT_H),
                    ps[:, 4 + tt, :].rearrange("p (h d) -> p h d", h=ATT_H),
                    small[:, 48 + 8 * tt:56 + 8 * tt].rearrange("p (h o) -> p h o", o=1).broadcast_to([P, ATT_H, ATT_D]), ALU.mult))
            v.wait_ge(hg_exp, 4)
            step(V.tensor_scalar(le, le, 1.0, None, ALU.add))
            step(V.reciprocal(le, le))
            zg = z[:, Z_G:Z_G + 2, :]
            step(V.tensor_tensor(zg.rearrange("p a n -> p (a n)"), zg.rearrange("p a n -> p (a n)"), le, ALU.mult))
            v.wait_ge(o_sq, 8)
            newton(3, 16, 8, 1.0 / HGRN_D)
            for tt in range(TT):
                oa = level_x[:, tt, 0:2, :].rearrange("p a t -> p (a t)")
                step(V.tensor_tensor(
                    oa.rearrange("p (h d) -> p h d", h=HGRN_H),
                    ps[:, 4 + tt, :].rearrange("p (h d) -> p h d", h=HGRN_H),
                    small[:, 32 + 4 * tt:36 + 4 * tt].rearrange("p (h o) -> p h o", o=1).broadcast_to([P, HGRN_H, P]), ALU.mult))
                step(V.tensor_tensor(oa, oa, onw[:, :], ALU.mult))
                after(oa_ready, tt + 1, V.tensor_tensor(
                    oa.rearrange("p (a n) -> p a n", a=2), oa.rearrange("p (a n) -> p a n", a=2),
                    zg[:, :, 256 * tt:256 * tt + 256], ALU.mult))
            v.wait_ge(z_ready, 22)
            zs = z[:, Z_GATE:Z_GATE + 8, :].rearrange("p a n -> p (a n)")
            step(V.tensor_scalar(zs, zs, 1.0, None, ALU.add))
            step(V.reciprocal(zs, zs))
            u = 0
            for nb in range(2):
                for tt in range(TT):
                    v.wait_ge(proj_mm, u + 1)
                    ga, gb = (z[:, Z_GATE + 4 * k + 2 * nb:Z_GATE + 4 * k + 2 * nb + 2, 256 * tt:256 * tt + 256] for k in range(2))
                    ya, yb = (ps[:, 2 * (u % 2) + k, :].rearrange("p (a n) -> p a n", a=2) for k in range(2))
                    step(V.tensor_tensor(ga, ga, ya, ALU.mult))
                    step(V.tensor_tensor(gb, gb, yb, ALU.mult))
                    after(merged, u + 1, V.tensor_tensor(
                        h[:, tt, 512 * nb:512 * nb + 512].rearrange("p (a n) -> p a n", a=2), ga, gb, ALU.add))
                    u += 1
            for n in range(4):
                v.wait_ge(out_mm, n + 1)
                for tt in range(TT):
                    cols = slice(256 * n, 256 * n + 256)
                    tmp = z[:, 4 + n, 256 * tt:256 * tt + 256]
                    step(V.tensor_tensor(tmp, ps[:, n, 256 * tt:256 * tt + 256], mod[:, 2, cols], ALU.mult))
                    ins = V.tensor_tensor(x_sb[:, tt, cols], x_sb[:, tt, cols], tmp, ALU.add)
                    if tt == 0:
                        step(ins)
                    else:
                        after(out_used, n + 1, ins)
            v.wait_ge(ld_ffn, 16)
            norm(3, 2, mod[:, 0, :], mod[:, 1, :], h2_ready)
            wk = z[:, 0, 0:128].rearrange("p (t n) -> p t n", t=TT)
            step(V.memset(wk[:, :, 0:4], 3.0e38))
            for tt in range(TT):
                R = route[:, tt]
                best = z[:, 1, 8 * tt:8 * tt + 8]
                v.wait_ge(rt_mm, tt + 1)
                step(V.tensor_tensor(R[:, 0, :], ps[:, 2 * tt, NE * tt:NE * tt + NE], br[:, :], ALU.add))
                step(V.tensor_copy(wk[:, tt, 4:36], R[:, 0, :]))
                step(V.max(out=best, in_=wk[:, tt, 0:36]))
                after(rt_max, tt + 1, V.tensor_scalar(small[:, 32 + tt:33 + tt], best[:, 4:5], -1.0, None, ALU.mult))
                step(V.match_replace(out=wk[:, tt, 0:36], in_to_replace=best, in_values=wk[:, tt, 0:36], imm_value=PICKED))
                step(V.tensor_scalar(R[:, 3, :], wk[:, tt, 4:36], PICKED / 2, None, ALU.is_lt))
                v.wait_ge(rt_exp, tt + 1)
                step(V.tensor_tensor(R[:, 4, :], R[:, 2, :], R[:, 3, :], ALU.mult))
                step(V.tensor_reduce(small[:, 34 + tt:35 + tt], R[:, 4, :], AX_X, ALU.add))
                step(V.reciprocal(small[:, 34 + tt:35 + tt], small[:, 34 + tt:35 + tt]))
                after(rt_sel, tt + 1, V.tensor_scalar(R[:, 4, :], R[:, 4, :], small[:, 34 + tt:35 + tt], None, ALU.mult))
            v.wait_ge(pos_mm, 1)
            for tt in range(TT):
                R = route[:, tt]
                step(V.tensor_scalar(R[:, 5, :], ps[:, 1, NE * tt:NE * tt + NE], 1.0, None, ALU.add))
                step(V.tensor_tensor(R[:, 5, :], R[:, 5, :], R[:, 3, :], ALU.mult))
                step(V.tensor_scalar(R[:, 5, :], R[:, 5, :], -1.0, None, ALU.add))
            step(V.tensor_scalar(small[0:96, 40:41], ps[0:96, 1, 64:65], more_c[:, 0:1], None, ALU.is_gt))
            after(flag_ready, 1, V.tensor_copy(small[0:96, 41:42], small[0:96, 40:41]))
            v.wait_ge(flag_mm, 1)
            hot = z[0:96, 2, 0:16]
            step(V.tensor_scalar(hot, iota[0:96, 0:16], ps[0:96, 1, 96:97], None, ALU.is_equal))
            after(hot_ready, 1, V.tensor_scalar(hot, hot, small[0:96, 40:41], None, ALU.mult))
            v.wait_ge(list_mm, 1)
            step(V.tensor_copy(lists[0:1, 0:1], ps[0:1, 1, 128:129]))
            step(V.tensor_copy(lists[0:1, 1:33], ps[0:1, 1, 160:192]))
            after(list_ready, 1, V.tensor_copy(lists_i[0:1, 0:33], lists[0:1, 0:33]))
            v.wait_ge(gT_mm, 1)
            after(gT_ready, 1, V.tensor_copy(z[0:NE, 3, 0:T], ps[0:NE, 2, 0:T]))
            for tt in range(TT):
                rest = z[:, 4 + 2 * tt:6 + 2 * tt, :].rearrange("p a n -> p (a n)")
                step(V.tensor_copy(h_parts[:, tt, 0, :], h[:, tt, :]))
                step(V.tensor_tensor(rest, h[:, tt, :], h_parts[:, tt, 0, :], ALU.subtract))
                step(V.tensor_copy(h_parts[:, tt, 1, :], rest))
                after(parts_ready, tt + 1, V.tensor_tensor(h_parts[:, tt, 2, :], rest, h_parts[:, tt, 1, :], ALU.subtract))
            v.wait_ge(rt_mm, 2)
            for n in range(4):
                v.wait_ge(b2_mm, n + 1)
                after(y_start, n + 1, V.tensor_copy(yacc[:, n // 2, 512 * (n % 2):512 * (n % 2) + 512], ps[:, 4 + n, :]))

            v.wait_ge(b1_ready, 1)
            n_more = v.value_load(lists_i[0:1, 0:1], min_val=0, max_val=MAX_MORE)

            def body(g, e, chunk0):
                g24 = g * 24

                def split_lo(u):
                    v.wait_ge(hi_ready, g24 + (u + 1))
                    src = raw(u // 2)[:, 1024 * (u % 2):1024 * (u % 2) + 1024]
                    V.tensor_tensor(w_lo[:, u % PARTS, :], src, w_hi[:, u % PARTS, :].bitcast(F32), ALU.subtract).then_inc(lo_ready, 1)

                def swiglu_in(half):
                    v.wait_ge(sum_mm, g * 4 + (2 * half + 2))
                    T0 = ps[:, 2, :].rearrange("p (c s) -> p c s", c=4)[:, :, 0:SLOTS]
                    T1 = ps[:, 3, :].rearrange("p (c s) -> p c s", c=4)[:, :, 0:SLOTS]
                    bg = b1T[:, bass.ds(e * 16 + 4 * half, 4)].rearrange("p (c o) -> p c o", o=1).broadcast_to([P, 4, SLOTS])
                    bl = b1T[:, bass.ds(e * 16 + (8 + 4 * half), 4)].rearrange("p (c o) -> p c o", o=1).broadcast_to([P, 4, SLOTS])
                    V.tensor_tensor(glu[:, :, :], T0, bg, ALU.add).then_inc(moe_step, 1)
                    V.tensor_tensor(lin[:, :, :], T1, bl, ALU.add).then_inc(t_free, 1)
                    v.wait_ge(moe_step, g * 6 + (3 * half + 1))
                    V.tensor_scalar(glu[:, :, :], glu[:, :, :], LIMIT, None, ALU.min).then_inc(glu_ready, 1)
                    v.wait_ge(t_free, g * 2 + (half + 1))
                    V.tensor_scalar(lin[:, :, :], lin[:, :, :], LIMIT, -LIMIT, ALU.min, ALU.max).then_inc(moe_step, 1)
                    v.wait_ge(moe_step, g * 6 + (3 * half + 2))
                    v.wait_ge(glu_ready, g * 2 + (half + 1))
                    V.scalar_tensor_tensor(out=lin[:, :, :], in0=lin[:, :, :], scalar=1.0, in1=glu[:, :, :],
                                           op0=ALU.add, op1=ALU.mult).then_inc(moe_step, 1)

                def swiglu_out(half):
                    v.wait_ge(sig_ready, g * 2 + (half + 1))
                    v.wait_ge(moe_step, g * 6 + (3 * half + 3))
                    V.tensor_tensor(act32[:, :, :], lin[:, :, :], sig[:, :, :], ALU.mult).then_inc(a32_ready, 1)

                def act_lo(half):
                    v.wait_ge(ahi_ready, g * 2 + (half + 1))
                    V.tensor_tensor(act[:, 4 * half:4 * half + 4, SLOTS:P], act32[:, :, :],
                                    act[:, 4 * half:4 * half + 4, 0:SLOTS].bitcast(F32), ALU.subtract).then_inc(act_ready, 1)

                def add_y(n):
                    v.wait_ge(sc_mm, (g * 4) + (n + 1))
                    dst = yacc[:, n // 2, 512 * (n % 2):512 * (n % 2) + 512]
                    V.tensor_tensor(dst, dst, ps[:, 6 + n % 2, :], ALU.add).then_inc(y_added, 1)

                for tt in range(TT):
                    rank = route[:, tt, 5, bass.ds(e, 1)]
                    slots = iota[:, bass.ds(chunk0, SLOTS)]
                    V.tensor_scalar(pick[:, tt, :], slots, rank, None, ALU.is_equal).then_inc(pick_ready, 1)
                for tt in range(TT):
                    rank = route[:, tt, 5, bass.ds(e, 1)]
                    gate = route[:, tt, 4, bass.ds(e, 1)]
                    for k in range(2):
                        V.tensor_scalar(pick_g[:, tt, k * SLOTS:(k + 1) * SLOTS], iota[:, bass.ds(chunk0, SLOTS)],
                                        rank, gate, ALU.is_equal, ALU.mult).then_inc(pickg_ready, 1)
                v.wait_ge(xhi_ready, g + 1)
                V.tensor_tensor(xs[:, :, SLOTS:P], ps[:, 6, :].rearrange("p (k s) -> p k s", k=KC),
                                xs[:, :, 0:SLOTS].bitcast(F32), ALU.subtract).then_inc(xs_ready, 1)
                for u in range(24):
                    split_lo(u)
                    if u == 11:
                        swiglu_in(0)
                    if u == 12:
                        swiglu_out(0)
                    if u == 14:
                        act_lo(0)
                    if u == 19:
                        swiglu_in(1)
                    if u == 20:
                        swiglu_out(1)
                    if u == 22:
                        act_lo(1)
                for n in range(4):
                    add_y(n)

            with v.Fori(0, NE) as i:
                body(i, i, 0)
            with v.If(n_more > 0):
                with v.Fori(0, n_more) as r:
                    e = v.value_load(lists_i[0:1, bass.ds(r + 1, 1)], min_val=0, max_val=NE - 1)
                    ck = v.value_load(lists_i[0:1, bass.ds(r + 17, 1)], min_val=0, max_val=3)
                    body(r + NE, e, ck * SLOTS)
            v.wait_ge(y_added, n_more * 4 + 4 * NE)
            for tt in range(TT):
                step(V.tensor_tensor(yacc[:, tt, :], yacc[:, tt, :], gate_f[:, :], ALU.mult))
                after(fin_sq, tt + 1, V.tensor_tensor(x_sb[:, tt, :], x_sb[:, tt, :], yacc[:, tt, :], ALU.add))
            v.wait_ge(ld_fin, 16)
            norm(5, 4, None, None, fin_ready)

        @block.tensor
        def _(pe):
            mm = nc.tensor.matmul
            tr = nc.tensor.transpose

            def ada(s):
                pe.wait_ge(acc_ready, s + 1)
                if s >= 1:
                    pe.wait_ge(mod_ready, s)
                for g in range(2):
                    last = mm(ps[:, 4 + g, :], upper[:, 1, :], acc[:, s % 2, 512 * g:512 * g + 512], start=True, stop=True)
                last.then_inc(ada_mm, 1)

            def transposes(src, bank, tt, sig):
                for k in range(KC):
                    last = tr(ps[:, bank + k // 4, P * (k % 4):P * (k % 4) + P], src[:, tt, P * k:P * k + P], ident[:, :])
                last.then_inc(sig, 1)

            pe.wait_ge(ld_small, 16 * (N_SMALL - 3))
            pe.wait_ge(ld_first, 16 * N_FIRST)
            mm(ps[0:ATT_H, 6, 0:384], relb, bucket, start=True, stop=True).then_inc(bias_mm, 1)
            ada(0)
            ada(1)
            for tt in range(TT):
                pe.wait_ge(h_ready, tt + 1)
                transposes(h, 2 * tt, tt, tr_mm)

            def z_block(n):
                w, full, at = tile_at("in", n)
                pe.wait_ge(full, at)
                if n < 2:
                    pe.wait_ge(hT_ready, 4)
                else:
                    pe.wait_ge(z_ready, n - 1)
                bank = ps[:, n % 2, :]
                kind = Z_BLOCKS[n][0]
                if kind == "T":
                    for j in range(2):
                        for k in range(KC):
                            last = mm(bank[:, T * j:T * j + T], w[:, k, P * j:P * j + P], hT[:, k, :], start=(k == 0), stop=(k == KC - 1))
                elif kind in ("IK", "KV"):
                    for k in range(KC):
                        mm(bank[0:64, 0:T], w[:, k, 0:64], hT[:, k, :], start=(k == 0), stop=(k == KC - 1))
                    wd = 8 if kind == "IK" else 64
                    for tt in range(TT):
                        for k in range(KC):
                            last = mm(bank[:, T + wd * tt:T + wd * tt + wd], hT[:, k, tt * P:(tt + 1) * P],
                                      w[:, k, 64:64 + wd], start=(k == 0), stop=(k == KC - 1))
                else:
                    for tt in range(TT):
                        for k in range(KC):
                            last = mm(bank[:, T * tt:T * tt + T], hT[:, k, tt * P:(tt + 1) * P], w[:, k, :], start=(k == 0), stop=(k == KC - 1))
                last.then_inc(z_mm, 1)

            for n in range(6):
                z_block(n)
            pe.wait_ge(z_ready, 4)
            for u in range(8):
                tt, S = u // 4, (u // 4 + 1) * P
                if u >= 2:
                    pe.wait_ge(relu_ready, u - 1)
                r, lo = u % 4, 64 * (u % 2)
                for j in range(2):
                    last = mm(ps[:, 2 + u % 2, j * S:(j + 1) * S],
                              z[lo:lo + 64, Z_IQ + r // 2, T * j + tt * P:T * j + tt * P + P],
                              z[lo:lo + 64, Z_IK, 0:S], start=True, stop=True)
                last.then_inc(score_mm, 1)
            ada(2)
            for n in range(6, 10):
                z_block(n)
            ada(3)
            for n in range(10, 12):
                z_block(n)
            ada(4)
            for n in range(12, 14):
                z_block(n)
            ada(5)
            zf4 = z[:, Z_F:Z_F + 2, :].rearrange("p a n -> p (a n)").rearrange("p (h t) -> p h t", h=HGRN_H)
            zq4 = z[:, Z_Q:Z_Q + 2, :].rearrange("p a n -> p (a n)").rearrange("p (h t) -> p h t", h=HGRN_H)
            pe.wait_ge(mod_ready, 6)
            for n in range(len(HALVES) + 2):
                if n < len(HALVES) + 1:
                    pe.wait_ge(lvl_x, n + 1)
                if n >= 1:
                    pe.wait_ge(lvl_at, n)
                if n == 0:
                    for hd in range(HGRN_H):
                        last = mm(ps[:, 4, P * hd:P * hd + P], level_x[:, 0, hd, 0:P], level_x[:, 0, hd, P:T], start=True, stop=True)
                else:
                    for tt in range(TT):
                        for hd in range(HGRN_H):
                            sl = slice(tt * P, tt * P + P)
                            if n <= len(HALVES):
                                left = right = level_x[:, n % 2, hd, sl]
                            else:
                                left, right = zf4[:, hd, sl], zq4[:, hd, sl]
                            last = mm(ps[:, 6 + tt, P * hd:P * hd + P], left, right, start=True, stop=True)
                last.then_inc(lvl_mm, 1)
            for u in range(8):
                tt, S = u // 4, (u // 4 + 1) * P
                pe.wait_ge(relu_ready, 8)
                if u >= 2:
                    pe.wait_ge(logit_ready, u - 1)
                r, lo = u % 4, 64 * (u % 2)
                for j in range(2):
                    last = mm(ps[:, 2 + u % 2, j * S:(j + 1) * S],
                              z[lo:lo + 64, Z_QB + r // 2, T * j + tt * P:T * j + tt * P + P],
                              z[lo:lo + 64, Z_KV, 0:S], start=True, stop=True)
                last.then_inc(logit_mm, 1)
            for n in range(14, 18):
                z_block(n)
            pe.wait_ge(logit_ready, 8)
            for u in range(6):
                pe.wait_ge(probs_ready, 4 * (u % 2) + 4 if u < 2 else 12 + 4 * (u % 2))
                if u >= 2:
                    pe.wait_ge(pT_ready, u - 1)
                for k in range(4):
                    last = tr(ps[:, 2 + u % 2, P * k:P * k + P], bias[:, u // 2, 4 * (u % 2) + k, :], ident[:, :])
                last.then_inc(pT_mm, 1)
            for tt in range(TT):
                pe.wait_ge(pT_ready, 2 if tt == 0 else 6)
                for hd in range(ATT_H):
                    for k in range(tt + 1):
                        last = mm(ps[:, 4 + tt, 64 * hd:64 * hd + 64], pT[:, tt + k, hd, :],
                                  z[:, Z_KV, T + 64 * k:T + 64 * k + 64], start=(k == 0), stop=(k == tt))
                last.then_inc(av_mm, 1)
            for tt in range(TT):
                pe.wait_ge(ob_ready, tt + 1)
                for k in range(4):
                    last = tr(ps[:, 2 + tt, P * k:P * k + P], relu[:, tt, P * k:P * k + P], ident[:, :])
                last.then_inc(br_mm, 1)
            pe.wait_ge(lvl_at, len(HALVES) + 2)
            for tt in range(TT):
                for hd in range(HGRN_H):
                    vb, vc = Z_V + hd // 2, P * (hd % 2)
                    dst = ps[:, 4 + tt, P * hd:P * hd + P]
                    if tt == 1:
                        mm(dst, aT_off[:, hd, :], z[:, vb, vc:vc + P], start=True, stop=False)
                    last = mm(dst, aT[:, tt, hd, :], z[:, vb, T * tt + vc:T * tt + vc + P], start=(tt == 0), stop=True)
                last.then_inc(o_mm, 1)
            for n in range(18, 20):
                z_block(n)
            for tt in range(TT):
                pe.wait_ge(oa_ready, tt + 1)
                pe.wait_ge(brT_ready, tt + 1)
                for k in range(4):
                    last = tr(ps[:, 2 + tt, P * k:P * k + P], level_x[:, tt, 0:2, :].rearrange("p a t -> p (a t)")[:, P * k:P * k + P], ident[:, :])
                last.then_inc(br_mm, 1)
            for n in range(20, 22):
                z_block(n)
            obT = acc[:, 0, :].rearrange("p (k t) -> p k t", k=4)
            oaT = acc[:, 1, :].rearrange("p (k t) -> p k t", k=4)
            pe.wait_ge(brT_ready, 4)
            pe.wait_ge(z_ready, 22)
            u = 0
            for nb in range(2):
                for tt in range(TT):
                    if u >= 2:
                        pe.wait_ge(merged, u - 1)
                    for kind, src, bk in (("pa", oaT, 0), ("pb", obT, 1)):
                        w, full, at = tile_at(kind, nb)
                        pe.wait_ge(full, at)
                        for k in range(4):
                            last = mm(ps[:, 2 * (u % 2) + bk, :], src[:, k, tt * P:(tt + 1) * P], w[:, k, :], start=(k == 0), stop=(k == 3))
                    last.then_inc(proj_mm, 1)
                    u += 1
            for tt in range(TT):
                pe.wait_ge(merged, 3 + tt)
                transposes(h, 4 + 2 * tt, tt, mT_mm)
            for n in range(4):
                w, full, at = tile_at("out", n)
                pe.wait_ge(full, at)
                pe.wait_ge(mT_ready, 4)
                for tt in range(TT):
                    for k in range(KC):
                        last = mm(ps[:, n, T * tt:T * tt + T], hT[:, k, tt * P:(tt + 1) * P], w[:, k, :], start=(k == 0), stop=(k == KC - 1))
                last.then_inc(out_mm, 1)
            for tt in range(TT):
                pe.wait_ge(h2_ready, tt + 1)
                transposes(h, 4 + 2 * tt, tt, h2_mm)
            for tt in range(TT):
                pe.wait_ge(h2T_ready, 2 * tt + 2)
                for k in range(KC):
                    last = mm(ps[:, 2 * tt, NE * tt:NE * tt + NE], hT[:, k, tt * P:(tt + 1) * P], wr[:, k, :], start=(k == 0), stop=(k == KC - 1))
                last.then_inc(rt_mm, 1)
            pe.wait_ge(ld_b, 32)
            for m in range(4):
                last = tr(ps[:, 3, P * m:P * m + P], z[:, 16, P * m:P * m + P], ident[:, :])
            last.then_inc(b1_mm, 1)
            pe.wait_ge(rt_sel, 2)
            mm(ps[:, 1, 0:NE], upper[:, 0, :], route[:, 0, 3, :], start=True, stop=True)
            mm(ps[:, 1, NE:2 * NE], upper[:, 1, :], route[:, 0, 3, :], start=True, stop=False)
            mm(ps[:, 1, NE:2 * NE], upper[:, 0, :], route[:, 1, 3, :], start=False, stop=True)
            for k in range(3):
                for tt in range(TT):
                    last = mm(ps[32 * k:32 * k + 32, 1, 64:65], route[:, tt, 3, :], upper[:, 1, 0:1], start=(tt == 0), stop=(tt == 1))
            last.then_inc(pos_mm, 1)
            for tt in range(TT):
                last = tr(ps[0:NE, 2, P * tt:P * tt + P], route[:, tt, 4, :], ident[:, :])
            last.then_inc(gT_mm, 1)
            pe.wait_ge(flag_ready, 1)
            mm(ps[0:96, 1, 96:97], upper[0:96, 0, 0:96], small[0:96, 41:42], start=True, stop=True).then_inc(flag_mm, 1)
            pe.wait_ge(hot_ready, 1)
            mm(ps[0:1, 1, 128:129], small[0:96, 41:42], upper[0:96, 1, 0:1], start=True, stop=True)
            mm(ps[0:1, 1, 160:176], more_c[:, 1:2], z[0:96, 2, 0:16], start=True, stop=True)
            mm(ps[0:1, 1, 176:192], more_c[:, 2:3], z[0:96, 2, 0:16], start=True, stop=True).then_inc(list_mm, 1)
            pe.wait_ge(gT_ready, 1)
            pe.wait_ge(h2T_ready, 4)
            for n in range(4):
                mm(ps[:, 4 + n, :], z[0:NE, 3, P * (n // 2):P * (n // 2) + P],
                   z[0:NE, 10 + n % 2, :], start=True, stop=True).then_inc(b2_mm, 1)

            pe.wait_ge(y_start, 4)
            pe.wait_ge(parts_ready, 2)
            pe.wait_ge(b1_ready, 1)
            n_more = pe.value_load(lists_i[0:1, 0:1], min_val=0, max_val=MAX_MORE)
            pe.nop().then_inc(w_free, PARTS)

            def body(g):
                g24 = g * 24

                def w1_unit(u):
                    b = u // 4
                    pe.wait_ge(lo_ready, g24 + (u + 1))
                    for kk in range(2):
                        k = 2 * (u % 4) + kk
                        for part in (w_hi, w_lo):
                            last = mm(ps[:, b % 2, :], xs[:, k, :], part[:, u % PARTS, 512 * kk:512 * kk + 512],
                                      start=(k == 0 and part is w_hi), stop=(k == KC - 1 and part is w_lo))
                    last.then_inc(w_free, 1)

                def fold_block(b):
                    pe.wait_ge(hs_ready, g * 4 + (b + 1))
                    if b == 2:
                        pe.wait_ge(t_free, g * 2 + 1)
                    for cch in range(4):
                        last = mm(ps[:, 2 + b % 2, P * cch:P * cch + P], hs[:, b % 2, P * cch:P * cch + P], fold[:, :], start=True, stop=True)
                    last.then_inc(sum_mm, 1)

                def w2_unit(u):
                    fc = u - 16
                    pe.wait_ge(lo_ready, g24 + (u + 1))
                    for part in (w_hi, w_lo):
                        for nb in range(2):
                            last = mm(ps[:, 4 + nb, :], act[:, fc, :], part[:, u % PARTS, 512 * nb:512 * nb + 512],
                                      start=(fc == 0 and part is w_hi), stop=(fc == 7 and part is w_lo))
                    last.then_inc(w_free, 1)

                pe.wait_ge(pick_ready, g * 2 + 2)
                for k in range(KC):
                    for tt in range(TT):
                        for part in range(3):
                            last = mm(ps[:, 6, SLOTS * k:SLOTS * k + SLOTS], h_parts[:, tt, part, P * k:P * k + P], pick[:, tt, :],
                                      start=(tt == 0 and part == 0), stop=(tt == 1 and part == 2))
                last.then_inc(gather_mm, 1)
                pe.wait_ge(pickg_ready, g * 4 + 4)
                for tt in range(TT):
                    last = tr(ps[:, 7, P * tt:P * tt + P], pick_g[:, tt, :], ident[:, :])
                last.then_inc(st_mm, 1)
                pe.wait_ge(xs_ready, g + 1)
                for u in range(16):
                    w1_unit(u)
                    if u == 6:
                        fold_block(0)
                    if u == 10:
                        fold_block(1)
                    if u == 14:
                        fold_block(2)
                fold_block(3)
                pe.wait_ge(act_ready, g * 2 + 1)
                for u in range(16, 20):
                    w2_unit(u)
                pe.wait_ge(act_ready, g * 2 + 2)
                for u in range(20, 24):
                    w2_unit(u)
                pe.wait_ge(ysb_ready, g * 2 + 2)
                pe.wait_ge(st_ready, g + 1)
                for n in range(4):
                    if n >= 2:
                        pe.wait_ge(y_added, g * 4 + (n - 1))
                    mm(ps[:, 6 + n % 2, :], st[:, P * (n // 2):P * (n // 2) + P], ysb[:, 512 * (n % 2):512 * (n % 2) + 512],
                       start=True, stop=True).then_inc(sc_mm, 1)
                pe.wait_ge(y_added, g * 4 + 4)

            with pe.Fori(0, NE) as i:
                body(i)
            with pe.If(n_more > 0):
                with pe.Fori(0, n_more) as r:
                    body(r + NE)


_INS = ["x", "c", "w_ada", "b_ada", "norm_mix_w", "w_in", "hgrn_lb_logits", "hgrn_norm_w", "rel_bias",
        "w_proj_a", "w_proj_b", "w_out", "norm_ffn_w", "w_router", "b_router", "w_mlp1", "b_mlp1",
        "w_mlp2", "b_mlp2", "final_norm_w"]


def constants():
    import math
    import numpy as np

    f = np.float32
    ident = np.eye(128, dtype=f)
    half = np.arange(128) % 64
    fold = (half[:, None] == half[None, :]).astype(f)
    dist = 255 - np.arange(256)
    large = 16 + (np.log(np.maximum(dist, 1).astype(f) / f(16)) / f(math.log(8)) * f(16)).astype(np.int32)
    bucket = np.where(dist < 16, dist, np.minimum(large, 31))
    hot = np.zeros((32, 384), f)
    hot[bucket, np.arange(256)] = 1
    s, t = np.arange(128)[:, None], np.arange(128)[None, :]
    masks = [(s // (2 * m) == t // (2 * m)) & (s % (2 * m) < m) & (t % (2 * m) >= m) for m in HALVES]
    masks = np.stack(masks + [s == t], 1).astype(f).reshape(128, 8 * 128)
    iota = np.broadcast_to(np.arange(256, dtype=f), (128, 256)).copy()
    upper = np.concatenate([(s < t).astype(f), np.ones((128, 128), f)], 1)
    q = np.arange(96)
    more = np.stack([64 * (q // 32 + 1), q % 32, q // 32 + 1, 0 * q], 1).astype(f)
    return {"k_ident": ident, "k_fold": fold, "k_bucket": hot, "k_masks": masks, "k_iota": iota,
            "k_upper": upper, "k_more": more}


def kernel(**inputs):
    import numpy as np
    import concourse.bacc as bacc
    from concourse.bass_utils import run_bass_kernel_spmd

    nc = bacc.Bacc("TRN2", target_bir_lowering=False, num_devices=1)
    arrays, args = {}, []
    for name, a in [(n, inputs[n]) for n in _INS] + list(constants().items()):
        a = np.ascontiguousarray(a)
        arrays[f"in_{name}_dram"] = a
        args.append(nc.dram_tensor(f"in_{name}_dram", a.shape, mybir.dt.from_np(a.dtype), kind="ExternalInput").ap())
    out = nc.dram_tensor("out_0_dram", (1, 256, 1024), F32, kind="ExternalOutput").ap()
    build(nc, *args, out)
    r = run_bass_kernel_spmd(nc, [arrays], core_ids=[0])
    return r.results[0]["out_0_dram"]
```

```python
import math
from contextlib import ExitStack

import concourse.bass as bass
from concourse import mybir

P = 128
F32 = mybir.dt.float32
F32R = mybir.dt.float32r
BF16 = mybir.dt.bfloat16
I32 = mybir.dt.int32
U8 = mybir.dt.uint8
ALU = mybir.AluOpType
ACT = mybir.ActivationFunctionType
AX_X = mybir.AxisListType.X

EPS = 1e-6
HGRN_H, HGRN_D = 4, 128
ATT_H, ATT_D = 8, 64
TOPK = 64
TOP_E = 4
LIMIT, ALPHA = 7.0, 1.702
SIG_LIMIT = 1.0 / (1.0 + math.exp(-ALPHA * LIMIT))
SLOTS = 64
MAX_MORE = 15
DEAD, PICKED = -1.0e30, -3.0e38
RING = 6
TILES = 12
PARTS = 8
WHOLE = (1, 21)
SPLIT = [u for u in range(24) if u not in WHOLE]
HALVES = (64, 32, 16, 8, 4, 2, 1)

Z_BLOCKS = (
    [("T", 2688 + 256 * i, 256) for i in range(2)]
    + [("IK", 3200, 72), ("KV", 2560, 128)]
    + [("T", 2048 + 256 * i, 256) for i in range(2)]
    + [("T", 512 + 256 * i, 256) for i in range(2)]
    + [("T", 256 * i, 256) for i in range(2)]
    + [("N", 1024 + 256 * i, 256) for i in range(2)]
    + [("N", 1536 + 256 * i, 256) for i in range(2)]
    + [("GATE", 3272 + 256 * i, 256) for i in range(8)]
)
Z_IQ, Z_IK, Z_KV, Z_QB, Z_F, Z_Q, Z_V, Z_G, Z_GATE = 0, 2, 3, 4, 6, 8, 10, 12, 14


def mixer_stream():
    tiles = [("ada", n) for n in range(8)]
    for n in range(len(Z_BLOCKS)):
        tiles.append(("in", n))
        if n < 16:
            tiles.append(("ada", 8 + n))
    tiles += [("pa", 0), ("pb", 0), ("pa", 1), ("pb", 1)]
    tiles += [("out", n) for n in range(4)]
    return tiles


def build(nc, x, c, w_ada, b_ada, norm_mix_w, w_in, hgrn_lb_logits, hgrn_norm_w, rel_bias, w_proj_a,
          w_proj_b, w_out, norm_ffn_w, w_router, b_router, w_mlp1, b_mlp1, w_mlp2, b_mlp2,
          final_norm_w, k_ident, k_fold, k_bucket, k_masks, k_iota, k_upper, k_more, k_items, out):
    T, D = x.shape[1], x.shape[2]
    TT, KC = T // P, D // P
    NE, FF2 = w_mlp1.shape[1], w_mlp1.shape[3]
    FF = FF2 // 2
    assert (T, D, TT, KC, NE, FF) == (256, 1024, 2, 8, 32, 1024)

    stream = mixer_stream()
    place = {key: (n % RING, 16 * (n // RING + 1)) for n, key in enumerate(stream)}
    MIX_ROUNDS = len(stream) // RING
    assert len(stream) % RING == 0

    bias_dram = nc.dram_tensor("bias_rows", [ATT_H, P, 384], F32, kind="Internal").ap()

    ctx = ExitStack()
    with ctx:
        def sem(name):
            return ctx.enter_context(nc.semaphore(name))

        def sb(name, shape, dt, stack=ctx):
            return stack.enter_context(nc.sbuf_tensor(name, shape, dt))

        ident = sb("ident", [P, P], F32)
        fold = sb("fold", [P, P], F32)
        iota = sb("iota", [P, 256], F32)
        x_sb = sb("x_sb", [P, TT, D], F32)
        h = sb("h", [P, TT, D], F32)
        hT = sb("hT", [P, KC, T], F32)
        mod = sb("mod", [P, 3, D], F32)
        gate_f = sb("gate_f", [P, D], F32)
        norm_w = sb("norm_w", [P, D], F32)
        raw_ring = sb("raw_ring", [P, RING, 2048], F32)
        ITEM_E, ITEM_C = 1, 1 + NE + MAX_MORE + 1
        route = sb("route", [P, TT, 8, NE], F32)
        small = sb("small", [P, 64], F32)
        lists = sb("lists", [1, 128], F32)
        lists_i = sb("lists_i", [1, 128], I32)

        mix = ExitStack()
        with mix:
            bias = sb("bias", [P, 3, ATT_H, P], F32, mix)
            relu = sb("relu", [P, 2, 512], F32, mix)
            score = sb("score", [P, TT, T], F32, mix)
            pT = sb("pT", [P, 3, ATT_H, P], F32, mix)
            decay = sb("decay", [P, HGRN_H, T], F32, mix)
            level_e = sb("level_e", [P, HGRN_H, T], F32, mix)
            level_x = sb("level_x", [P, 2, HGRN_H, T], F32, mix)
            aT = sb("aT", [P, 2, HGRN_H, P], F32, mix)
            aT_off = sb("aT_off", [P, HGRN_H, P], F32, mix)
            z = sb("z", [P, len(Z_BLOCKS), 512], F32, mix)
            acc = sb("acc", [P, 2, D], F32, mix)
            masks = sb("masks", [P, 8, P], U8, mix)
            upper = sb("upper", [P, 2, P], F32, mix)
            onw = sb("onw", [P, 512], F32, mix)
            lb = sb("lb", [P, 4, HGRN_H], F32, mix)
            wr = sb("wr", [P, KC, NE], F32, mix)
            br = sb("br", [P, NE], F32, mix)
            cc = sb("cc", [P, 4, KC], F32, mix)
            more_c = sb("more_c", [96, 4], F32, mix)
        bucket = pT[0:32, 0, 0:3, :].rearrange("p a n -> p (a n)")
        brow = pT[0:ATT_H, 1, 0:3, :].rearrange("p a n -> p (a n)")
        relb = pT[0:32, 2, 0, 0:ATT_H]
        moe = ctx
        w_hi = sb("w_hi", [P, PARTS, 1024], F32R, moe)
        w_lo = sb("w_lo", [P, PARTS, 1024], F32R, moe)
        xs = sb("xs", [P, KC, P], F32R, moe)
        act = sb("act", [P, KC, P], F32R, moe)
        sb("z_scratch_kept", [P, 4096], F32, moe)
        h_parts = sb("h_parts", [P, TT, 3, D], BF16, moe)
        b1T = sb("b1T", [P, NE * 16], F32, moe)
        st = sb("st", [P, T], F32, moe)
        pick = sb("pick", [P, TT, SLOTS], BF16, moe)
        pick_g = sb("pick_g", [P, TT, P], F32, moe)
        glu = sb("glu", [P, 4, SLOTS], F32, moe)
        lin = sb("lin", [P, 4, SLOTS], F32, moe)
        sig = sb("sig", [P, 4, SLOTS], F32, moe)
        act32 = sb("act32", [P, 4, SLOTS], F32, moe)
        hs = h[:, 0, :].rearrange("p (b n) -> p b n", b=2)
        ysb = h[:, 1, :]
        yacc = hT[:, :, :].rearrange("p k t -> p (k t)").rearrange("p (a n) -> p a n", a=TT)

        ps = ctx.enter_context(nc.psum_tensor("ps", [P, 8, 512], F32))

        ld_first = sem("ld_first")
        ld_small = sem("ld_small")
        ld_x = sem("ld_x")
        ld_bada = [sem(f"ld_bada{n}") for n in range(6)]
        ld_ffn = sem("ld_ffn")
        ld_fin = sem("ld_fin")
        ld_b = sem("ld_b")
        raw_full = [sem(f"raw_full{s}") for s in range(RING)]
        ada_used = sem("ada_used")
        dve_step = sem("dve_step")
        act_step = sem("act_step")
        pool_step = sem("pool_step")
        c_exp = sem("c_exp")
        acc_ready = sem("acc_ready")
        ada_mm = sem("ada_mm")
        mod_ready = sem("mod_ready")
        sq_done = sem("sq_done")
        ln_in = sem("ln_in")
        ln_out = sem("ln_out")
        h_ready = sem("h_ready")
        tr_mm = sem("tr_mm")
        hT_ready = sem("hT_ready")
        z_mm = sem("z_mm")
        z_ready = sem("z_ready")
        bias_mm = sem("bias_mm")
        brow_ready = sem("brow_ready")
        brow_out = sem("brow_out")
        bias_in = sem("bias_in")
        score_mm = sem("score_mm")
        relu_ready = sem("relu_ready")
        relu_used = sem("relu_used")
        score_sum = sem("score_sum")
        score_causal = sem("score_causal")
        picked = sem("picked")
        pick_causal = sem("pick_causal")
        logit_mm = sem("logit_mm")
        logit_ready = sem("logit_ready")
        max_ready = sem("max_ready")
        probs_ready = sem("probs_ready")
        pT_mm = sem("pT_mm")
        pT_ready = sem("pT_ready")
        av_mm = sem("av_mm")
        ob_ready = sem("ob_ready")
        hg_exp = sem("hg_exp")
        hg_lin = sem("hg_lin")
        lvl_d = sem("lvl_d")
        lvl_e = sem("lvl_e")
        lvl_x = sem("lvl_x")
        lvl_mm = sem("lvl_mm")
        lvl_at = sem("lvl_at")
        o_mm = sem("o_mm")
        o_sq = sem("o_sq")
        oa_ready = sem("oa_ready")
        br_mm = sem("br_mm")
        brT_ready = sem("brT_ready")
        gates_ready = sem("gates_ready")
        proj_mm = sem("proj_mm")
        merged = sem("merged")
        mT_mm = sem("mT_mm")
        mT_ready = sem("mT_ready")
        out_mm = sem("out_mm")
        out_used = sem("out_used")
        h2_ready = sem("h2_ready")
        h2_mm = sem("h2_mm")
        h2T_ready = sem("h2T_ready")
        rt_mm = sem("rt_mm")
        rt_max = sem("rt_max")
        rt_exp = sem("rt_exp")
        rt_sel = sem("rt_sel")
        pos_mm = sem("pos_mm")
        cnt_ready = sem("cnt_ready")
        flag_ready = sem("flag_ready")
        flag_mm = sem("flag_mm")
        hot_ready = sem("hot_ready")
        list_mm = sem("list_mm")
        list_ready = sem("list_ready")
        b1_mm = sem("b1_mm")
        b1_ready = sem("b1_ready")
        b2_mm = sem("b2_mm")
        y_start = sem("y_start")
        parts_ready = sem("parts_ready")
        hi_ready = sem("hi_ready")
        lo_ready = sem("lo_ready")
        w_free = sem("w_free")
        pick_ready = sem("pick_ready")
        pickg_ready = sem("pickg_ready")
        lin_ready = sem("lin_ready")
        doubled = sem("doubled")
        gather_mm = sem("gather_mm")
        xhi_ready = sem("xhi_ready")
        xs_ready = sem("xs_ready")
        st_mm = sem("st_mm")
        st_ready = sem("st_ready")
        hs_ready = sem("hs_ready")
        sum_mm = sem("sum_mm")
        glu_ready = sem("glu_ready")
        sig_ready = sem("sig_ready")
        a32_ready = sem("a32_ready")
        ahi_ready = sem("ahi_ready")
        act_ready = sem("act_ready")
        t_free = sem("t_free")
        ysb_ready = sem("ysb_ready")
        sc_mm = sem("sc_mm")
        y_added = sem("y_added")
        moe_step = sem("moe_step")
        fin_sq = sem("fin_sq")
        fin_ready = sem("fin_ready")
        st_out = sem("st_out")

        N_FIRST, N_SMALL = 2, 15
        bada_rows = b_ada[0].rearrange("(s n) -> s n", n=D)
        BADA_DST = [mod[:, 0, :], mod[:, 1, :], mod[:, 2, :], mod[:, 0, :], mod[:, 1, :], gate_f[:, :]]

        def raw(s):
            return raw_ring[:, s, :]

        def raw_unit(u):
            return raw_ring[:, (u // 2) % RING, 1024 * (u % 2):1024 * (u % 2) + 1024]

        def tile_src(kind, n):
            if kind == "ada":
                return w_ada[0].rearrange("(p j) n -> p j n", j=KC)[:, :, 256 * n:256 * n + 256]
            if kind == "in":
                _, c0, w = Z_BLOCKS[n]
                return w_in[0].rearrange("(k p) n -> p k n", p=P)[:, :, c0:c0 + w]
            if kind in ("pa", "pb"):
                w = (w_proj_a if kind == "pa" else w_proj_b)[0]
                return w.rearrange("(k p) n -> p k n", p=P)[:, :, 512 * n:512 * n + 512]
            return w_out[0].rearrange("(k p) n -> p k n", p=P)[:, :, 256 * n:256 * n + 256]

        def tile_at(kind, n):
            s, full = place[(kind, n)]
            a, w = tile_src(kind, n).shape[1:]
            return raw(s)[:, 0:a * w].rearrange("p (a w) -> p a w", a=a), raw_full[s], full

        w1_v = w_mlp1[0].rearrange("e (k p) n -> p e k n", p=P)
        w2_v = w_mlp2[0].rearrange("e (k p) n -> p e k n", p=P)
        W1_COL = [0, FF, 512, FF + 512]

        def split_count(u):
            return sum(n <= u for n in SPLIT)

        def wait_tile(engine, g, q):
            engine.wait_ge(raw_full[q % RING], g * (16 * TILES // RING) + 16 * (MIX_ROUNDS + q // RING + 1))

        block = ctx.enter_context(nc.Block())

        @block.sync
        def _(sp):
            def slot_read(kind, i):
                if kind == "ada":
                    sp.wait_ge(ada_used, i + 1)
                elif kind == "in":
                    sp.wait_ge(z_mm, i + 1)
                elif kind == "out":
                    sp.wait_ge(out_mm, i + 1)
                else:
                    sp.wait_ge(proj_mm, 2 * i + 2)

            for n, (kind, i) in enumerate(stream):
                if n >= RING:
                    slot_read(*stream[n - RING])
                dst, full, _ = tile_at(kind, i)
                sp.dma_start(dst, tile_src(kind, i)).then_inc(full, 16)

            def expert_tile(e, q):
                dst = raw(q % RING)
                if q < 8:
                    c0 = W1_COL[q // 2]
                    src = w1_v[:, bass.ds(e, 1), 4 * (q % 2):4 * (q % 2) + 4, c0:c0 + 512]
                    dst = dst.rearrange("p (k n) -> p k n", k=4)
                else:
                    src = w2_v[:, bass.ds(e, 1), 2 * (q - 8):2 * (q - 8) + 2, :]
                    dst = dst.rearrange("p (k n) -> p k n", k=2)
                sp.dma_start(dst, src.rearrange("p e k n -> p (e k) n")).then_inc(raw_full[q % RING], 16)

            def slot_free(g, q):
                if any(u in SPLIT for u in (2 * q, 2 * q + 1)):
                    sp.wait_ge(lo_ready, g * len(SPLIT) + split_count(2 * q + 1))
                for u in (2 * q, 2 * q + 1):
                    if u in WHOLE:
                        sp.wait_ge(w_free, g * 24 + (PARTS + u + 1))

            def item_tiles(g, e):
                for q in range(TILES):
                    if q < RING:
                        slot_free(g - 1, q + TILES - RING)
                    else:
                        slot_free(g, q - RING)
                    expert_tile(e, q)

            for q in range(TILES):
                if q < RING:
                    slot_read(*stream[len(stream) - RING + q])
                else:
                    slot_free(0, q - RING)
                expert_tile(0, q)
            with sp.Fori(1, NE) as i:
                item_tiles(i, i)
            sp.wait_ge(list_ready, 1)
            n_more = sp.value_load(lists_i[0:1, 0:1], min_val=0, max_val=MAX_MORE)
            with sp.If(n_more > 0):
                with sp.Fori(0, n_more) as r:
                    e = sp.value_load(lists_i[0:1, bass.ds(r + (ITEM_E + NE), 1)], min_val=0, max_val=NE - 1)
                    item_tiles(r + NE, e)
            for tt in range(TT):
                sp.wait_ge(fin_ready, tt + 1)
                sp.dma_start(out[0, tt * P:(tt + 1) * P, :], h[:, tt, :]).then_inc(st_out, 16)
            sp.wait_ge(st_out, 32)

        @block.gpsimd
        def _(pool):
            small_loads = [
                (fold[:, :], k_fold), (iota[:, :], k_iota),
                (bucket, k_bucket), (relb, rel_bias),
                (z[:, 20:22, :].rearrange("p a n -> p (a n)"), k_masks),
                (upper[:, :, :], k_upper.rearrange("p (a n) -> p a n", a=2)),
                (onw[:, :], hgrn_norm_w[0:1, :].broadcast_to([P, 512])),
                (wr[:, :, :], w_router[0].rearrange("(k p) n -> p k n", p=P)),
                (br[:, :], b_router[0:1, :].broadcast_to([P, NE])),
                (more_c[:, :], k_more),
                (lists[0:1, 0:2 * (NE + MAX_MORE + 1) + 1], k_items),
                (norm_w[:, :], norm_mix_w[0:1, :].broadcast_to([P, D])),
            ]
            for dst, src in small_loads:
                pool.dma_start(dst, src).then_inc(ld_small, 16)
            for n in range(3):
                pool.dma_start(BADA_DST[n], bada_rows[n:n + 1, :].broadcast_to([P, D])).then_inc(ld_bada[n], 16)
            assert len(small_loads) + 3 == N_SMALL

            pool.wait_ge(brow_ready, 1)
            pool.dma_start(bias_dram, brow.rearrange("h (o j) -> h o j", o=1).broadcast_to([ATT_H, P, 384])).then_inc(brow_out, 16)
            pool.wait_ge(brow_out, 16)
            for n, (tt, st_) in enumerate(((0, 0), (1, 0), (1, 1))):
                src = bass.AP(tensor=bias_dram.tensor, offset=255 - tt * P + st_ * P,
                              ap=[[383, P], [384 * P, ATT_H], [1, P]])
                pool.dma_start(bias[:, n, :, :], src).then_inc(bias_in, 16)

            pool.wait_ge(h_ready, 2)
            for n in range(3, 6):
                pool.dma_start(BADA_DST[n], bada_rows[n:n + 1, :].broadcast_to([P, D])).then_inc(ld_bada[n], 16)
            pool.dma_start(norm_w[:, :], norm_ffn_w[0:1, :].broadcast_to([P, D])).then_inc(ld_ffn, 16)

            for tt in range(TT):
                S = (tt + 1) * P
                pool.wait_ge(score_sum, tt + 1)
                nc.gpsimd.affine_select(out=score[:, tt, 0:S], in_=score[:, tt, 0:S], compare_op=ALU.is_ge,
                                        fill=DEAD, base=tt * P, pattern=[[-1, S]],
                                        channel_multiplier=1).then_inc(score_causal, 1)
            for tt in range(TT):
                S = (tt + 1) * P
                pool.wait_ge(picked, tt + 1)
                nc.gpsimd.affine_select(out=score[:, tt, 0:S], in_=score[:, tt, 0:S], compare_op=ALU.is_ge,
                                        fill=DEAD, base=tt * P, pattern=[[-1, S]],
                                        channel_multiplier=1).then_inc(pick_causal, 1)
            pool.wait_ge(merged, 4)
            pool.dma_start(z[:, 16:17, :].rearrange("p a (m n) -> p (a m) n", m=4),
                           b_mlp1[0].rearrange("e (c n) -> (e c) n", n=P)
                           .rearrange("(m p) n -> p m n", p=P)).then_inc(ld_b, 16)
            pool.dma_start(z[0:NE, 10:12, :].rearrange("p a n -> p (a n)"), b_mlp2[0]).then_inc(ld_b, 16)
            pool.wait_ge(h2_ready, 2)
            pool.dma_start(norm_w[:, :], final_norm_w.rearrange("(a n) -> a n", a=1).broadcast_to([P, D])).then_inc(ld_fin, 16)

            pool.wait_ge(list_ready, 1)
            pool.wait_ge(y_start, 1)
            n_more = pool.value_load(lists_i[0:1, 0:1], min_val=0, max_val=MAX_MORE)

            def body(g):
                e = pool.value_load(lists_i[0:1, bass.ds(g + ITEM_E, 1)], min_val=0, max_val=NE - 1)
                pool.wait_ge(pick_ready, g * 2 + 2)
                pool.wait_ge(st_mm, g + 1)
                for tt in range(TT):
                    gate = route[:, tt, 4, bass.ds(e, 1)].broadcast_to([P, SLOTS])
                    for k in range(2):
                        nc.gpsimd.tensor_tensor(pick_g[:, tt, k * SLOTS:(k + 1) * SLOTS], pick[:, tt, :], gate,
                                                ALU.mult).then_inc(doubled, 1)

            with pool.Fori(0, NE) as i:
                body(i)
            with pool.If(n_more > 0):
                with pool.Fori(0, n_more) as r:
                    body(r + NE)

        @block.scalar
        def _(a):
            a.dma_start(cc[:, 0, :], c[0].rearrange("(p j) -> p j", j=KC)).then_inc(ld_first, 16)
            a.dma_start(ident[:, :], k_ident).then_inc(ld_first, 16)
            a.dma_start(x_sb[:, :, :], x[0].rearrange("(t p) d -> p t d", p=P)).then_inc(ld_x, 16)
            a.dma_start(lb[:, 0, :], hgrn_lb_logits[0].rearrange("(h d) -> d h", d=P), allow_slow_non_contiguous=True).then_inc(ld_x, 16)

            count = [0]

            def step(ins):
                count[0] += 1
                ins.then_inc(act_step, 1)
                a.wait_ge(act_step, count[0])

            a.wait_ge(ld_first, 16 * N_FIRST)
            nc.scalar.activation(cc[:, 1, :], cc[:, 0, :], ACT.Exp, scale=-1.0).then_inc(c_exp, 1)
            a.wait_ge(ld_x, 32)

            def norm_square(tt):
                nc.scalar.activation(h[:, tt, :], x_sb[:, tt, :], ACT.Square,
                                     accum_out=small[:, 8 * tt:8 * tt + 1]).then_inc(sq_done, 1)

            def rsqrt_guess(n, lo, w):
                a.wait_ge(ln_in, n)
                step(nc.scalar.activation(small[:, lo + w:lo + 2 * w], small[:, lo:lo + w], ACT.Ln))
                nc.scalar.activation(small[:, lo + 2 * w:lo + 3 * w], small[:, lo + w:lo + 2 * w], ACT.Exp,
                                     scale=-0.5).then_inc(ln_out, 1)

            def copy_T(src_banks, dst, tt, sig):
                for g in range(2):
                    nc.scalar.activation(dst[:, 4 * g:4 * g + 4, tt * P:(tt + 1) * P],
                                         ps[:, src_banks + g, :].rearrange("p (k t) -> p k t", k=4),
                                         ACT.Copy).then_inc(sig, 1)

            for tt in range(TT):
                norm_square(tt)
            for tt in range(TT):
                rsqrt_guess(tt + 1, 8 * tt + 1, 1)
            for tt in range(TT):
                a.wait_ge(tr_mm, tt + 1)
                copy_T(2 * tt, hT, tt, hT_ready)

            a.wait_ge(bias_mm, 1)
            nc.scalar.activation(brow, ps[0:ATT_H, 6, 0:384], ACT.Copy).then_inc(brow_ready, 1)

            def evac_z(n):
                a.wait_ge(z_mm, n + 1)
                bank = ps[:, n % 2, :]
                kind = Z_BLOCKS[n][0]
                if kind == "IK":
                    nc.scalar.activation(z[0:64, n, 0:T], bank[0:64, 0:T], ACT.Copy)
                    nc.scalar.activation(z[64:128, n, 0:T], bank[0:64, 0:T], ACT.Copy)
                    nc.scalar.activation(z[:, n, T:T + 16], bank[:, T:T + 16], ACT.Copy,
                                         scale=ATT_H ** -0.5 * ATT_D ** -0.5).then_inc(z_ready, 1)
                elif kind == "KV":
                    nc.scalar.activation(z[0:64, n, 0:T], bank[0:64, 0:T], ACT.Copy)
                    nc.scalar.activation(z[64:128, n, 0:T], bank[0:64, 0:T], ACT.Copy)
                    nc.scalar.activation(z[:, n, T:T + 128], bank[:, T:T + 128], ACT.Copy).then_inc(z_ready, 1)
                elif kind == "GATE":
                    nc.scalar.activation(z[:, n, :], bank, ACT.Exp, scale=-1.0).then_inc(z_ready, 1)
                else:
                    nc.scalar.activation(z[:, n, :], bank, ACT.Copy).then_inc(z_ready, 1)

            for n in range(6):
                evac_z(n)
            for u in range(8):
                S = (u // 4 + 1) * P
                a.wait_ge(score_mm, u + 1)
                if u >= 2:
                    a.wait_ge(relu_used, u - 1)
                nc.scalar.activation(relu[:, u % 2, 0:2 * S], ps[:, 2 + u % 2, 0:2 * S], ACT.Relu).then_inc(relu_ready, 1)
            for n in range(6, 10):
                evac_z(n)
            zf = z[:, Z_F:Z_F + 2, :].rearrange("p a n -> p (a n)")
            zq = z[:, Z_Q:Z_Q + 2, :].rearrange("p a n -> p (a n)")
            le = level_e[:, :, :].rearrange("p h t -> p (h t)")
            lx0 = level_x[:, 0, :, :].rearrange("p h t -> p (h t)")
            lx1 = level_x[:, 1, :, :].rearrange("p h t -> p (h t)")
            a.wait_ge(z_ready, 10)
            step(nc.scalar.activation(le, zf, ACT.Abs))
            step(nc.scalar.activation(le, le, ACT.Exp, scale=-1.0))
            nc.scalar.activation(le, le, ACT.Ln, bias=1.0).then_inc(hg_exp, 1)
            nc.scalar.activation(lx0, zq, ACT.Exp, scale=-1.0).then_inc(hg_exp, 1)
            evac_z(10)
            evac_z(11)
            evac_z(12)
            evac_z(13)
            a.wait_ge(hg_lin, 1)
            nc.scalar.activation(lx1, lx1, ACT.Exp, scale=-1.0).then_inc(hg_exp, 1)
            for n in range(1 + len(HALVES)):
                a.wait_ge(lvl_d, n + 1)
                nc.scalar.activation(le, le, ACT.Exp).then_inc(lvl_e, 1)
            a.wait_ge(max_ready, 1)
            for tt in range(TT):
                for hd in range(ATT_H):
                    if tt == 0:
                        nc.scalar.activation(bias[:, 0, hd, :], bias[:, 0, hd, :], ACT.Exp,
                                             bias=small[:, 32 + hd:33 + hd],
                                             accum_out=small[:, 48 + hd:49 + hd]).then_inc(probs_ready, 1)
                    else:
                        nc.scalar.activation(bias[:, 1:3, hd, :], bias[:, 1:3, hd, :], ACT.Exp,
                                             bias=small[:, 40 + hd:41 + hd],
                                             accum_out=small[:, 56 + hd:57 + hd]).then_inc(probs_ready, 1)
            for n in range(14, 18):
                evac_z(n)
            a.wait_ge(brow_out, 16)
            for u in range(6):
                a.wait_ge(pT_mm, u + 1)
                nc.scalar.activation(pT[:, u // 2, 4 * (u % 2):4 * (u % 2) + 4, :],
                                     ps[:, 2 + u % 2, :].rearrange("p (h t) -> p h t", h=4),
                                     ACT.Copy).then_inc(pT_ready, 1)
            obT = acc[:, 0, :].rearrange("p (k t) -> p k t", k=4)
            oaT = acc[:, 1, :].rearrange("p (k t) -> p k t", k=4)
            a.wait_ge(mod_ready, 6)
            for tt in range(TT):
                a.wait_ge(br_mm, tt + 1)
                nc.scalar.activation(obT[:, :, tt * P:(tt + 1) * P],
                                     ps[:, 2 + tt, :].rearrange("p (k t) -> p k t", k=4), ACT.Copy).then_inc(brT_ready, 1)
            for tt in range(TT):
                a.wait_ge(o_mm, tt + 1)
                for hd in range(HGRN_H):
                    nc.scalar.activation(level_x[:, tt, hd, 0:P], ps[:, 4 + tt, hd * P:(hd + 1) * P], ACT.Square,
                                         accum_out=small[:, 16 + 4 * tt + hd:17 + 4 * tt + hd]).then_inc(o_sq, 1)
            a.wait_ge(z_ready, 14)
            nc.scalar.activation(le, z[:, Z_G:Z_G + 2, :].rearrange("p a n -> p (a n)"), ACT.Exp, scale=-1.0).then_inc(hg_exp, 1)
            rsqrt_guess(3, 16, 8)
            for tt in range(TT):
                a.wait_ge(br_mm, 2 + tt + 1)
                nc.scalar.activation(oaT[:, :, tt * P:(tt + 1) * P],
                                     ps[:, 2 + tt, :].rearrange("p (k t) -> p k t", k=4), ACT.Copy).then_inc(brT_ready, 1)
            for n in range(18, 22):
                evac_z(n)
            for tt in range(TT):
                a.wait_ge(mT_mm, tt + 1)
                copy_T(4 + 2 * tt, hT, tt, mT_ready)
            for tt in range(TT):
                a.wait_ge(out_used, 4)
                norm_square(tt)
            for tt in range(TT):
                rsqrt_guess(4 + tt, 8 * tt + 1, 1)
            for tt in range(TT):
                a.wait_ge(h2_mm, tt + 1)
                copy_T(4 + 2 * tt, hT, tt, h2T_ready)
            for tt in range(TT):
                a.wait_ge(rt_max, tt + 1)
                nc.scalar.activation(route[:, tt, 2, :], route[:, tt, 0, :], ACT.Exp,
                                     bias=small[:, 32 + tt:33 + tt]).then_inc(rt_exp, 1)
            a.wait_ge(b1_mm, 1)
            nc.scalar.activation(b1T[:, :], ps[:, 3, :], ACT.Copy).then_inc(b1_ready, 1)

            a.wait_ge(b2_mm, 2)
            a.wait_ge(y_start, 1)
            a.wait_ge(parts_ready, 2)
            def split_hi(g, u):
                wait_tile(a, g, u // 2)
                a.wait_ge(w_free, g * 24 + (u + 1))
                nc.scalar.activation(w_hi[:, u % PARTS, :], raw_unit(u), ACT.Copy).then_inc(hi_ready, 1)

            def body(g):
                def evac_h(b):
                    a.wait_ge(w_free, g * 24 + (PARTS + 4 * b + 4))
                    if b >= 2:
                        a.wait_ge(sum_mm, g * 4 + (b - 1))
                    nc.scalar.activation(hs[:, b % 2, :], ps[:, b % 2, :], ACT.Copy).then_inc(hs_ready, 1)

                def sigmoid(half):
                    a.wait_ge(glu_ready, g * 2 + (half + 1))
                    nc.scalar.activation(sig[:, :, :], glu[:, :, :], ACT.Sigmoid, scale=ALPHA).then_inc(sig_ready, 1)

                def act_hi(half):
                    a.wait_ge(a32_ready, g * 2 + (half + 1))
                    nc.scalar.activation(act[:, 4 * half:4 * half + 4, 0:SLOTS], act32[:, :, :], ACT.Copy).then_inc(ahi_ready, 1)

                for u in range(24):
                    if u == 6:
                        a.wait_ge(w_free, g * 24 + PARTS)
                        y_out()
                    if u in (7, 12, 16, 19):
                        evac_h((7, 12, 16, 19).index(u))
                    if u == 15:
                        sigmoid(0)
                    if u == 17:
                        st_copy(g + 1)
                    if u == 17:
                        act_hi(0)
                    if u == 20:
                        sigmoid(1)
                    if u == 21:
                        act_hi(1)
                    if u == 22:
                        xs_hi(g + 1)
                    if u in SPLIT:
                        split_hi(g, u)

            def y_out():
                nc.scalar.activation(ysb[:, 0:512], ps[:, 4, :], ACT.Copy).then_inc(ysb_ready, 1)
                nc.scalar.activation(ysb[:, 512:1024], ps[:, 5, :], ACT.Copy).then_inc(ysb_ready, 1)

            def xs_hi(n):
                a.wait_ge(gather_mm, n + 1)
                nc.scalar.activation(xs[:, :, 0:SLOTS], ps[:, 6, :].rearrange("p (k s) -> p k s", k=KC),
                                     ACT.Copy).then_inc(xhi_ready, 1)

            def st_copy(n):
                a.wait_ge(st_mm, n + 1)
                nc.scalar.activation(st[:, :], ps[:, 7, 0:T], ACT.Copy).then_inc(st_ready, 1)

            st_copy(0)
            xs_hi(0)
            with a.Fori(0, NE) as i:
                body(i)
            a.wait_ge(list_ready, 1)
            n_more = a.value_load(lists_i[0:1, 0:1], min_val=0, max_val=MAX_MORE)
            with a.If(n_more > 0):
                with a.Fori(0, n_more) as r:
                    body(r + NE)
            a.wait_ge(w_free, n_more * 24 + (24 * NE + PARTS))
            y_out()
            for tt in range(TT):
                a.wait_ge(fin_sq, tt + 1)
                norm_square(tt)
            for tt in range(TT):
                rsqrt_guess(6 + tt, 8 * tt + 1, 1)

        @block.vector
        def _(v):
            count = [0]

            def step(ins):
                count[0] += 1
                ins.then_inc(dve_step, 1)
                v.wait_ge(dve_step, count[0])

            def after(sem_, n, ins):
                ins.then_inc(sem_, 1)
                v.wait_ge(sem_, n)

            V = nc.vector
            v.wait_ge(c_exp, 1)
            step(V.tensor_scalar(cc[:, 2, :], cc[:, 1, :], 1.0, None, ALU.add))
            step(V.reciprocal(cc[:, 3, :], cc[:, 2, :]))
            step(V.tensor_tensor(cc[:, 1, :], cc[:, 0, :], cc[:, 3, :], ALU.mult))

            def ada_section(s):
                dst = acc[:, s % 2, :]
                if s >= 2:
                    v.wait_ge(ada_mm, s - 1)
                for n in range(4):
                    w, full, at = tile_at("ada", 4 * s + n)
                    v.wait_ge(full, at)
                    part = dst[:, 256 * n:256 * n + 256]
                    step(V.tensor_scalar(part, w[:, 0, :], cc[:, 1, 0:1], None, ALU.mult))
                    for j in range(1, KC):
                        ins = V.scalar_tensor_tensor(out=part, in0=w[:, j, :], scalar=cc[:, 1, j:j + 1], in1=part,
                                                     op0=ALU.mult, op1=ALU.add)
                        if j < KC - 1:
                            step(ins)
                        else:
                            after(ada_used, 4 * s + n + 1, ins)
                V.tensor_copy(small[:, 63:64], dst[:, 1023:1024]).then_inc(acc_ready, 1)

            def mod_section(s):
                v.wait_ge(ada_mm, s + 1)
                v.wait_ge(ld_bada[s], 16)
                for g in range(2):
                    dst = BADA_DST[s][:, 512 * g:512 * g + 512]
                    ins = V.tensor_tensor(dst, ps[:, 4 + g, :], dst, ALU.add)
                    if g == 0:
                        step(ins)
                    else:
                        after(mod_ready, s + 1, ins)

            def newton(n, lo, w, scale):
                val, guess, tmp = (small[:, lo + k * w:lo + (k + 1) * w] for k in range(3))
                step(V.tensor_scalar(val, val, scale, EPS, ALU.mult, ALU.add))
                V.tensor_copy(small[:, 62:63], val[:, 0:1]).then_inc(ln_in, 1)
                v.wait_ge(ln_out, n)
                r = tmp
                step(V.tensor_tensor(guess, r, r, ALU.mult))
                step(V.tensor_tensor(guess, guess, val, ALU.mult))
                step(V.tensor_scalar(guess, guess, -0.5, 1.5, ALU.mult, ALU.add))
                step(V.tensor_tensor(r, r, guess, ALU.mult))

            def norm(base, sq_n, shift, scale, sig):
                if scale is not None:
                    step(V.scalar_tensor_tensor(out=scale, in0=scale, scalar=1.0, in1=norm_w[:, :], op0=ALU.add, op1=ALU.mult))
                for tt in range(TT):
                    v.wait_ge(sq_done, sq_n + tt + 1)
                    step(V.tensor_copy(small[:, 8 * tt + 1:8 * tt + 2], small[:, 8 * tt:8 * tt + 1]))
                    newton(base + tt + 1, 8 * tt + 1, 1, 1.0 / D)
                    ins = V.scalar_tensor_tensor(out=h[:, tt, :], in0=x_sb[:, tt, :], scalar=small[:, 8 * tt + 3:8 * tt + 4],
                                                 in1=scale if scale is not None else norm_w[:, :],
                                                 op0=ALU.mult, op1=ALU.mult)
                    if shift is None:
                        after(sig, tt + 1, ins)
                    else:
                        step(ins)
                        after(sig, tt + 1, V.tensor_tensor(h[:, tt, :], h[:, tt, :], shift, ALU.add))

            v.wait_ge(ld_small, 16 * (N_SMALL - 3))
            step(V.tensor_copy(masks[:, :, :].rearrange("p a n -> p (a n)"), z[:, 20:22, :].rearrange("p a n -> p (a n)")))
            ada_section(0)
            ada_section(1)
            mod_section(0)
            mod_section(1)
            norm(0, 0, mod[:, 0, :], mod[:, 1, :], h_ready)
            step(V.tensor_tensor(lb[:, 1, :], lb[:, 0, :], lb[:, 0, :], ALU.subtract))
            step(V.tensor_scalar(lb[:, 2, :], lb[:, 1, :], 1.0, None, ALU.add))
            step(V.tensor_tensor(lb[:, 1, :], lb[:, 2, :], lb[:, 2, :], ALU.subtract))
            step(V.tensor_scalar(lb[:, 2, :], lb[:, 1, :], -1.0, 1.0, ALU.mult, ALU.add))
            ada_section(2)
            v.wait_ge(z_ready, 3)
            for tt in range(TT):
                S = (tt + 1) * P
                for hp in range(4):
                    u = 4 * tt + hp
                    v.wait_ge(relu_ready, u + 1)
                    for j in range(2):
                        hd = 4 * (hp // 2) + hp % 2 + 2 * j
                        iw = z[:, Z_IK, T + 8 * tt + hd:T + 8 * tt + hd + 1]
                        src = relu[:, u % 2, j * S:(j + 1) * S]
                        dst = score[:, tt, 0:S]
                        if hp == 0 and j == 0:
                            ins = V.tensor_scalar(dst, src, iw, None, ALU.mult)
                        else:
                            ins = V.scalar_tensor_tensor(out=dst, in0=src, scalar=iw, in1=dst, op0=ALU.mult, op1=ALU.add)
                        if j == 0:
                            step(ins)
                        else:
                            after(relu_used, u + 1, ins)
                V.tensor_copy(small[:, 61:62], score[:, tt, 0:1]).then_inc(score_sum, 1)
            mod_section(2)
            best = small[:, 16:24]
            for tt in range(TT):
                S = (tt + 1) * P
                v.wait_ge(score_causal, tt + 1)
                for _ in range(TOPK // 8):
                    step(V.max(out=best, in_=score[:, tt, 0:S]))
                    step(V.match_replace(out=score[:, tt, 0:S], in_to_replace=best, in_values=score[:, tt, 0:S],
                                         imm_value=PICKED))
                after(picked, tt + 1, V.tensor_scalar(score[:, tt, 0:S], score[:, tt, 0:S], PICKED / 2, DEAD, ALU.is_gt, ALU.mult))
                ada_section(3 + tt)
                mod_section(3 + tt)
            ada_section(5)
            mod_section(5)
            zf = z[:, Z_F:Z_F + 2, :].rearrange("p a n -> p (a n)")
            zq = z[:, Z_Q:Z_Q + 2, :].rearrange("p a n -> p (a n)")
            zf4 = zf.rearrange("p (h t) -> p h t", h=HGRN_H)
            zq4 = zq.rearrange("p (h t) -> p h t", h=HGRN_H)
            le = level_e[:, :, :].rearrange("p h t -> p (h t)")
            lx0 = level_x[:, 0, :, :].rearrange("p h t -> p (h t)")
            lx1 = level_x[:, 1, :, :].rearrange("p h t -> p (h t)")
            dec = decay[:, :, :].rearrange("p h t -> p (h t)")
            v.wait_ge(hg_exp, 1)
            step(V.scalar_tensor_tensor(out=dec, in0=zf, scalar=0.0, in1=le, op0=ALU.min, op1=ALU.subtract))
            after(hg_lin, 1, V.scalar_tensor_tensor(out=lx1, in0=zf, scalar=0.0, in1=le, op0=ALU.max, op1=ALU.add))
            step(V.memset(zf, 1.0))
            for hd in range(HGRN_H):
                step(V.tensor_tensor_scan(level_e[:, hd, :], zf4[:, hd, :], decay[:, hd, :], 0.0, ALU.mult, ALU.add))
            step(V.tensor_copy(dec, le))
            v.wait_ge(hg_exp, 2)
            step(V.tensor_scalar(lx0, lx0, 1.0, None, ALU.add))
            step(V.reciprocal(lx0, lx0))
            step(V.tensor_tensor(zq, zq, lx0, ALU.mult))
            v.wait_ge(hg_exp, 3)
            for hd in range(HGRN_H):
                step(V.tensor_scalar(zf4[:, hd, :], level_x[:, 1, hd, :], lb[:, 2, hd:hd + 1], None, ALU.mult))
            step(V.memset(aT[:, :, :, :], 0.0))
            for n, half in enumerate((128,) + HALVES):
                nb = T * HGRN_H // (2 * half)
                b_v = dec.rearrange("p (n w) -> p n w", w=2 * half)
                e_v = le.rearrange("p (n w) -> p n w", w=2 * half)
                x_v = level_x[:, n % 2, :, :].rearrange("p h t -> p (h t)").rearrange("p (n w) -> p n w", w=2 * half)
                k_v = zf.rearrange("p (n w) -> p n w", w=2 * half)
                q_v = zq.rearrange("p (n w) -> p n w", w=2 * half)
                mid = b_v[:, :, half - 1:half].broadcast_to([P, nb, half])
                step(V.tensor_tensor(e_v[:, :, 0:half], mid, b_v[:, :, 0:half], ALU.subtract))
                after(lvl_d, n + 1, V.tensor_tensor(e_v[:, :, half:], b_v[:, :, half:], mid, ALU.subtract))
                v.wait_ge(lvl_e, n + 1)
                if n >= 2:
                    v.wait_ge(lvl_mm, n - 1)
                step(V.tensor_tensor(x_v[:, :, 0:half], e_v[:, :, 0:half], k_v[:, :, 0:half], ALU.mult))
                after(lvl_x, n + 1, V.tensor_tensor(x_v[:, :, half:], e_v[:, :, half:], q_v[:, :, half:], ALU.mult))
                v.wait_ge(lvl_mm, n + 1)
                if n == 0:
                    after(lvl_at, 1, V.tensor_copy(aT_off[:, :, :], ps[:, 4, :].rearrange("p (h t) -> p h t", h=HGRN_H)))
                else:
                    for tt in range(TT):
                        ins = V.copy_predicated(aT[:, tt, :, :], masks[:, n - 1:n, :].broadcast_to([P, HGRN_H, P]),
                                                ps[:, 6 + tt, :].rearrange("p (h t) -> p h t", h=HGRN_H))
                        if tt == 0:
                            step(ins)
                        else:
                            after(lvl_at, n + 1, ins)
            v.wait_ge(lvl_mm, len(HALVES) + 2)
            for tt in range(TT):
                ins = V.copy_predicated(aT[:, tt, :, :], masks[:, len(HALVES):len(HALVES) + 1, :].broadcast_to([P, HGRN_H, P]),
                                        ps[:, 6 + tt, :].rearrange("p (h t) -> p h t", h=HGRN_H))
                if tt == 0:
                    step(ins)
                else:
                    after(lvl_at, len(HALVES) + 2, ins)
            v.wait_ge(bias_in, 48)
            v.wait_ge(pick_causal, 2)
            for n, (tt, s0) in enumerate(((0, 0), (1, 0), (1, 1))):
                step(V.tensor_tensor(bias[:, n, :, :], bias[:, n, :, :],
                                     score[:, tt:tt + 1, s0 * P:(s0 + 1) * P].broadcast_to([P, ATT_H, P]), ALU.add))
            for tt in range(TT):
                for hp in range(4):
                    u = 4 * tt + hp
                    v.wait_ge(logit_mm, u + 1)
                    n0, w = (0, 1) if tt == 0 else (1, 2)
                    hd = 4 * (hp // 2) + hp % 2
                    dst = bias[:, n0:n0 + w, hd:hd + 3:2, :]
                    src = ps[:, 2 + u % 2, 0:2 * w * P].rearrange("p (h n s) -> p n h s", h=2, n=w)
                    for k in range(w):
                        ins = V.scalar_tensor_tensor(out=dst[:, k], in0=src[:, k], scalar=ATT_D ** -0.5, in1=dst[:, k],
                                                     op0=ALU.mult, op1=ALU.add)
                        if k < w - 1:
                            step(ins)
                        else:
                            after(logit_ready, u + 1, ins)
            for tt in range(TT):
                if tt == 0:
                    step(V.tensor_reduce(small[:, 32:40], bias[:, 0, :, :], AX_X, ALU.max))
                else:
                    step(V.tensor_reduce(small[:, 16:32].rearrange("p (n h) -> p n h", n=2), bias[:, 1:3, :, :], AX_X, ALU.max))
                    step(V.tensor_tensor(small[:, 40:48], small[:, 16:24], small[:, 24:32], ALU.max))
            after(max_ready, 1, V.tensor_scalar(small[:, 32:48], small[:, 32:48], -1.0, None, ALU.mult))
            v.wait_ge(probs_ready, 16)
            step(V.reciprocal(small[:, 48:64], small[:, 48:64]))
            for tt in range(TT):
                v.wait_ge(av_mm, tt + 1)
                after(ob_ready, tt + 1, V.tensor_tensor(
                    relu[:, tt, :].rearrange("p (h d) -> p h d", h=ATT_H),
                    ps[:, 4 + tt, :].rearrange("p (h d) -> p h d", h=ATT_H),
                    small[:, 48 + 8 * tt:56 + 8 * tt].rearrange("p (h o) -> p h o", o=1).broadcast_to([P, ATT_H, ATT_D]), ALU.mult))
            v.wait_ge(hg_exp, 4)
            step(V.tensor_scalar(le, le, 1.0, None, ALU.add))
            step(V.reciprocal(le, le))
            zg = z[:, Z_G:Z_G + 2, :]
            step(V.tensor_tensor(zg.rearrange("p a n -> p (a n)"), zg.rearrange("p a n -> p (a n)"), le, ALU.mult))
            v.wait_ge(o_sq, 8)
            newton(3, 16, 8, 1.0 / HGRN_D)
            for tt in range(TT):
                oa = level_x[:, tt, 0:2, :].rearrange("p a t -> p (a t)")
                step(V.tensor_tensor(
                    oa.rearrange("p (h d) -> p h d", h=HGRN_H),
                    ps[:, 4 + tt, :].rearrange("p (h d) -> p h d", h=HGRN_H),
                    small[:, 32 + 4 * tt:36 + 4 * tt].rearrange("p (h o) -> p h o", o=1).broadcast_to([P, HGRN_H, P]), ALU.mult))
                step(V.tensor_tensor(oa, oa, onw[:, :], ALU.mult))
                after(oa_ready, tt + 1, V.tensor_tensor(
                    oa.rearrange("p (a n) -> p a n", a=2), oa.rearrange("p (a n) -> p a n", a=2),
                    zg[:, :, 256 * tt:256 * tt + 256], ALU.mult))
            v.wait_ge(z_ready, 22)
            zs = z[:, Z_GATE:Z_GATE + 8, :].rearrange("p a n -> p (a n)")
            step(V.tensor_scalar(zs, zs, 1.0, None, ALU.add))
            step(V.reciprocal(zs, zs))
            u = 0
            for nb in range(2):
                for tt in range(TT):
                    v.wait_ge(proj_mm, u + 1)
                    ga, gb = (z[:, Z_GATE + 4 * k + 2 * nb:Z_GATE + 4 * k + 2 * nb + 2, 256 * tt:256 * tt + 256] for k in range(2))
                    ya, yb = (ps[:, 2 * (u % 2) + k, :].rearrange("p (a n) -> p a n", a=2) for k in range(2))
                    step(V.tensor_tensor(ga, ga, ya, ALU.mult))
                    step(V.tensor_tensor(gb, gb, yb, ALU.mult))
                    after(merged, u + 1, V.tensor_tensor(
                        h[:, tt, 512 * nb:512 * nb + 512].rearrange("p (a n) -> p a n", a=2), ga, gb, ALU.add))
                    u += 1
            for n in range(4):
                v.wait_ge(out_mm, n + 1)
                for tt in range(TT):
                    cols = slice(256 * n, 256 * n + 256)
                    tmp = z[:, 4 + n, 256 * tt:256 * tt + 256]
                    step(V.tensor_tensor(tmp, ps[:, n, 256 * tt:256 * tt + 256], mod[:, 2, cols], ALU.mult))
                    ins = V.tensor_tensor(x_sb[:, tt, cols], x_sb[:, tt, cols], tmp, ALU.add)
                    if tt == 0:
                        step(ins)
                    else:
                        after(out_used, n + 1, ins)
            v.wait_ge(ld_ffn, 16)
            norm(3, 2, mod[:, 0, :], mod[:, 1, :], h2_ready)
            wk = z[:, 0, 0:128].rearrange("p (t n) -> p t n", t=TT)
            step(V.memset(wk[:, :, 0:4], 3.0e38))
            for tt in range(TT):
                R = route[:, tt]
                best = z[:, 1, 8 * tt:8 * tt + 8]
                v.wait_ge(rt_mm, tt + 1)
                step(V.tensor_tensor(R[:, 0, :], ps[:, 2 * tt, NE * tt:NE * tt + NE], br[:, :], ALU.add))
                step(V.tensor_copy(wk[:, tt, 4:36], R[:, 0, :]))
                step(V.max(out=best, in_=wk[:, tt, 0:36]))
                after(rt_max, tt + 1, V.tensor_scalar(small[:, 32 + tt:33 + tt], best[:, 4:5], -1.0, None, ALU.mult))
                step(V.match_replace(out=wk[:, tt, 0:36], in_to_replace=best, in_values=wk[:, tt, 0:36], imm_value=PICKED))
                step(V.tensor_scalar(R[:, 3, :], wk[:, tt, 4:36], PICKED / 2, None, ALU.is_lt))
                v.wait_ge(rt_exp, tt + 1)
                step(V.tensor_tensor(R[:, 4, :], R[:, 2, :], R[:, 3, :], ALU.mult))
                step(V.tensor_reduce(small[:, 34 + tt:35 + tt], R[:, 4, :], AX_X, ALU.add))
                step(V.reciprocal(small[:, 34 + tt:35 + tt], small[:, 34 + tt:35 + tt]))
                after(rt_sel, tt + 1, V.tensor_scalar(R[:, 4, :], R[:, 4, :], small[:, 34 + tt:35 + tt], None, ALU.mult))
            v.wait_ge(pos_mm, 1)
            for tt in range(TT):
                R = route[:, tt]
                step(V.tensor_scalar(R[:, 5, :], ps[:, 1, NE * tt:NE * tt + NE], 1.0, None, ALU.add))
                step(V.tensor_tensor(R[:, 5, :], R[:, 5, :], R[:, 3, :], ALU.mult))
                step(V.tensor_scalar(R[:, 5, :], R[:, 5, :], -1.0, None, ALU.add))
            step(V.tensor_scalar(small[0:96, 40:41], ps[0:96, 1, 64:65], more_c[:, 0:1], None, ALU.is_gt))
            after(flag_ready, 1, V.tensor_copy(small[0:96, 41:42], small[0:96, 40:41]))
            v.wait_ge(flag_mm, 1)
            hot = z[0:96, 2, 0:16]
            step(V.tensor_scalar(hot, iota[0:96, 0:16], ps[0:96, 1, 96:97], None, ALU.is_equal))
            after(hot_ready, 1, V.tensor_scalar(hot, hot, small[0:96, 40:41], None, ALU.mult))
            v.wait_ge(list_mm, 1)
            step(V.tensor_copy(lists[0:1, 0:1], ps[0:1, 1, 128:129]))
            step(V.tensor_copy(lists[0:1, ITEM_E + NE:ITEM_C], ps[0:1, 1, 160:176]))
            step(V.tensor_copy(lists[0:1, ITEM_C + NE:ITEM_C + NE + 16], ps[0:1, 1, 176:192]))
            after(list_ready, 1, V.tensor_copy(lists_i[0:1, 0:ITEM_C + NE + 16], lists[0:1, 0:ITEM_C + NE + 16]))
            step(V.memset(pick_g[:, :, :], 0.0))
            for tt in range(TT):
                V.tensor_copy(pick_g[:, tt, 0:NE], route[:, tt, 4, :]).then_inc(pickg_ready, 1)
            for tt in range(TT):
                rest = z[:, 4 + 2 * tt:6 + 2 * tt, :].rearrange("p a n -> p (a n)")
                step(V.tensor_copy(h_parts[:, tt, 0, :], h[:, tt, :]))
                step(V.tensor_tensor(rest, h[:, tt, :], h_parts[:, tt, 0, :], ALU.subtract))
                step(V.tensor_copy(h_parts[:, tt, 1, :], rest))
                after(parts_ready, tt + 1, V.tensor_tensor(h_parts[:, tt, 2, :], rest, h_parts[:, tt, 1, :], ALU.subtract))
            v.wait_ge(rt_mm, 2)
            after(y_start, 1, V.memset(yacc, 0.0))

            v.wait_ge(b1_ready, 1)
            b1_lin = b1T[:, :].rearrange("p (e c) -> p e c", c=16)[:, :, 8:16]
            step(V.tensor_scalar(b1_lin, b1_lin, 1.0, None, ALU.add))
            n_more = v.value_load(lists_i[0:1, 0:1], min_val=0, max_val=MAX_MORE)

            def xs_lo(n):
                v.wait_ge(xhi_ready, n + 1)
                V.tensor_tensor(xs[:, :, SLOTS:P], ps[:, 6, :].rearrange("p (k s) -> p k s", k=KC),
                                xs[:, :, 0:SLOTS].bitcast(F32), ALU.subtract).then_inc(xs_ready, 1)

            def pick_tokens(e, chunk0):
                for tt in range(TT):
                    V.tensor_scalar(pick[:, tt, :], iota[:, bass.ds(chunk0, SLOTS)], route[:, tt, 5, bass.ds(e, 1)],
                                    None, ALU.is_equal).then_inc(pick_ready, 1)

            def add_y(g, n):
                v.wait_ge(sc_mm, g * 4 + (n + 1))
                dst = yacc[:, n // 2, 512 * (n % 2):512 * (n % 2) + 512]
                V.tensor_tensor(dst, dst, ps[:, 6 + n % 2, :], ALU.add).then_inc(y_added, 1)

            def body(g, e):
                def split_lo(u):
                    v.wait_ge(hi_ready, g * len(SPLIT) + split_count(u))
                    V.tensor_tensor(w_lo[:, u % PARTS, :], raw_unit(u), w_hi[:, u % PARTS, :].bitcast(F32), ALU.subtract).then_inc(lo_ready, 1)

                def swiglu_in(half):
                    v.wait_ge(sum_mm, g * 4 + (2 * half + 2))
                    T0 = ps[:, 2, :].rearrange("p (c s) -> p c s", c=4)[:, :, 0:SLOTS]
                    T1 = ps[:, 3, :].rearrange("p (c s) -> p c s", c=4)[:, :, 0:SLOTS]
                    bg = b1T[:, bass.ds(e * 16 + 4 * half, 4)].rearrange("p (c o) -> p c o", o=1).broadcast_to([P, 4, SLOTS])
                    bl = b1T[:, bass.ds(e * 16 + (8 + 4 * half), 4)].rearrange("p (c o) -> p c o", o=1).broadcast_to([P, 4, SLOTS])
                    V.tensor_tensor(glu[:, :, :], T0, bg, ALU.add).then_inc(glu_ready, 1)
                    V.tensor_tensor(lin[:, :, :], T1, bl, ALU.add).then_inc(t_free, 1)
                    v.wait_ge(t_free, g * 2 + (half + 1))
                    V.tensor_scalar(lin[:, :, :], lin[:, :, :], 1.0 + LIMIT, 1.0 - LIMIT, ALU.min, ALU.max).then_inc(lin_ready, 1)

                def swiglu_out(half):
                    v.wait_ge(sig_ready, g * 2 + (half + 1))
                    v.wait_ge(lin_ready, g * 2 + (half + 1))
                    V.scalar_tensor_tensor(out=lin[:, :, :], in0=sig[:, :, :], scalar=SIG_LIMIT, in1=lin[:, :, :],
                                           op0=ALU.min, op1=ALU.mult).then_inc(moe_step, 1)
                    v.wait_ge(moe_step, g * 2 + (half + 1))
                    V.scalar_tensor_tensor(out=act32[:, :, :], in0=glu[:, :, :], scalar=LIMIT, in1=lin[:, :, :],
                                           op0=ALU.min, op1=ALU.mult).then_inc(a32_ready, 1)

                def act_lo(half):
                    v.wait_ge(ahi_ready, g * 2 + (half + 1))
                    V.tensor_tensor(act[:, 4 * half:4 * half + 4, SLOTS:P], act32[:, :, :],
                                    act[:, 4 * half:4 * half + 4, 0:SLOTS].bitcast(F32), ALU.subtract).then_inc(act_ready, 1)

                e_next = v.value_load(lists_i[0:1, bass.ds(g + (ITEM_E + 1), 1)], min_val=0, max_val=NE - 1)
                c_next = v.value_load(lists_i[0:1, bass.ds(g + (ITEM_C + 1), 1)], min_val=0, max_val=3 * SLOTS)
                for u in range(24):
                    if u in SPLIT:
                        split_lo(u)
                    if u == 5:
                        v.wait_ge(gather_mm, g + 1)
                        v.wait_ge(doubled, g * 4 + 4)
                        pick_tokens(e_next, c_next)
                    if u == 9:
                        add_y(g, 0)
                        add_y(g, 1)
                    if u == 12:
                        add_y(g, 2)
                        add_y(g, 3)
                    if u == 13:
                        swiglu_in(0)
                    if u == 15:
                        swiglu_out(0)
                    if u == 16:
                        act_lo(0)
                    if u == 18:
                        swiglu_in(1)
                    if u == 19:
                        swiglu_out(1)
                    if u == 20:
                        act_lo(1)
                    if u == 22:
                        xs_lo(g + 1)

            pick_tokens(0, 0)
            xs_lo(0)
            with v.Fori(0, NE) as i:
                body(i, i)
            with v.If(n_more > 0):
                with v.Fori(0, n_more) as r:
                    e = v.value_load(lists_i[0:1, bass.ds(r + (ITEM_E + NE), 1)], min_val=0, max_val=NE - 1)
                    body(r + NE, e)
            for n in range(4):
                add_y(n_more + NE, n)
            v.wait_ge(y_added, n_more * 4 + (4 * NE + 4))
            for tt in range(TT):
                step(V.tensor_tensor(yacc[:, tt, :], yacc[:, tt, :], gate_f[:, :], ALU.mult))
                after(fin_sq, tt + 1, V.tensor_tensor(x_sb[:, tt, :], x_sb[:, tt, :], yacc[:, tt, :], ALU.add))
            v.wait_ge(ld_fin, 16)
            norm(5, 4, None, None, fin_ready)

        @block.tensor
        def _(pe):
            mm = nc.tensor.matmul
            tr = nc.tensor.transpose

            def ada(s):
                pe.wait_ge(acc_ready, s + 1)
                if s >= 1:
                    pe.wait_ge(mod_ready, s)
                for g in range(2):
                    last = mm(ps[:, 4 + g, :], upper[:, 1, :], acc[:, s % 2, 512 * g:512 * g + 512], start=True, stop=True)
                last.then_inc(ada_mm, 1)

            def transposes(src, bank, tt, sig):
                for k in range(KC):
                    last = tr(ps[:, bank + k // 4, P * (k % 4):P * (k % 4) + P], src[:, tt, P * k:P * k + P], ident[:, :])
                last.then_inc(sig, 1)

            pe.wait_ge(ld_small, 16 * (N_SMALL - 3))
            pe.wait_ge(ld_first, 16 * N_FIRST)
            mm(ps[0:ATT_H, 6, 0:384], relb, bucket, start=True, stop=True).then_inc(bias_mm, 1)
            ada(0)
            ada(1)
            for tt in range(TT):
                pe.wait_ge(h_ready, tt + 1)
                transposes(h, 2 * tt, tt, tr_mm)

            def z_block(n):
                w, full, at = tile_at("in", n)
                pe.wait_ge(full, at)
                if n < 2:
                    pe.wait_ge(hT_ready, 4)
                else:
                    pe.wait_ge(z_ready, n - 1)
                bank = ps[:, n % 2, :]
                kind = Z_BLOCKS[n][0]
                if kind == "T":
                    for j in range(2):
                        for k in range(KC):
                            last = mm(bank[:, T * j:T * j + T], w[:, k, P * j:P * j + P], hT[:, k, :], start=(k == 0), stop=(k == KC - 1))
                elif kind in ("IK", "KV"):
                    for k in range(KC):
                        mm(bank[0:64, 0:T], w[:, k, 0:64], hT[:, k, :], start=(k == 0), stop=(k == KC - 1))
                    wd = 8 if kind == "IK" else 64
                    for tt in range(TT):
                        for k in range(KC):
                            last = mm(bank[:, T + wd * tt:T + wd * tt + wd], hT[:, k, tt * P:(tt + 1) * P],
                                      w[:, k, 64:64 + wd], start=(k == 0), stop=(k == KC - 1))
                else:
                    for tt in range(TT):
                        for k in range(KC):
                            last = mm(bank[:, T * tt:T * tt + T], hT[:, k, tt * P:(tt + 1) * P], w[:, k, :], start=(k == 0), stop=(k == KC - 1))
                last.then_inc(z_mm, 1)

            for n in range(6):
                z_block(n)
            pe.wait_ge(z_ready, 4)
            for u in range(8):
                tt, S = u // 4, (u // 4 + 1) * P
                if u >= 2:
                    pe.wait_ge(relu_ready, u - 1)
                r, lo = u % 4, 64 * (u % 2)
                for j in range(2):
                    last = mm(ps[:, 2 + u % 2, j * S:(j + 1) * S],
                              z[lo:lo + 64, Z_IQ + r // 2, T * j + tt * P:T * j + tt * P + P],
                              z[lo:lo + 64, Z_IK, 0:S], start=True, stop=True)
                last.then_inc(score_mm, 1)
            ada(2)
            for n in range(6, 10):
                z_block(n)
            ada(3)
            for n in range(10, 12):
                z_block(n)
            ada(4)
            for n in range(12, 14):
                z_block(n)
            ada(5)
            zf4 = z[:, Z_F:Z_F + 2, :].rearrange("p a n -> p (a n)").rearrange("p (h t) -> p h t", h=HGRN_H)
            zq4 = z[:, Z_Q:Z_Q + 2, :].rearrange("p a n -> p (a n)").rearrange("p (h t) -> p h t", h=HGRN_H)
            pe.wait_ge(mod_ready, 6)
            for n in range(len(HALVES) + 2):
                if n < len(HALVES) + 1:
                    pe.wait_ge(lvl_x, n + 1)
                if n >= 1:
                    pe.wait_ge(lvl_at, n)
                if n == 0:
                    for hd in range(HGRN_H):
                        last = mm(ps[:, 4, P * hd:P * hd + P], level_x[:, 0, hd, 0:P], level_x[:, 0, hd, P:T], start=True, stop=True)
                else:
                    for tt in range(TT):
                        for hd in range(HGRN_H):
                            sl = slice(tt * P, tt * P + P)
                            if n <= len(HALVES):
                                left = right = level_x[:, n % 2, hd, sl]
                            else:
                                left, right = zf4[:, hd, sl], zq4[:, hd, sl]
                            last = mm(ps[:, 6 + tt, P * hd:P * hd + P], left, right, start=True, stop=True)
                last.then_inc(lvl_mm, 1)
            for u in range(8):
                tt, S = u // 4, (u // 4 + 1) * P
                pe.wait_ge(relu_ready, 8)
                if u >= 2:
                    pe.wait_ge(logit_ready, u - 1)
                r, lo = u % 4, 64 * (u % 2)
                for j in range(2):
                    last = mm(ps[:, 2 + u % 2, j * S:(j + 1) * S],
                              z[lo:lo + 64, Z_QB + r // 2, T * j + tt * P:T * j + tt * P + P],
                              z[lo:lo + 64, Z_KV, 0:S], start=True, stop=True)
                last.then_inc(logit_mm, 1)
            for n in range(14, 18):
                z_block(n)
            pe.wait_ge(logit_ready, 8)
            for u in range(6):
                pe.wait_ge(probs_ready, 4 * (u % 2) + 4 if u < 2 else 12 + 4 * (u % 2))
                if u >= 2:
                    pe.wait_ge(pT_ready, u - 1)
                for k in range(4):
                    last = tr(ps[:, 2 + u % 2, P * k:P * k + P], bias[:, u // 2, 4 * (u % 2) + k, :], ident[:, :])
                last.then_inc(pT_mm, 1)
            for tt in range(TT):
                pe.wait_ge(pT_ready, 2 if tt == 0 else 6)
                for hd in range(ATT_H):
                    for k in range(tt + 1):
                        last = mm(ps[:, 4 + tt, 64 * hd:64 * hd + 64], pT[:, tt + k, hd, :],
                                  z[:, Z_KV, T + 64 * k:T + 64 * k + 64], start=(k == 0), stop=(k == tt))
                last.then_inc(av_mm, 1)
            for tt in range(TT):
                pe.wait_ge(ob_ready, tt + 1)
                for k in range(4):
                    last = tr(ps[:, 2 + tt, P * k:P * k + P], relu[:, tt, P * k:P * k + P], ident[:, :])
                last.then_inc(br_mm, 1)
            pe.wait_ge(lvl_at, len(HALVES) + 2)
            for tt in range(TT):
                for hd in range(HGRN_H):
                    vb, vc = Z_V + hd // 2, P * (hd % 2)
                    dst = ps[:, 4 + tt, P * hd:P * hd + P]
                    if tt == 1:
                        mm(dst, aT_off[:, hd, :], z[:, vb, vc:vc + P], start=True, stop=False)
                    last = mm(dst, aT[:, tt, hd, :], z[:, vb, T * tt + vc:T * tt + vc + P], start=(tt == 0), stop=True)
                last.then_inc(o_mm, 1)
            for n in range(18, 20):
                z_block(n)
            for tt in range(TT):
                pe.wait_ge(oa_ready, tt + 1)
                pe.wait_ge(brT_ready, tt + 1)
                for k in range(4):
                    last = tr(ps[:, 2 + tt, P * k:P * k + P], level_x[:, tt, 0:2, :].rearrange("p a t -> p (a t)")[:, P * k:P * k + P], ident[:, :])
                last.then_inc(br_mm, 1)
            for n in range(20, 22):
                z_block(n)
            obT = acc[:, 0, :].rearrange("p (k t) -> p k t", k=4)
            oaT = acc[:, 1, :].rearrange("p (k t) -> p k t", k=4)
            pe.wait_ge(brT_ready, 4)
            pe.wait_ge(z_ready, 22)
            u = 0
            for nb in range(2):
                for tt in range(TT):
                    if u >= 2:
                        pe.wait_ge(merged, u - 1)
                    for kind, src, bk in (("pa", oaT, 0), ("pb", obT, 1)):
                        w, full, at = tile_at(kind, nb)
                        pe.wait_ge(full, at)
                        for k in range(4):
                            last = mm(ps[:, 2 * (u % 2) + bk, :], src[:, k, tt * P:(tt + 1) * P], w[:, k, :], start=(k == 0), stop=(k == 3))
                    last.then_inc(proj_mm, 1)
                    u += 1
            for tt in range(TT):
                pe.wait_ge(merged, 3 + tt)
                transposes(h, 4 + 2 * tt, tt, mT_mm)
            for n in range(4):
                w, full, at = tile_at("out", n)
                pe.wait_ge(full, at)
                pe.wait_ge(mT_ready, 4)
                for tt in range(TT):
                    for k in range(KC):
                        last = mm(ps[:, n, T * tt:T * tt + T], hT[:, k, tt * P:(tt + 1) * P], w[:, k, :], start=(k == 0), stop=(k == KC - 1))
                last.then_inc(out_mm, 1)
            for tt in range(TT):
                pe.wait_ge(h2_ready, tt + 1)
                transposes(h, 4 + 2 * tt, tt, h2_mm)
            for tt in range(TT):
                pe.wait_ge(h2T_ready, 2 * tt + 2)
                for k in range(KC):
                    last = mm(ps[:, 2 * tt, NE * tt:NE * tt + NE], hT[:, k, tt * P:(tt + 1) * P], wr[:, k, :], start=(k == 0), stop=(k == KC - 1))
                last.then_inc(rt_mm, 1)
            pe.wait_ge(ld_b, 32)
            for m in range(4):
                last = tr(ps[:, 3, P * m:P * m + P], z[:, 16, P * m:P * m + P], ident[:, :])
            last.then_inc(b1_mm, 1)
            pe.wait_ge(rt_sel, 2)
            mm(ps[:, 1, 0:NE], upper[:, 0, :], route[:, 0, 3, :], start=True, stop=True)
            mm(ps[:, 1, NE:2 * NE], upper[:, 1, :], route[:, 0, 3, :], start=True, stop=False)
            mm(ps[:, 1, NE:2 * NE], upper[:, 0, :], route[:, 1, 3, :], start=False, stop=True)
            for k in range(3):
                for tt in range(TT):
                    last = mm(ps[32 * k:32 * k + 32, 1, 64:65], route[:, tt, 3, :], upper[:, 1, 0:1], start=(tt == 0), stop=(tt == 1))
            last.then_inc(pos_mm, 1)
            pe.wait_ge(flag_ready, 1)
            mm(ps[0:96, 1, 96:97], upper[0:96, 0, 0:96], small[0:96, 41:42], start=True, stop=True).then_inc(flag_mm, 1)
            pe.wait_ge(hot_ready, 1)
            mm(ps[0:1, 1, 128:129], small[0:96, 41:42], upper[0:96, 1, 0:1], start=True, stop=True)
            mm(ps[0:1, 1, 160:176], more_c[:, 1:2], z[0:96, 2, 0:16], start=True, stop=True)
            mm(ps[0:1, 1, 176:192], more_c[:, 0:1], z[0:96, 2, 0:16], start=True, stop=True).then_inc(list_mm, 1)
            pe.wait_ge(h2T_ready, 4)
            for n in range(2):
                mm(ps[:, 4 + n, :], ident[0:NE, :], z[0:NE, 10 + n, :], start=True, stop=True).then_inc(b2_mm, 1)

            pe.wait_ge(parts_ready, 2)
            pe.wait_ge(b1_ready, 1)
            n_more = pe.value_load(lists_i[0:1, 0:1], min_val=0, max_val=MAX_MORE)
            pe.nop().then_inc(w_free, PARTS)

            def turn_gates(n):
                for tt in range(TT):
                    last = tr(ps[:, 7, P * tt:P * tt + P], pick_g[:, tt, :], ident[:, :])
                last.then_inc(st_mm, 1)

            def gather(n):
                pe.wait_ge(pick_ready, n * 2 + 2)
                for k in range(KC):
                    for tt in range(TT):
                        for part in range(3):
                            last = mm(ps[:, 6, SLOTS * k:SLOTS * k + SLOTS], h_parts[:, tt, part, P * k:P * k + P], pick[:, tt, :],
                                      start=(tt == 0 and part == 0), stop=(tt == 1 and part == 2))
                last.then_inc(gather_mm, 1)

            def into_tokens(g, n):
                if n == 0:
                    pe.wait_ge(ysb_ready, g * 2 + 2)
                    pe.wait_ge(st_ready, g + 1)
                if n >= 2:
                    pe.wait_ge(y_added, g * 4 + (n - 1))
                mm(ps[:, 6 + n % 2, :], st[:, P * (n // 2):P * (n // 2) + P], ysb[:, 512 * (n % 2):512 * (n % 2) + 512],
                   start=True, stop=True).then_inc(sc_mm, 1)

            def body(g):
                def operands(u, stationary):
                    if u in WHOLE:
                        wait_tile(pe, g, u // 2)
                        return [(stationary.bitcast(F32), raw_unit(u))]
                    pe.wait_ge(lo_ready, g * len(SPLIT) + split_count(u))
                    return [(stationary, w_hi[:, u % PARTS, :]), (stationary, w_lo[:, u % PARTS, :])]

                def w1_unit(u):
                    b, k0 = u // 4, 2 * (u % 4)
                    pairs = operands(u, xs[:, k0:k0 + 2, :])
                    for kk in range(2):
                        for n, (x_, w_) in enumerate(pairs):
                            last = mm(ps[:, b % 2, :], x_[:, kk, :], w_[:, 512 * kk:512 * kk + 512],
                                      start=(k0 + kk == 0 and n == 0), stop=(k0 + kk == KC - 1 and n == len(pairs) - 1))
                    last.then_inc(w_free, 1)

                def fold_block(b):
                    pe.wait_ge(hs_ready, g * 4 + (b + 1))
                    if b == 2:
                        pe.wait_ge(t_free, g * 2 + 1)
                    for cch in range(4):
                        last = mm(ps[:, 2 + b % 2, P * cch:P * cch + P], hs[:, b % 2, P * cch:P * cch + P], fold[:, :], start=True, stop=True)
                    last.then_inc(sum_mm, 1)

                def w2_unit(u):
                    fc = u - 16
                    pairs = operands(u, act[:, fc, :])
                    for n, (a_, w_) in enumerate(pairs):
                        for nb in range(2):
                            last = mm(ps[:, 4 + nb, :], a_, w_[:, 512 * nb:512 * nb + 512],
                                      start=(fc == 0 and n == 0), stop=(fc == 7 and n == len(pairs) - 1))
                    last.then_inc(w_free, 1)

                pe.wait_ge(xs_ready, g + 1)
                for u in range(24):
                    if u == 16 or u == 20:
                        pe.wait_ge(act_ready, g * 2 + (u // 4 - 3))
                    if u < 16:
                        w1_unit(u)
                    else:
                        w2_unit(u)
                    if u == 6:
                        into_tokens(g, 0)
                        into_tokens(g, 1)
                    if u == 5:
                        fold_block(0)
                    if u == 9:
                        into_tokens(g, 2)
                        into_tokens(g, 3)
                    if u == 9:
                        fold_block(1)
                    if u == 13:
                        pe.wait_ge(y_added, g * 4 + 4)
                        pe.wait_ge(doubled, g * 4 + 4)
                        turn_gates(g + 1)
                    if u == 14:
                        gather(g + 1)
                    if u == 14:
                        fold_block(2)
                    if u == 16:
                        fold_block(3)

            pe.wait_ge(pickg_ready, 2)
            turn_gates(0)
            gather(0)
            with pe.Fori(0, NE) as i:
                body(i)
            with pe.If(n_more > 0):
                with pe.Fori(0, n_more) as r:
                    body(r + NE)
            for n in range(4):
                into_tokens(n_more + NE, n)


_INS = ["x", "c", "w_ada", "b_ada", "norm_mix_w", "w_in", "hgrn_lb_logits", "hgrn_norm_w", "rel_bias",
        "w_proj_a", "w_proj_b", "w_out", "norm_ffn_w", "w_router", "b_router", "w_mlp1", "b_mlp1",
        "w_mlp2", "b_mlp2", "final_norm_w"]


def constants():
    import math
    import numpy as np

    f = np.float32
    ident = np.eye(128, dtype=f)
    half = np.arange(128) % 64
    fold = (half[:, None] == half[None, :]).astype(f)
    dist = 255 - np.arange(256)
    large = 16 + (np.log(np.maximum(dist, 1).astype(f) / f(16)) / f(math.log(8)) * f(16)).astype(np.int32)
    bucket = np.where(dist < 16, dist, np.minimum(large, 31))
    hot = np.zeros((32, 384), f)
    hot[bucket, np.arange(256)] = 1
    s, t = np.arange(128)[:, None], np.arange(128)[None, :]
    masks = [(s // (2 * m) == t // (2 * m)) & (s % (2 * m) < m) & (t % (2 * m) >= m) for m in HALVES]
    masks = np.stack(masks + [s == t], 1).astype(f).reshape(128, 8 * 128)
    iota = np.broadcast_to(np.arange(256, dtype=f), (128, 256)).copy()
    upper = np.concatenate([(s < t).astype(f), np.ones((128, 128), f)], 1)
    q = np.arange(96)
    more = np.stack([64 * (q // 32 + 1), q % 32, q // 32 + 1, 0 * q], 1).astype(f)
    n = 32 + MAX_MORE + 1
    items = np.zeros((1, 2 * n + 1), f)
    items[0, 1:33] = np.arange(32)
    return {"k_ident": ident, "k_fold": fold, "k_bucket": hot, "k_masks": masks, "k_iota": iota,
            "k_upper": upper, "k_more": more, "k_items": items}


def kernel(**inputs):
    import numpy as np
    import concourse.bacc as bacc
    from concourse.bass_utils import run_bass_kernel_spmd

    nc = bacc.Bacc("TRN2", target_bir_lowering=False, num_devices=1)
    arrays, args = {}, []
    for name, a in [(n, inputs[n]) for n in _INS] + list(constants().items()):
        a = np.ascontiguousarray(a)
        arrays[f"in_{name}_dram"] = a
        args.append(nc.dram_tensor(f"in_{name}_dram", a.shape, mybir.dt.from_np(a.dtype), kind="ExternalInput").ap())
    out = nc.dram_tensor("out_0_dram", (1, 256, 1024), F32, kind="ExternalOutput").ap()
    build(nc, *args, out)
    r = run_bass_kernel_spmd(nc, [arrays], core_ids=[0])
    return r.results[0]["out_0_dram"]
```

```python
import math
from contextlib import ExitStack

import concourse.bass as bass
from concourse import mybir

P = 128
F32 = mybir.dt.float32
F32R = mybir.dt.float32r
BF16 = mybir.dt.bfloat16
I32 = mybir.dt.int32
U8 = mybir.dt.uint8
ALU = mybir.AluOpType
ACT = mybir.ActivationFunctionType
AX_X = mybir.AxisListType.X

EPS = 1e-6
HGRN_H, HGRN_D = 4, 128
ATT_H, ATT_D = 8, 64
TOPK = 64
TOP_E = 4
LIMIT, ALPHA = 7.0, 1.702
SIG_LIMIT = 1.0 / (1.0 + math.exp(-ALPHA * LIMIT))
SLOTS = 64
MAX_MORE = 15
DEAD, PICKED = -1.0e30, -3.0e38
RING = 6
TILES = 12
PARTS = 8
WHOLE = (1, 21)
SPLIT = [u for u in range(24) if u not in WHOLE]
EARLY = [u for u in SPLIT if u < PARTS]
HALVES = (64, 32, 16, 8, 4, 2, 1)

Z_BLOCKS = (
    [("T", 2688 + 256 * i, 256) for i in range(2)]
    + [("IK", 3200, 72), ("KV", 2560, 128)]
    + [("T", 2048 + 256 * i, 256) for i in range(2)]
    + [("T", 512 + 256 * i, 256) for i in range(2)]
    + [("T", 256 * i, 256) for i in range(2)]
    + [("N", 1024 + 256 * i, 256) for i in range(2)]
    + [("N", 1536 + 256 * i, 256) for i in range(2)]
    + [("GATE", 3272 + 256 * i, 256) for i in range(8)]
)
Z_IQ, Z_IK, Z_KV, Z_QB, Z_F, Z_Q, Z_V, Z_G, Z_GATE = 0, 2, 3, 4, 6, 8, 10, 12, 14


def mixer_stream():
    tiles = []
    for n in range(4):
        tiles += [("ada", n), ("ada", 4 + n)]
    ada_after = {0: 1, 1: 1, 2: 2, 6: 1, 7: 1, 8: 1, 9: 3, 12: 1, 14: 1, 16: 1, 17: 1, 18: 1, 19: 1}
    ada = 8
    for n in range(len(Z_BLOCKS)):
        tiles.append(("in", n))
        for _ in range(ada_after.get(n, 0)):
            tiles.append(("ada", ada))
            ada += 1
    assert ada == 24
    tiles += [("pa", 0), ("pb", 0), ("pa", 1), ("pb", 1)]
    tiles += [("out", n) for n in range(4)]
    return tiles


def build(nc, x, c, w_ada, b_ada, norm_mix_w, w_in, hgrn_lb_logits, hgrn_norm_w, rel_bias, w_proj_a,
          w_proj_b, w_out, norm_ffn_w, w_router, b_router, w_mlp1, b_mlp1, w_mlp2, b_mlp2,
          final_norm_w, k_ident, k_fold, k_bucket, k_masks, k_iota, k_upper, k_more, k_items, out):
    T, D = x.shape[1], x.shape[2]
    TT, KC = T // P, D // P
    NE, FF2 = w_mlp1.shape[1], w_mlp1.shape[3]
    FF = FF2 // 2
    assert (T, D, TT, KC, NE, FF) == (256, 1024, 2, 8, 32, 1024)

    stream = mixer_stream()
    place = {key: (n % RING, 16 * (n // RING + 1)) for n, key in enumerate(stream)}
    MIX_ROUNDS = len(stream) // RING
    assert len(stream) % RING == 0

    bias_dram = nc.dram_tensor("bias_rows", [ATT_H, P, 384], F32, kind="Internal").ap()

    ctx = ExitStack()
    with ctx:
        def sem(name):
            return ctx.enter_context(nc.semaphore(name))

        def sb(name, shape, dt, stack=ctx):
            return stack.enter_context(nc.sbuf_tensor(name, shape, dt))

        ident = sb("ident", [P, P], F32)
        fold = sb("fold", [P, P], F32)
        iota = sb("iota", [P, 256], F32)
        x_sb = sb("x_sb", [P, TT, D], F32)
        h = sb("h", [P, TT, D], F32)
        hT = sb("hT", [P, KC, T], F32)
        mod = sb("mod", [P, 3, D], F32)
        gate_f = sb("gate_f", [P, D], F32)
        norm_w = sb("norm_w", [P, D], F32)
        raw_ring = sb("raw_ring", [P, RING, 2048], F32)
        ITEM_E, ITEM_C = 1, 1 + NE + MAX_MORE + 1
        route = sb("route", [P, TT, 8, NE], F32)
        small = sb("small", [P, 68], F32)
        lists = sb("lists", [1, 128], F32)
        lists_i = sb("lists_i", [1, 128], I32)

        mix = ExitStack()
        with mix:
            bias = sb("bias", [P, 3, ATT_H, P], F32, mix)
            relu = sb("relu", [P, 2, 512], F32, mix)
            score = sb("score", [P, TT, T], F32, mix)
            pT = sb("pT", [P, 3, ATT_H, P], F32, mix)
            decay = sb("decay", [P, HGRN_H, T], F32, mix)
            level_e = sb("level_e", [P, HGRN_H, T], F32, mix)
            level_x = sb("level_x", [P, 2, HGRN_H, T], F32, mix)
            aT = sb("aT", [P, 2, HGRN_H, P], F32, mix)
            aT_off = sb("aT_off", [P, HGRN_H, P], F32, mix)
            z = sb("z", [P, len(Z_BLOCKS), 512], F32, mix)
            acc = sb("acc", [P, 2, D], F32, mix)
            masks = sb("masks", [P, 8, P], U8, mix)
            upper = sb("upper", [P, 2, P], F32, mix)
            onw = sb("onw", [P, 512], F32, mix)
            lb = sb("lb", [P, 4, HGRN_H], F32, mix)
            wr = sb("wr", [P, KC, NE], F32, mix)
            br = sb("br", [P, NE], F32, mix)
            cc = sb("cc", [P, 4, KC], F32, mix)
            more_c = sb("more_c", [96, 4], F32, mix)
        c_wide = z[:, Z_GATE + 2:Z_GATE + 4, :].rearrange("p a n -> p (a n)").rearrange("p (j m) -> p j m", j=KC)
        level_es = [level_e[:, :, :].rearrange("p h t -> p (h t)"),
                    z[:, Z_GATE + 6:Z_GATE + 8, :].rearrange("p a n -> p (a n)")]
        bucket = pT[0:32, 0, 0:3, :].rearrange("p a n -> p (a n)")
        brow = pT[0:ATT_H, 1, 0:3, :].rearrange("p a n -> p (a n)")
        relb = pT[0:32, 2, 0, 0:ATT_H]
        moe = ctx
        w_hi = sb("w_hi", [P, PARTS, 1024], F32R, moe)
        w_lo = sb("w_lo", [P, PARTS, 1024], F32R, moe)
        xs = sb("xs", [P, KC, P], F32R, moe)
        act = sb("act", [P, KC, P], F32R, moe)
        sb("z_scratch_kept", [P, 4096], F32, moe)
        h_parts = sb("h_parts", [P, TT, 3, D], BF16, moe)
        b1T = sb("b1T", [P, NE * 16], F32, moe)
        st = sb("st", [P, T], F32, moe)
        pick = sb("pick", [P, TT, SLOTS], BF16, moe)
        pick_g = sb("pick_g", [P, TT, P], F32, moe)
        glu = sb("glu", [P, 4, SLOTS], F32, moe)
        lin = sb("lin", [P, 4, SLOTS], F32, moe)
        sig = sb("sig", [P, 4, SLOTS], F32, moe)
        act32 = sb("act32", [P, 4, SLOTS], F32, moe)
        hs = h[:, 0, :].rearrange("p (b n) -> p b n", b=2)
        ysb = h[:, 1, :]
        yacc = hT[:, :, :].rearrange("p k t -> p (k t)").rearrange("p (a n) -> p a n", a=TT)

        ps = ctx.enter_context(nc.psum_tensor("ps", [P, 8, 512], F32))

        ld_first = sem("ld_first")
        ld_small = sem("ld_small")
        ld_x = sem("ld_x")
        ld_mix = sem("ld_mix")
        ld_bias = sem("ld_bias")
        ld_upper = sem("ld_upper")
        ld_bada = [sem(f"ld_bada{n}") for n in range(6)]
        ld_ffn = sem("ld_ffn")
        ld_fin = sem("ld_fin")
        ld_b = sem("ld_b")
        raw_full = [sem(f"raw_full{s}") for s in range(RING)]
        ada_used = sem("ada_used")
        ada_taken = sem("ada_taken")
        c_ready = sem("c_ready")
        dve_step = sem("dve_step")
        act_step = sem("act_step")
        c_exp = sem("c_exp")
        acc_ready = sem("acc_ready")
        ada_mm = sem("ada_mm")
        mod_ready = sem("mod_ready")
        sq_done = sem("sq_done")
        ln_in = sem("ln_in")
        ln_out = sem("ln_out")
        h_ready = sem("h_ready")
        tr_mm = sem("tr_mm")
        hT_ready = sem("hT_ready")
        z_mm = sem("z_mm")
        z_ready = sem("z_ready")
        bias_mm = sem("bias_mm")
        brow_ready = sem("brow_ready")
        brow_out = sem("brow_out")
        bias_in = sem("bias_in")
        score_mm = sem("score_mm")
        relu_ready = sem("relu_ready")
        relu_used = sem("relu_used")
        score_sum = sem("score_sum")
        score_causal = sem("score_causal")
        picked = sem("picked")
        pick_causal = sem("pick_causal")
        logit_mm = sem("logit_mm")
        logit_ready = sem("logit_ready")
        max_ready = sem("max_ready")
        probs_ready = sem("probs_ready")
        pT_mm = sem("pT_mm")
        pT_ready = sem("pT_ready")
        av_mm = sem("av_mm")
        ob_ready = sem("ob_ready")
        hg_exp = sem("hg_exp")
        hg_lin = sem("hg_lin")
        lvl_d = sem("lvl_d")
        lvl_e = sem("lvl_e")
        lvl_x = sem("lvl_x")
        lvl_mm = sem("lvl_mm")
        lvl_at = sem("lvl_at")
        o_mm = sem("o_mm")
        o_sq = sem("o_sq")
        oa_ready = sem("oa_ready")
        br_mm = sem("br_mm")
        brT_ready = sem("brT_ready")
        proj_mm = sem("proj_mm")
        merged = sem("merged")
        mT_mm = sem("mT_mm")
        mT_ready = sem("mT_ready")
        out_mm = sem("out_mm")
        out_used = sem("out_used")
        h2_ready = sem("h2_ready")
        h2_mm = sem("h2_mm")
        h2T_ready = sem("h2T_ready")
        rt_mm = sem("rt_mm")
        rt_max = sem("rt_max")
        rt_exp = sem("rt_exp")
        rt_sel = sem("rt_sel")
        pos_mm = sem("pos_mm")
        flag_ready = sem("flag_ready")
        flag_mm = sem("flag_mm")
        hot_ready = sem("hot_ready")
        list_mm = sem("list_mm")
        list_ready = sem("list_ready")
        b1_mm = sem("b1_mm")
        b1_ready = sem("b1_ready")
        b2_mm = sem("b2_mm")
        y_start = sem("y_start")
        parts_ready = sem("parts_ready")
        hi_ready = sem("hi_ready")
        lo_ready = sem("lo_ready")
        w_free = sem("w_free")
        pick_ready = sem("pick_ready")
        pickg_ready = sem("pickg_ready")
        lin_ready = sem("lin_ready")
        doubled = sem("doubled")
        gather_mm = sem("gather_mm")
        xhi_ready = sem("xhi_ready")
        xs_ready = sem("xs_ready")
        st_mm = sem("st_mm")
        st_ready = sem("st_ready")
        hs_ready = sem("hs_ready")
        sum_mm = sem("sum_mm")
        glu_ready = sem("glu_ready")
        sig_ready = sem("sig_ready")
        a32_ready = sem("a32_ready")
        ahi_ready = sem("ahi_ready")
        act_ready = sem("act_ready")
        t_free = sem("t_free")
        ysb_ready = sem("ysb_ready")
        sc_mm = sem("sc_mm")
        y_added = sem("y_added")
        moe_step = sem("moe_step")
        fin_sq = sem("fin_sq")
        fin_ready = sem("fin_ready")
        st_out = sem("st_out")

        N_FIRST, N_SMALL = 2, 8
        bada_rows = b_ada[0].rearrange("(s n) -> s n", n=D)
        BADA_DST = [mod[:, 0, :], mod[:, 1, :], mod[:, 2, :], mod[:, 0, :], mod[:, 1, :], gate_f[:, :]]

        def raw(s):
            return raw_ring[:, s, :]

        def raw_unit(u):
            return raw_ring[:, (u // 2) % RING, 1024 * (u % 2):1024 * (u % 2) + 1024]

        def tile_src(kind, n):
            if kind == "ada":
                return w_ada[0].rearrange("(p j) n -> p j n", j=KC)[:, :, 256 * n:256 * n + 256]
            if kind == "in":
                _, c0, w = Z_BLOCKS[n]
                return w_in[0].rearrange("(k p) n -> p k n", p=P)[:, :, c0:c0 + w]
            if kind in ("pa", "pb"):
                w = (w_proj_a if kind == "pa" else w_proj_b)[0]
                return w.rearrange("(k p) n -> p k n", p=P)[:, :, 512 * n:512 * n + 512]
            return w_out[0].rearrange("(k p) n -> p k n", p=P)[:, :, 256 * n:256 * n + 256]

        def tile_at(kind, n):
            s, full = place[(kind, n)]
            a, w = tile_src(kind, n).shape[1:]
            return raw(s)[:, 0:a * w].rearrange("p (a w) -> p a w", a=a), raw_full[s], full

        w1_v = w_mlp1[0].rearrange("e (k p) n -> p e k n", p=P)
        w2_v = w_mlp2[0].rearrange("e (k p) n -> p e k n", p=P)
        W1_COL = [0, FF, 512, FF + 512]

        def split_count(u):
            return sum(n <= u for n in SPLIT)

        def wait_tile(engine, g, q):
            engine.wait_ge(raw_full[q % RING], g * (16 * TILES // RING) + 16 * (MIX_ROUNDS + q // RING + 1))

        PE_SECTION = 1

        def dve_section(s):
            return s - (s > PE_SECTION)

        def level_bank(n):
            return 4 if n % 2 == 0 else 6

        block = ctx.enter_context(nc.Block())

        @block.sync
        def _(sp):
            def slot_read(kind, i):
                if kind == "ada" and i // 4 == PE_SECTION:
                    sp.wait_ge(ada_taken, i % 4 + 1)
                elif kind == "ada":
                    sp.wait_ge(ada_used, 4 * dve_section(i // 4) + i % 4 + 1)
                elif kind == "in":
                    sp.wait_ge(z_mm, i + 1)
                elif kind == "out":
                    sp.wait_ge(out_mm, i + 1)
                else:
                    sp.wait_ge(proj_mm, 2 * i + 2)

            for n, (kind, i) in enumerate(stream):
                if n >= RING:
                    slot_read(*stream[n - RING])
                dst, full, _ = tile_at(kind, i)
                sp.dma_start(dst, tile_src(kind, i)).then_inc(full, 16)

            def expert_tile(e, q):
                dst = raw(q % RING)
                if q < 8:
                    c0 = W1_COL[q // 2]
                    src = w1_v[:, bass.ds(e, 1), 4 * (q % 2):4 * (q % 2) + 4, c0:c0 + 512]
                    dst = dst.rearrange("p (k n) -> p k n", k=4)
                else:
                    src = w2_v[:, bass.ds(e, 1), 2 * (q - 8):2 * (q - 8) + 2, :]
                    dst = dst.rearrange("p (k n) -> p k n", k=2)
                sp.dma_start(dst, src.rearrange("p e k n -> p (e k) n")).then_inc(raw_full[q % RING], 16)

            def slot_free(g, q):
                if any(u in SPLIT for u in (2 * q, 2 * q + 1)):
                    sp.wait_ge(lo_ready, g * len(SPLIT) + split_count(2 * q + 1))
                for u in (2 * q, 2 * q + 1):
                    if u in WHOLE:
                        sp.wait_ge(w_free, g * 24 + (PARTS + u + 1))

            def item_tiles(g, e):
                for q in range(TILES):
                    if q < RING:
                        slot_free(g - 1, q + TILES - RING)
                    else:
                        slot_free(g, q - RING)
                    expert_tile(e, q)

            for q in range(TILES):
                if q < RING:
                    slot_read(*stream[len(stream) - RING + q])
                else:
                    slot_free(0, q - RING)
                expert_tile(0, q)
            with sp.Fori(1, NE) as i:
                item_tiles(i, i)
            sp.wait_ge(list_ready, 1)
            n_more = sp.value_load(lists_i[0:1, 0:1], min_val=0, max_val=MAX_MORE)
            with sp.If(n_more > 0):
                with sp.Fori(0, n_more) as r:
                    e = sp.value_load(lists_i[0:1, bass.ds(r + (ITEM_E + NE), 1)], min_val=0, max_val=NE - 1)
                    item_tiles(r + NE, e)
            for tt in range(TT):
                sp.wait_ge(fin_ready, tt + 1)
                sp.dma_start(out[0, tt * P:(tt + 1) * P, :], h[:, tt, :]).then_inc(st_out, 16)
            sp.wait_ge(st_out, 32)

        @block.gpsimd
        def _(pool):
            pool.dma_start(bucket, k_bucket).then_inc(ld_bias, 16)
            pool.dma_start(relb, rel_bias).then_inc(ld_bias, 16)
            for n in range(2):
                pool.dma_start(BADA_DST[n], bada_rows[n:n + 1, :].broadcast_to([P, D])).then_inc(ld_bada[n], 16)
            pool.dma_start(norm_w[:, :], norm_mix_w[0:1, :].broadcast_to([P, D])).then_inc(ld_mix, 16)
            small_loads = [
                (fold[:, :], k_fold), (iota[:, :], k_iota),
                (z[:, 20:22, :].rearrange("p a n -> p (a n)"), k_masks),
                (onw[:, :], hgrn_norm_w[0:1, :].broadcast_to([P, 512])),
                (wr[:, :, :], w_router[0].rearrange("(k p) n -> p k n", p=P)),
                (br[:, :], b_router[0:1, :].broadcast_to([P, NE])),
                (more_c[:, :], k_more),
                (lists[0:1, 0:2 * (NE + MAX_MORE + 1) + 1], k_items),
            ]
            pool.wait_ge(ada_taken, 3)
            for dst, src in small_loads:
                pool.dma_start(dst, src).then_inc(ld_small, 16)
            pool.dma_start(BADA_DST[2], bada_rows[2:3, :].broadcast_to([P, D])).then_inc(ld_bada[2], 16)
            assert len(small_loads) == N_SMALL

            pool.wait_ge(brow_ready, 1)
            pool.dma_start(bias_dram, brow.rearrange("h (o j) -> h o j", o=1).broadcast_to([ATT_H, P, 384])).then_inc(brow_out, 16)
            pool.wait_ge(brow_out, 16)
            for n, (tt, st_) in enumerate(((0, 0), (1, 0), (1, 1))):
                src = bass.AP(tensor=bias_dram.tensor, offset=255 - tt * P + st_ * P,
                              ap=[[383, P], [384 * P, ATT_H], [1, P]])
                pool.dma_start(bias[:, n, :, :], src).then_inc(bias_in, 16)

            pool.wait_ge(h_ready, 2)
            for n in range(3, 6):
                pool.dma_start(BADA_DST[n], bada_rows[n:n + 1, :].broadcast_to([P, D])).then_inc(ld_bada[n], 16)
            pool.dma_start(norm_w[:, :], norm_ffn_w[0:1, :].broadcast_to([P, D])).then_inc(ld_ffn, 16)

            for tt in range(TT):
                S = (tt + 1) * P
                pool.wait_ge(score_sum, tt + 1)
                nc.gpsimd.affine_select(out=score[:, tt, 0:S], in_=score[:, tt, 0:S], compare_op=ALU.is_ge,
                                        fill=DEAD, base=tt * P, pattern=[[-1, S]],
                                        channel_multiplier=1).then_inc(score_causal, 1)
            for tt in range(TT):
                S = (tt + 1) * P
                pool.wait_ge(picked, tt + 1)
                nc.gpsimd.affine_select(out=score[:, tt, 0:S], in_=score[:, tt, 0:S], compare_op=ALU.is_ge,
                                        fill=DEAD, base=tt * P, pattern=[[-1, S]],
                                        channel_multiplier=1).then_inc(pick_causal, 1)
            pool.wait_ge(merged, 4)
            pool.dma_start(z[:, 16:17, :].rearrange("p a (m n) -> p (a m) n", m=4),
                           b_mlp1[0].rearrange("e (c n) -> (e c) n", n=P)
                           .rearrange("(m p) n -> p m n", p=P)).then_inc(ld_b, 16)
            pool.dma_start(z[0:NE, 10:12, :].rearrange("p a n -> p (a n)"), b_mlp2[0]).then_inc(ld_b, 16)
            pool.wait_ge(h2_ready, 2)
            pool.dma_start(norm_w[:, :], final_norm_w.rearrange("(a n) -> a n", a=1).broadcast_to([P, D])).then_inc(ld_fin, 16)

            pool.wait_ge(rt_mm, 2)
            nc.gpsimd.memset(yacc, 0.0).then_inc(y_start, 1)

            pool.wait_ge(list_ready, 1)
            pool.wait_ge(y_start, 1)
            n_more = pool.value_load(lists_i[0:1, 0:1], min_val=0, max_val=MAX_MORE)

            def body(g):
                e = pool.value_load(lists_i[0:1, bass.ds(g + ITEM_E, 1)], min_val=0, max_val=NE - 1)
                pool.wait_ge(pick_ready, g * 2 + 2)
                pool.wait_ge(st_mm, g + 1)
                for tt in range(TT):
                    gate = route[:, tt, 4, bass.ds(e, 1)].broadcast_to([P, SLOTS])
                    for k in range(2):
                        nc.gpsimd.tensor_tensor(pick_g[:, tt, k * SLOTS:(k + 1) * SLOTS], pick[:, tt, :], gate,
                                                ALU.mult).then_inc(doubled, 1)

            with pool.Fori(0, NE) as i:
                body(i)
            with pool.If(n_more > 0):
                with pool.Fori(0, n_more) as r:
                    body(r + NE)

        @block.scalar
        def _(a):
            a.dma_start(cc[:, 0, :], c[0].rearrange("(p j) -> p j", j=KC)).then_inc(ld_first, 16)
            a.dma_start(ident[:, :], k_ident).then_inc(ld_first, 16)
            a.dma_start(upper[:, :, :], k_upper.rearrange("p (a n) -> p a n", a=2)).then_inc(ld_upper, 16)
            a.dma_start(x_sb[:, :, :], x[0].rearrange("(t p) d -> p t d", p=P)).then_inc(ld_x, 16)
            a.dma_start(lb[:, 0, :], hgrn_lb_logits[0].rearrange("(h d) -> d h", d=P), allow_slow_non_contiguous=True).then_inc(ld_x, 16)

            count = [0]

            def step(ins):
                count[0] += 1
                ins.then_inc(act_step, 1)
                a.wait_ge(act_step, count[0])

            a.wait_ge(ld_first, 16 * N_FIRST)
            nc.scalar.activation(cc[:, 1, :], cc[:, 0, :], ACT.Exp, scale=-1.0).then_inc(c_exp, 1)
            a.wait_ge(ld_x, 32)

            def norm_square(tt):
                nc.scalar.activation(h[:, tt, :], x_sb[:, tt, :], ACT.Square,
                                     accum_out=small[:, tt:tt + 1]).then_inc(sq_done, 1)

            def rsqrt_guess(n, lo, w):
                a.wait_ge(ln_in, n)
                step(nc.scalar.activation(small[:, lo + w:lo + 2 * w], small[:, lo:lo + w], ACT.Ln))
                nc.scalar.activation(small[:, lo + 2 * w:lo + 3 * w], small[:, lo + w:lo + 2 * w], ACT.Exp,
                                     scale=-0.5).then_inc(ln_out, 1)

            def copy_T(src_banks, dst, tt, sig):
                for g in range(2):
                    nc.scalar.activation(dst[:, 4 * g:4 * g + 4, tt * P:(tt + 1) * P],
                                         ps[:, src_banks + g, :].rearrange("p (k t) -> p k t", k=4),
                                         ACT.Copy).then_inc(sig, 1)

            for tt in range(TT):
                norm_square(tt)
            rsqrt_guess(1, TT, TT)
            a.wait_ge(bias_mm, 1)
            nc.scalar.activation(brow, ps[0:ATT_H, 3, 0:384], ACT.Copy).then_inc(brow_ready, 1)
            for tt in range(TT):
                a.wait_ge(tr_mm, tt + 1)
                copy_T(2 * tt, hT, tt, hT_ready)


            def evac_z(n):
                a.wait_ge(z_mm, n + 1)
                bank = ps[:, n % 2, :]
                kind = Z_BLOCKS[n][0]
                if kind == "IK":
                    nc.scalar.activation(z[0:64, n, 0:T], bank[0:64, 0:T], ACT.Copy)
                    nc.scalar.activation(z[64:128, n, 0:T], bank[0:64, 0:T], ACT.Copy)
                    nc.scalar.activation(z[:, n, T:T + 16], bank[:, T:T + 16], ACT.Copy,
                                         scale=ATT_H ** -0.5 * ATT_D ** -0.5).then_inc(z_ready, 1)
                elif kind == "KV":
                    nc.scalar.activation(z[0:64, n, 0:T], bank[0:64, 0:T], ACT.Copy)
                    nc.scalar.activation(z[64:128, n, 0:T], bank[0:64, 0:T], ACT.Copy)
                    nc.scalar.activation(z[:, n, T:T + 128], bank[:, T:T + 128], ACT.Copy).then_inc(z_ready, 1)
                elif kind == "GATE":
                    nc.scalar.activation(z[:, n, :], bank, ACT.Sigmoid).then_inc(z_ready, 1)
                else:
                    nc.scalar.activation(z[:, n, :], bank, ACT.Copy).then_inc(z_ready, 1)

            for n in range(3):
                evac_z(n)
            for u in range(8):
                S = (u // 4 + 1) * P
                a.wait_ge(score_mm, u + 1)
                if u >= 2:
                    a.wait_ge(relu_used, u - 1)
                nc.scalar.activation(relu[:, u % 2, 0:2 * S], ps[:, 2 + u % 2, 0:2 * S], ACT.Relu).then_inc(relu_ready, 1)
            for n in range(3, 6):
                evac_z(n)
            a.wait_ge(max_ready, 1)
            for tt in range(TT):
                for hd in range(ATT_H):
                    if tt == 0:
                        nc.scalar.activation(bias[:, 0, hd, :], bias[:, 0, hd, :], ACT.Exp,
                                             bias=small[:, 32 + hd:33 + hd],
                                             accum_out=small[:, 48 + hd:49 + hd]).then_inc(probs_ready, 1)
                    else:
                        nc.scalar.activation(bias[:, 1:3, hd, :], bias[:, 1:3, hd, :], ACT.Exp,
                                             bias=small[:, 40 + hd:41 + hd],
                                             accum_out=small[:, 56 + hd:57 + hd]).then_inc(probs_ready, 1)
            evac_z(6)
            evac_z(7)
            a.wait_ge(brow_out, 16)
            for u in range(6):
                a.wait_ge(pT_mm, u + 1)
                nc.scalar.activation(pT[:, u // 2, 4 * (u % 2):4 * (u % 2) + 4, :],
                                     ps[:, 2 + u % 2, :].rearrange("p (h t) -> p h t", h=4),
                                     ACT.Copy).then_inc(pT_ready, 1)
            zf = z[:, Z_F:Z_F + 2, :].rearrange("p a n -> p (a n)")
            zq = z[:, Z_Q:Z_Q + 2, :].rearrange("p a n -> p (a n)")
            le = level_e[:, :, :].rearrange("p h t -> p (h t)")
            lx0 = level_x[:, 0, :, :].rearrange("p h t -> p (h t)")
            lx1 = level_x[:, 1, :, :].rearrange("p h t -> p (h t)")
            a.wait_ge(z_ready, 8)
            step(nc.scalar.activation(le, zf, ACT.Abs))
            step(nc.scalar.activation(le, le, ACT.Exp, scale=-1.0))
            nc.scalar.activation(le, le, ACT.Ln, bias=1.0).then_inc(hg_exp, 1)
            evac_z(8)
            obT = bias[:, 0, :, :].rearrange("p a t -> p (a t)").rearrange("p (k t) -> p k t", k=4)
            oaT = bias[:, 1, :, :].rearrange("p a t -> p (a t)").rearrange("p (k t) -> p k t", k=4)
            for tt in range(TT):
                a.wait_ge(br_mm, tt + 1)
                nc.scalar.activation(obT[:, :, tt * P:(tt + 1) * P],
                                     ps[:, 2 + tt, :].rearrange("p (k t) -> p k t", k=4), ACT.Copy).then_inc(brT_ready, 1)
            a.wait_ge(hg_lin, 1)
            nc.scalar.activation(lx1, lx1, ACT.Exp, scale=-1.0).then_inc(hg_exp, 1)
            evac_z(9)
            a.wait_ge(z_ready, 10)
            nc.scalar.activation(lx0, zq, ACT.Sigmoid).then_inc(hg_exp, 1)
            evac_z(10)
            for n in range(1 + len(HALVES)):
                a.wait_ge(lvl_d, n + 1)
                nc.scalar.activation(level_es[n % 2], level_es[n % 2], ACT.Exp).then_inc(lvl_e, 1)
                if n == 1 or n == 3 or n == 5:
                    evac_z(11 + n // 2)
            for n in range(14, 17):
                evac_z(n)
            for tt in range(TT):
                a.wait_ge(o_mm, tt + 1)
                for hd in range(HGRN_H):
                    nc.scalar.activation(level_x[:, tt, hd, 0:P], ps[:, 6 + tt, hd * P:(hd + 1) * P], ACT.Square,
                                         accum_out=small[:, 16 + 4 * tt + hd:17 + 4 * tt + hd]).then_inc(o_sq, 1)
            a.wait_ge(z_ready, 14)
            nc.scalar.activation(le, z[:, Z_G:Z_G + 2, :].rearrange("p a n -> p (a n)"), ACT.Sigmoid).then_inc(hg_exp, 1)
            evac_z(17)
            evac_z(18)
            rsqrt_guess(2, 16, 8)
            evac_z(19)
            for tt in range(TT):
                a.wait_ge(br_mm, 2 + tt + 1)
                nc.scalar.activation(oaT[:, :, tt * P:(tt + 1) * P],
                                     ps[:, 2 + tt, :].rearrange("p (k t) -> p k t", k=4), ACT.Copy).then_inc(brT_ready, 1)
            evac_z(20)
            evac_z(21)
            for tt in range(TT):
                a.wait_ge(mT_mm, tt + 1)
                copy_T(4 + 2 * tt, hT, tt, mT_ready)

            def split_hi(g, u, first_use=False):
                wait_tile(a, g, u // 2)
                if not first_use:
                    a.wait_ge(w_free, g * 24 + (u + 1))
                nc.scalar.activation(w_hi[:, u % PARTS, :], raw_unit(u), ACT.Copy).then_inc(hi_ready, 1)

            a.wait_ge(proj_mm, 4)
            for u in EARLY:
                split_hi(0, u, first_use=True)
            for tt in range(TT):
                a.wait_ge(out_used, 4)
                norm_square(tt)
            rsqrt_guess(3, TT, TT)
            for tt in range(TT):
                a.wait_ge(h2_mm, tt + 1)
                copy_T(4 + 2 * tt, hT, tt, h2T_ready)
            for tt in range(TT):
                a.wait_ge(rt_max, tt + 1)
                nc.scalar.activation(route[:, tt, 2, :], route[:, tt, 0, :], ACT.Exp,
                                     bias=small[:, 32 + tt:33 + tt]).then_inc(rt_exp, 1)
            a.wait_ge(b1_mm, 1)
            nc.scalar.activation(b1T[:, :], ps[:, 3, :], ACT.Copy).then_inc(b1_ready, 1)

            a.wait_ge(b2_mm, 2)
            a.wait_ge(parts_ready, 2)
            def body(g, early=()):
                def evac_h(b):
                    a.wait_ge(w_free, g * 24 + (PARTS + 4 * b + 4))
                    if b >= 2:
                        a.wait_ge(sum_mm, g * 4 + (b - 1))
                    nc.scalar.activation(hs[:, b % 2, :], ps[:, b % 2, :], ACT.Copy).then_inc(hs_ready, 1)

                def sigmoid(half):
                    a.wait_ge(glu_ready, g * 2 + (half + 1))
                    nc.scalar.activation(sig[:, :, :], glu[:, :, :], ACT.Sigmoid, scale=ALPHA).then_inc(sig_ready, 1)

                def act_hi(half):
                    a.wait_ge(a32_ready, g * 2 + (half + 1))
                    nc.scalar.activation(act[:, 4 * half:4 * half + 4, 0:SLOTS], act32[:, :, :], ACT.Copy).then_inc(ahi_ready, 1)

                for u in range(24):
                    if u == 6:
                        a.wait_ge(w_free, g * 24 + PARTS)
                        y_out()
                    if u in (7, 12, 16, 19):
                        evac_h((7, 12, 16, 19).index(u))
                    if u == 15:
                        sigmoid(0)
                    if u == 17:
                        st_copy(g + 1)
                    if u == 17:
                        act_hi(0)
                    if u == 20:
                        sigmoid(1)
                    if u == 21:
                        act_hi(1)
                    if u == 22:
                        xs_hi(g + 1)
                    if u in SPLIT and u not in early:
                        split_hi(g, u)

            def y_out():
                nc.scalar.activation(ysb[:, 0:512], ps[:, 4, :], ACT.Copy).then_inc(ysb_ready, 1)
                nc.scalar.activation(ysb[:, 512:1024], ps[:, 5, :], ACT.Copy).then_inc(ysb_ready, 1)

            def xs_hi(n):
                a.wait_ge(gather_mm, n + 1)
                nc.scalar.activation(xs[:, :, 0:SLOTS], ps[:, 6, :].rearrange("p (k s) -> p k s", k=KC),
                                     ACT.Copy).then_inc(xhi_ready, 1)

            def st_copy(n):
                a.wait_ge(st_mm, n + 1)
                nc.scalar.activation(st[:, :], ps[:, 7, 0:T], ACT.Copy).then_inc(st_ready, 1)

            st_copy(0)
            xs_hi(0)
            body(0, early=EARLY)
            with a.Fori(1, NE) as i:
                body(i)
            a.wait_ge(list_ready, 1)
            n_more = a.value_load(lists_i[0:1, 0:1], min_val=0, max_val=MAX_MORE)
            with a.If(n_more > 0):
                with a.Fori(0, n_more) as r:
                    body(r + NE)
            a.wait_ge(w_free, n_more * 24 + (24 * NE + PARTS))
            y_out()
            for tt in range(TT):
                a.wait_ge(fin_sq, tt + 1)
                norm_square(tt)
            rsqrt_guess(4, TT, TT)

        @block.vector
        def _(v):
            count = [0]

            def step(ins):
                count[0] += 1
                ins.then_inc(dve_step, 1)
                v.wait_ge(dve_step, count[0])

            def after(sem_, n, ins):
                ins.then_inc(sem_, 1)
                v.wait_ge(sem_, n)

            V = nc.vector
            v.wait_ge(c_exp, 1)
            step(V.tensor_scalar(cc[:, 2, :], cc[:, 1, :], 1.0, None, ALU.add))
            step(V.reciprocal(cc[:, 3, :], cc[:, 2, :]))
            step(V.tensor_tensor(cc[:, 1, :], cc[:, 0, :], cc[:, 3, :], ALU.mult))

            def ada_tile(s, n):
                dst = acc[:, dve_section(s) % 2, :]
                if dve_section(s) >= 2 and n == 0:
                    v.wait_ge(ada_mm, dve_section(s) - 1)
                w, full, at = tile_at("ada", 4 * s + n)
                v.wait_ge(full, at)
                part = dst[:, 256 * n:256 * n + 256]
                step(V.tensor_scalar(part, w[:, 0, :], cc[:, 1, 0:1], None, ALU.mult))
                for j in range(1, KC):
                    ins = V.scalar_tensor_tensor(out=part, in0=w[:, j, :], scalar=cc[:, 1, j:j + 1], in1=part,
                                                 op0=ALU.mult, op1=ALU.add)
                    if j < KC - 1:
                        step(ins)
                    else:
                        after(ada_used, 4 * dve_section(s) + n + 1, ins)
                if n == 3:
                    V.tensor_copy(small[:, 66:67], dst[:, 1023:1024]).then_inc(acc_ready, 1)

            def ada_section(s):
                for n in range(4):
                    ada_tile(s, n)

            def mod_section(s):
                if s == PE_SECTION:
                    v.wait_ge(ada_taken, 4)
                else:
                    v.wait_ge(ada_mm, dve_section(s) + 1)
                v.wait_ge(ld_bada[s], 16)
                for g in range(2):
                    dst = BADA_DST[s][:, 512 * g:512 * g + 512]
                    ins = V.tensor_tensor(dst, ps[:, (6 if s == PE_SECTION else 4) + g, :], dst, ALU.add)
                    if g == 0:
                        step(ins)
                    else:
                        after(mod_ready, s + 1, ins)

            def newton(n, lo, w, scale):
                val, guess, tmp = (small[:, lo + k * w:lo + (k + 1) * w] for k in range(3))
                step(V.tensor_scalar(val, val, scale, EPS, ALU.mult, ALU.add))
                V.tensor_copy(small[:, 65:66], val[:, 0:1]).then_inc(ln_in, 1)
                v.wait_ge(ln_out, n)
                r = tmp
                step(V.tensor_tensor(guess, r, r, ALU.mult))
                step(V.tensor_tensor(guess, guess, val, ALU.mult))
                step(V.tensor_scalar(guess, guess, -0.5, 1.5, ALU.mult, ALU.add))
                step(V.tensor_tensor(r, r, guess, ALU.mult))

            def rstd(n, sq_n):
                v.wait_ge(sq_done, sq_n)
                step(V.tensor_copy(small[:, TT:2 * TT], small[:, 0:TT]))
                newton(n, TT, TT, 1.0 / D)

            def scaled_weight(scale):
                step(V.scalar_tensor_tensor(out=scale, in0=scale, scalar=1.0, in1=norm_w[:, :], op0=ALU.add, op1=ALU.mult))

            def norm(tt, shift, weight, sig):
                ins = V.scalar_tensor_tensor(out=h[:, tt, :], in0=x_sb[:, tt, :], scalar=small[:, 3 * TT + tt:3 * TT + tt + 1],
                                             in1=weight, op0=ALU.mult, op1=ALU.mult)
                if shift is None:
                    after(sig, tt + 1, ins)
                else:
                    step(ins)
                    after(sig, tt + 1, V.tensor_tensor(h[:, tt, :], h[:, tt, :], shift, ALU.add))

            v.wait_ge(dve_step, count[0])
            V.tensor_copy(c_wide, cc[:, 1, :].rearrange("p (j o) -> p j o", o=1).broadcast_to([P, KC, P])).then_inc(c_ready, 1)
            ada_section(0)
            rstd(1, 2)
            mod_section(0)
            mod_section(1)
            v.wait_ge(ld_mix, 16)
            scaled_weight(mod[:, 1, :])
            for tt in range(TT):
                norm(tt, mod[:, 0, :], mod[:, 1, :], h_ready)
            step(V.tensor_tensor(lb[:, 1, :], lb[:, 0, :], lb[:, 0, :], ALU.subtract))
            step(V.tensor_scalar(lb[:, 2, :], lb[:, 1, :], 1.0, None, ALU.add))
            step(V.tensor_tensor(lb[:, 1, :], lb[:, 2, :], lb[:, 2, :], ALU.subtract))
            step(V.tensor_scalar(lb[:, 2, :], lb[:, 1, :], -1.0, 1.0, ALU.mult, ALU.add))
            v.wait_ge(ld_small, 16 * N_SMALL)
            step(V.tensor_copy(masks[:, :, :].rearrange("p a n -> p (a n)"), z[:, 20:22, :].rearrange("p a n -> p (a n)")))
            ada_section(2)
            v.wait_ge(z_ready, 3)
            for tt in range(TT):
                S = (tt + 1) * P
                for hp in range(4):
                    u = 4 * tt + hp
                    v.wait_ge(relu_ready, u + 1)
                    for j in range(2):
                        hd = 4 * (hp // 2) + hp % 2 + 2 * j
                        iw = z[:, Z_IK, T + 8 * tt + hd:T + 8 * tt + hd + 1]
                        src = relu[:, u % 2, j * S:(j + 1) * S]
                        dst = score[:, tt, 0:S]
                        if hp == 0 and j == 0:
                            ins = V.tensor_scalar(dst, src, iw, None, ALU.mult)
                        else:
                            ins = V.scalar_tensor_tensor(out=dst, in0=src, scalar=iw, in1=dst, op0=ALU.mult, op1=ALU.add)
                        if j == 0:
                            step(ins)
                        else:
                            after(relu_used, u + 1, ins)
                V.tensor_copy(small[:, 64:65], score[:, tt, 0:1]).then_inc(score_sum, 1)
            mod_section(2)
            best = small[:, 16:24]
            for tt in range(TT):
                S = (tt + 1) * P
                v.wait_ge(score_causal, tt + 1)
                for _ in range(TOPK // 8):
                    step(V.max(out=best, in_=score[:, tt, 0:S]))
                    step(V.match_replace(out=score[:, tt, 0:S], in_to_replace=best, in_values=score[:, tt, 0:S],
                                         imm_value=PICKED))
                after(picked, tt + 1, V.tensor_scalar(score[:, tt, 0:S], score[:, tt, 0:S], PICKED / 2, DEAD, ALU.is_gt, ALU.mult))
            v.wait_ge(bias_in, 48)
            v.wait_ge(pick_causal, 2)
            for n, (tt, s0) in enumerate(((0, 0), (1, 0), (1, 1))):
                step(V.tensor_tensor(bias[:, n, :, :], bias[:, n, :, :],
                                     score[:, tt:tt + 1, s0 * P:(s0 + 1) * P].broadcast_to([P, ATT_H, P]), ALU.add))
            for tt in range(TT):
                for hp in range(4):
                    u = 4 * tt + hp
                    v.wait_ge(logit_mm, u + 1)
                    n0, w = (0, 1) if tt == 0 else (1, 2)
                    hd = 4 * (hp // 2) + hp % 2
                    dst = bias[:, n0:n0 + w, hd:hd + 3:2, :]
                    src = ps[:, 2 + u % 2, 0:2 * w * P].rearrange("p (h n s) -> p n h s", h=2, n=w)
                    for k in range(w):
                        ins = V.scalar_tensor_tensor(out=dst[:, k], in0=src[:, k], scalar=ATT_D ** -0.5, in1=dst[:, k],
                                                     op0=ALU.mult, op1=ALU.add)
                        if k < w - 1:
                            step(ins)
                        else:
                            after(logit_ready, u + 1, ins)
            for tt in range(TT):
                if tt == 0:
                    step(V.tensor_reduce(small[:, 32:40], bias[:, 0, :, :], AX_X, ALU.max))
                else:
                    step(V.tensor_reduce(small[:, 16:32].rearrange("p (n h) -> p n h", n=2), bias[:, 1:3, :, :], AX_X, ALU.max))
                    step(V.tensor_tensor(small[:, 40:48], small[:, 16:24], small[:, 24:32], ALU.max))
            after(max_ready, 1, V.tensor_scalar(small[:, 32:48], small[:, 32:48], -1.0, None, ALU.mult))
            ada_section(3)
            v.wait_ge(probs_ready, 16)
            step(V.reciprocal(small[:, 48:64], small[:, 48:64]))
            for tt in range(TT):
                v.wait_ge(av_mm, tt + 1)
                after(ob_ready, tt + 1, V.tensor_tensor(
                    relu[:, tt, :].rearrange("p (h d) -> p h d", h=ATT_H),
                    ps[:, 4 + tt, :].rearrange("p (h d) -> p h d", h=ATT_H),
                    small[:, 48 + 8 * tt:56 + 8 * tt].rearrange("p (h o) -> p h o", o=1).broadcast_to([P, ATT_H, ATT_D]), ALU.mult))
            zf = z[:, Z_F:Z_F + 2, :].rearrange("p a n -> p (a n)")
            zq = z[:, Z_Q:Z_Q + 2, :].rearrange("p a n -> p (a n)")
            zf4 = zf.rearrange("p (h t) -> p h t", h=HGRN_H)
            zq4 = zq.rearrange("p (h t) -> p h t", h=HGRN_H)
            le = level_e[:, :, :].rearrange("p h t -> p (h t)")
            lx0 = level_x[:, 0, :, :].rearrange("p h t -> p (h t)")
            lx1 = level_x[:, 1, :, :].rearrange("p h t -> p (h t)")
            dec = decay[:, :, :].rearrange("p h t -> p (h t)")
            v.wait_ge(hg_exp, 1)
            step(V.scalar_tensor_tensor(out=dec, in0=zf, scalar=0.0, in1=le, op0=ALU.min, op1=ALU.subtract))
            after(hg_lin, 1, V.scalar_tensor_tensor(out=lx1, in0=zf, scalar=0.0, in1=le, op0=ALU.max, op1=ALU.add))
            step(V.memset(zf, 1.0))
            for hd in range(HGRN_H):
                step(V.tensor_tensor_scan(level_e[:, hd, :], zf4[:, hd, :], decay[:, hd, :], 0.0, ALU.mult, ALU.add))
            step(V.tensor_copy(dec, le))
            ada_tile(4, 0)
            ada_tile(4, 1)
            v.wait_ge(hg_exp, 3)
            step(V.tensor_tensor(zq, zq, lx0, ALU.mult))
            for hd in range(HGRN_H):
                step(V.tensor_scalar(zf4[:, hd, :], level_x[:, 1, hd, :], lb[:, 2, hd:hd + 1], None, ALU.mult))
            step(V.memset(aT[:, :, :, :], 0.0))
            LEVELS = (128,) + HALVES

            def blocks(t, half):
                return t.rearrange("p (n w) -> p n w", w=2 * half)

            def level_exponents(n):
                half = LEVELS[n]
                b_v, e_v = blocks(dec, half), blocks(level_es[n % 2], half)
                mid = b_v[:, :, half - 1:half].broadcast_to([P, T * HGRN_H // (2 * half), half])
                step(V.tensor_tensor(e_v[:, :, 0:half], mid, b_v[:, :, 0:half], ALU.subtract))
                after(lvl_d, n + 1, V.tensor_tensor(e_v[:, :, half:], b_v[:, :, half:], mid, ALU.subtract))

            def level_operands(n):
                half = LEVELS[n]
                e_v = blocks(level_es[n % 2], half)
                x_v = blocks(level_x[:, n % 2, :, :].rearrange("p h t -> p (h t)"), half)
                v.wait_ge(lvl_e, n + 1)
                if n >= 2:
                    v.wait_ge(lvl_mm, n - 1)
                step(V.tensor_tensor(x_v[:, :, 0:half], e_v[:, :, 0:half], blocks(zf, half)[:, :, 0:half], ALU.mult))
                after(lvl_x, n + 1, V.tensor_tensor(x_v[:, :, half:], e_v[:, :, half:], blocks(zq, half)[:, :, half:], ALU.mult))

            def level_part(n):
                v.wait_ge(lvl_mm, n + 1)
                if n == 0:
                    after(lvl_at, 1, V.tensor_copy(aT_off[:, :, :], ps[:, 4, :].rearrange("p (h t) -> p h t", h=HGRN_H)))
                    return
                for tt in range(TT):
                    ins = V.copy_predicated(aT[:, tt, :, :], masks[:, n - 1:n, :].broadcast_to([P, HGRN_H, P]),
                                            ps[:, level_bank(n) + tt, :].rearrange("p (h t) -> p h t", h=HGRN_H))
                    if tt == 0:
                        step(ins)
                    else:
                        after(lvl_at, n + 1, ins)

            level_exponents(0)
            level_exponents(1)
            mod_section(3)
            for n in range(len(LEVELS)):
                level_operands(n)
                if n + 2 < len(LEVELS):
                    level_exponents(n + 2)
                if n >= 1:
                    level_part(n - 1)
                if n == 1 or n == 5:
                    ada_tile(4, 2 + n // 4)
            level_part(len(LEVELS) - 1)
            level_part(len(LEVELS))
            mod_section(4)
            ada_section(5)
            mod_section(5)
            v.wait_ge(hg_exp, 4)
            zg = z[:, Z_G:Z_G + 2, :]
            step(V.tensor_tensor(zg.rearrange("p a n -> p (a n)"), zg.rearrange("p a n -> p (a n)"), le, ALU.mult))
            v.wait_ge(o_sq, 8)
            newton(2, 16, 8, 1.0 / HGRN_D)
            for tt in range(TT):
                oa = level_x[:, tt, 0:2, :].rearrange("p a t -> p (a t)")
                step(V.tensor_tensor(
                    oa.rearrange("p (h d) -> p h d", h=HGRN_H),
                    ps[:, 6 + tt, :].rearrange("p (h d) -> p h d", h=HGRN_H),
                    small[:, 32 + 4 * tt:36 + 4 * tt].rearrange("p (h o) -> p h o", o=1).broadcast_to([P, HGRN_H, P]), ALU.mult))
                step(V.tensor_tensor(oa, oa, onw[:, :], ALU.mult))
                after(oa_ready, tt + 1, V.tensor_tensor(
                    oa.rearrange("p (a n) -> p a n", a=2), oa.rearrange("p (a n) -> p a n", a=2),
                    zg[:, :, 256 * tt:256 * tt + 256], ALU.mult))
            v.wait_ge(z_ready, 22)
            u = 0
            for nb in range(2):
                for tt in range(TT):
                    v.wait_ge(proj_mm, u + 1)
                    ga, gb = (z[:, Z_GATE + 4 * k + 2 * nb:Z_GATE + 4 * k + 2 * nb + 2, 256 * tt:256 * tt + 256] for k in range(2))
                    ya, yb = (ps[:, 2 * (u % 2) + k, :].rearrange("p (a n) -> p a n", a=2) for k in range(2))
                    step(V.tensor_tensor(ga, ga, ya, ALU.mult))
                    step(V.tensor_tensor(gb, gb, yb, ALU.mult))
                    after(merged, u + 1, V.tensor_tensor(
                        h[:, tt, 512 * nb:512 * nb + 512].rearrange("p (a n) -> p a n", a=2), ga, gb, ALU.add))
                    u += 1
            def split_lo(g, u):
                v.wait_ge(hi_ready, g * len(SPLIT) + split_count(u))
                V.tensor_tensor(w_lo[:, u % PARTS, :], raw_unit(u), w_hi[:, u % PARTS, :].bitcast(F32), ALU.subtract).then_inc(lo_ready, 1)

            v.wait_ge(ld_ffn, 16)
            scaled_weight(mod[:, 1, :])
            for n in range(4):
                v.wait_ge(out_mm, n + 1)
                for tt in range(TT):
                    cols = slice(256 * n, 256 * n + 256)
                    tmp = z[:, 12 + n, 256 * tt:256 * tt + 256]
                    step(V.tensor_tensor(tmp, ps[:, n, 256 * tt:256 * tt + 256], mod[:, 2, cols], ALU.mult))
                    ins = V.tensor_tensor(x_sb[:, tt, cols], x_sb[:, tt, cols], tmp, ALU.add)
                    if tt == 0:
                        step(ins)
                    else:
                        after(out_used, n + 1, ins)
                if n < 3:
                    for u in EARLY[2 * n:2 * n + 2]:
                        split_lo(0, u)
            rstd(3, 4)
            for tt in range(TT):
                norm(tt, mod[:, 0, :], mod[:, 1, :], h2_ready)
            for tt in range(TT):
                rest = z[:, 6:8, :].rearrange("p a n -> p (a n)")
                step(V.tensor_copy(h_parts[:, tt, 0, :], h[:, tt, :]))
                step(V.tensor_tensor(rest, h[:, tt, :], h_parts[:, tt, 0, :], ALU.subtract))
                step(V.tensor_copy(h_parts[:, tt, 1, :], rest))
                after(parts_ready, tt + 1, V.tensor_tensor(h_parts[:, tt, 2, :], rest, h_parts[:, tt, 1, :], ALU.subtract))
            for u in EARLY[6:]:
                split_lo(0, u)
            wk = z[:, 12, 0:128].rearrange("p (t n) -> p t n", t=TT)
            step(V.memset(wk[:, :, 0:4], 3.0e38))
            for tt in range(TT):
                R = route[:, tt]
                best = z[:, 13, 8 * tt:8 * tt + 8]
                v.wait_ge(rt_mm, tt + 1)
                step(V.tensor_tensor(R[:, 0, :], ps[:, 2 * tt, NE * tt:NE * tt + NE], br[:, :], ALU.add))
                step(V.tensor_copy(wk[:, tt, 4:36], R[:, 0, :]))
                step(V.max(out=best, in_=wk[:, tt, 0:36]))
                after(rt_max, tt + 1, V.tensor_scalar(small[:, 32 + tt:33 + tt], best[:, 4:5], -1.0, None, ALU.mult))
                step(V.match_replace(out=wk[:, tt, 0:36], in_to_replace=best, in_values=wk[:, tt, 0:36], imm_value=PICKED))
                step(V.tensor_scalar(R[:, 3, :], wk[:, tt, 4:36], PICKED / 2, None, ALU.is_lt))
                v.wait_ge(rt_exp, tt + 1)
                step(V.tensor_tensor(R[:, 4, :], R[:, 2, :], R[:, 3, :], ALU.mult))
                step(V.tensor_reduce(small[:, 34 + tt:35 + tt], R[:, 4, :], AX_X, ALU.add))
                step(V.reciprocal(small[:, 34 + tt:35 + tt], small[:, 34 + tt:35 + tt]))
                after(rt_sel, tt + 1, V.tensor_scalar(R[:, 4, :], R[:, 4, :], small[:, 34 + tt:35 + tt], None, ALU.mult))
            v.wait_ge(pos_mm, 1)
            for tt in range(TT):
                R = route[:, tt]
                step(V.tensor_scalar(R[:, 5, :], ps[:, 1, NE * tt:NE * tt + NE], 1.0, None, ALU.add))
                step(V.tensor_tensor(R[:, 5, :], R[:, 5, :], R[:, 3, :], ALU.mult))
                step(V.tensor_scalar(R[:, 5, :], R[:, 5, :], -1.0, None, ALU.add))
            step(V.tensor_scalar(small[0:96, 40:41], ps[0:96, 1, 64:65], more_c[:, 0:1], None, ALU.is_gt))
            after(flag_ready, 1, V.tensor_copy(small[0:96, 41:42], small[0:96, 40:41]))
            v.wait_ge(flag_mm, 1)
            hot = z[0:96, 14, 0:16]
            step(V.tensor_scalar(hot, iota[0:96, 0:16], ps[0:96, 1, 96:97], None, ALU.is_equal))
            after(hot_ready, 1, V.tensor_scalar(hot, hot, small[0:96, 40:41], None, ALU.mult))
            v.wait_ge(list_mm, 1)
            step(V.tensor_copy(lists[0:1, 0:1], ps[0:1, 1, 128:129]))
            step(V.tensor_copy(lists[0:1, ITEM_E + NE:ITEM_C], ps[0:1, 1, 160:176]))
            step(V.tensor_copy(lists[0:1, ITEM_C + NE:ITEM_C + NE + 16], ps[0:1, 1, 176:192]))
            after(list_ready, 1, V.tensor_copy(lists_i[0:1, 0:ITEM_C + NE + 16], lists[0:1, 0:ITEM_C + NE + 16]))
            step(V.memset(pick_g[:, :, :], 0.0))
            for tt in range(TT):
                V.tensor_copy(pick_g[:, tt, 0:NE], route[:, tt, 4, :]).then_inc(pickg_ready, 1)

            v.wait_ge(b1_ready, 1)
            b1_lin = b1T[:, :].rearrange("p (e c) -> p e c", c=16)[:, :, 8:16]
            step(V.tensor_scalar(b1_lin, b1_lin, 1.0, None, ALU.add))
            n_more = v.value_load(lists_i[0:1, 0:1], min_val=0, max_val=MAX_MORE)

            def xs_lo(n):
                v.wait_ge(xhi_ready, n + 1)
                V.tensor_tensor(xs[:, :, SLOTS:P], ps[:, 6, :].rearrange("p (k s) -> p k s", k=KC),
                                xs[:, :, 0:SLOTS].bitcast(F32), ALU.subtract).then_inc(xs_ready, 1)

            def pick_tokens(e, chunk0):
                for tt in range(TT):
                    V.tensor_scalar(pick[:, tt, :], iota[:, bass.ds(chunk0, SLOTS)], route[:, tt, 5, bass.ds(e, 1)],
                                    None, ALU.is_equal).then_inc(pick_ready, 1)

            def add_y(g, n):
                v.wait_ge(sc_mm, g * 4 + (n + 1))
                dst = yacc[:, n // 2, 512 * (n % 2):512 * (n % 2) + 512]
                V.tensor_tensor(dst, dst, ps[:, 6 + n % 2, :], ALU.add).then_inc(y_added, 1)

            def body(g, e, early=()):
                def swiglu_in(half):
                    v.wait_ge(sum_mm, g * 4 + (2 * half + 2))
                    T0 = ps[:, 2, :].rearrange("p (c s) -> p c s", c=4)[:, :, 0:SLOTS]
                    T1 = ps[:, 3, :].rearrange("p (c s) -> p c s", c=4)[:, :, 0:SLOTS]
                    bg = b1T[:, bass.ds(e * 16 + 4 * half, 4)].rearrange("p (c o) -> p c o", o=1).broadcast_to([P, 4, SLOTS])
                    bl = b1T[:, bass.ds(e * 16 + (8 + 4 * half), 4)].rearrange("p (c o) -> p c o", o=1).broadcast_to([P, 4, SLOTS])
                    V.tensor_tensor(glu[:, :, :], T0, bg, ALU.add).then_inc(glu_ready, 1)
                    V.tensor_tensor(lin[:, :, :], T1, bl, ALU.add).then_inc(t_free, 1)
                    v.wait_ge(t_free, g * 2 + (half + 1))
                    V.tensor_scalar(lin[:, :, :], lin[:, :, :], 1.0 + LIMIT, 1.0 - LIMIT, ALU.min, ALU.max).then_inc(lin_ready, 1)

                def swiglu_out(half):
                    v.wait_ge(sig_ready, g * 2 + (half + 1))
                    v.wait_ge(lin_ready, g * 2 + (half + 1))
                    V.scalar_tensor_tensor(out=lin[:, :, :], in0=sig[:, :, :], scalar=SIG_LIMIT, in1=lin[:, :, :],
                                           op0=ALU.min, op1=ALU.mult).then_inc(moe_step, 1)
                    v.wait_ge(moe_step, g * 2 + (half + 1))
                    V.scalar_tensor_tensor(out=act32[:, :, :], in0=glu[:, :, :], scalar=LIMIT, in1=lin[:, :, :],
                                           op0=ALU.min, op1=ALU.mult).then_inc(a32_ready, 1)

                def act_lo(half):
                    v.wait_ge(ahi_ready, g * 2 + (half + 1))
                    V.tensor_tensor(act[:, 4 * half:4 * half + 4, SLOTS:P], act32[:, :, :],
                                    act[:, 4 * half:4 * half + 4, 0:SLOTS].bitcast(F32), ALU.subtract).then_inc(act_ready, 1)

                e_next = v.value_load(lists_i[0:1, bass.ds(g + (ITEM_E + 1), 1)], min_val=0, max_val=NE - 1)
                c_next = v.value_load(lists_i[0:1, bass.ds(g + (ITEM_C + 1), 1)], min_val=0, max_val=3 * SLOTS)
                for u in range(24):
                    if u in SPLIT and u not in early:
                        split_lo(g, u)
                    if u == 5:
                        v.wait_ge(gather_mm, g + 1)
                        v.wait_ge(doubled, g * 4 + 4)
                        pick_tokens(e_next, c_next)
                    if u == 9:
                        add_y(g, 0)
                        add_y(g, 1)
                    if u == 12:
                        add_y(g, 2)
                        add_y(g, 3)
                    if u == 13:
                        swiglu_in(0)
                    if u == 15:
                        swiglu_out(0)
                    if u == 16:
                        act_lo(0)
                    if u == 18:
                        swiglu_in(1)
                    if u == 19:
                        swiglu_out(1)
                    if u == 20:
                        act_lo(1)
                    if u == 22:
                        xs_lo(g + 1)

            v.wait_ge(y_start, 1)
            pick_tokens(0, 0)
            xs_lo(0)
            body(0, 0, early=EARLY)
            with v.Fori(1, NE) as i:
                body(i, i)
            with v.If(n_more > 0):
                with v.Fori(0, n_more) as r:
                    e = v.value_load(lists_i[0:1, bass.ds(r + (ITEM_E + NE), 1)], min_val=0, max_val=NE - 1)
                    body(r + NE, e)
            for n in range(4):
                add_y(n_more + NE, n)
            v.wait_ge(y_added, n_more * 4 + (4 * NE + 4))
            for tt in range(TT):
                step(V.tensor_tensor(yacc[:, tt, :], yacc[:, tt, :], gate_f[:, :], ALU.mult))
                after(fin_sq, tt + 1, V.tensor_tensor(x_sb[:, tt, :], x_sb[:, tt, :], yacc[:, tt, :], ALU.add))
            v.wait_ge(ld_fin, 16)
            rstd(4, 6)
            for tt in range(TT):
                norm(tt, None, norm_w[:, :], fin_ready)

        @block.tensor
        def _(pe):
            mm = nc.tensor.matmul
            tr = nc.tensor.transpose

            def ada(s):
                pe.wait_ge(acc_ready, dve_section(s) + 1)
                if s >= 1:
                    pe.wait_ge(mod_ready, s)
                for g in range(2):
                    last = mm(ps[:, 4 + g, :], upper[:, 1, :], acc[:, dve_section(s) % 2, 512 * g:512 * g + 512], start=True, stop=True)
                last.then_inc(ada_mm, 1)

            def ada_whole(s):
                for n in range(4):
                    w, full, at = tile_at("ada", 4 * s + n)
                    pe.wait_ge(full, at)
                    for j in range(KC):
                        last = mm(ps[:, 6 + n // 2, 256 * (n % 2):256 * (n % 2) + 256], c_wide[:, j, :], w[:, j, :],
                                  start=(j == 0), stop=(j == KC - 1))
                    last.then_inc(ada_taken, 1)

            def transposes(src, bank, tt, sig):
                for k in range(KC):
                    last = tr(ps[:, bank + k // 4, P * (k % 4):P * (k % 4) + P], src[:, tt, P * k:P * k + P], ident[:, :])
                last.then_inc(sig, 1)

            pe.wait_ge(c_ready, 1)
            ada_whole(PE_SECTION)
            pe.wait_ge(ld_upper, 16)
            ada(0)
            pe.wait_ge(ld_bias, 32)
            pe.wait_ge(ld_first, 16 * N_FIRST)
            mm(ps[0:ATT_H, 3, 0:384], relb, bucket, start=True, stop=True).then_inc(bias_mm, 1)
            for tt in range(TT):
                pe.wait_ge(h_ready, tt + 1)
                if tt == 1:
                    pe.wait_ge(brow_ready, 1)
                transposes(h, 2 * tt, tt, tr_mm)

            def z_block(n):
                w, full, at = tile_at("in", n)
                pe.wait_ge(full, at)
                if n < 2:
                    pe.wait_ge(hT_ready, 4)
                else:
                    pe.wait_ge(z_ready, n - 1)
                bank = ps[:, n % 2, :]
                kind = Z_BLOCKS[n][0]
                if kind == "T":
                    for j in range(2):
                        for k in range(KC):
                            last = mm(bank[:, T * j:T * j + T], w[:, k, P * j:P * j + P], hT[:, k, :], start=(k == 0), stop=(k == KC - 1))
                elif kind in ("IK", "KV"):
                    for k in range(KC):
                        mm(bank[0:64, 0:T], w[:, k, 0:64], hT[:, k, :], start=(k == 0), stop=(k == KC - 1))
                    wd = 8 if kind == "IK" else 64
                    for tt in range(TT):
                        for k in range(KC):
                            last = mm(bank[:, T + wd * tt:T + wd * tt + wd], hT[:, k, tt * P:(tt + 1) * P],
                                      w[:, k, 64:64 + wd], start=(k == 0), stop=(k == KC - 1))
                else:
                    for tt in range(TT):
                        for k in range(KC):
                            last = mm(bank[:, T * tt:T * tt + T], hT[:, k, tt * P:(tt + 1) * P], w[:, k, :], start=(k == 0), stop=(k == KC - 1))
                last.then_inc(z_mm, 1)

            for n in range(3):
                z_block(n)
            pe.wait_ge(z_ready, 3)
            for u in range(8):
                tt, S = u // 4, (u // 4 + 1) * P
                if u >= 2:
                    pe.wait_ge(relu_ready, u - 1)
                r, lo = u % 4, 64 * (u % 2)
                for j in range(2):
                    last = mm(ps[:, 2 + u % 2, j * S:(j + 1) * S],
                              z[lo:lo + 64, Z_IQ + r // 2, T * j + tt * P:T * j + tt * P + P],
                              z[lo:lo + 64, Z_IK, 0:S], start=True, stop=True)
                last.then_inc(score_mm, 1)
            ada(2)
            for n in range(3, 6):
                z_block(n)
            pe.wait_ge(relu_ready, 8)
            pe.wait_ge(z_ready, 6)
            for u in range(8):
                tt, S = u // 4, (u // 4 + 1) * P
                if u >= 2:
                    pe.wait_ge(logit_ready, u - 1)
                r, lo = u % 4, 64 * (u % 2)
                for j in range(2):
                    last = mm(ps[:, 2 + u % 2, j * S:(j + 1) * S],
                              z[lo:lo + 64, Z_QB + r // 2, T * j + tt * P:T * j + tt * P + P],
                              z[lo:lo + 64, Z_KV, 0:S], start=True, stop=True)
                last.then_inc(logit_mm, 1)
            z_block(6)
            z_block(7)
            pe.wait_ge(logit_ready, 8)
            for u in range(6):
                pe.wait_ge(probs_ready, 4 * (u % 2) + 4 if u < 2 else 12 + 4 * (u % 2))
                if u >= 2:
                    pe.wait_ge(pT_ready, u - 1)
                for k in range(4):
                    last = tr(ps[:, 2 + u % 2, P * k:P * k + P], bias[:, u // 2, 4 * (u % 2) + k, :], ident[:, :])
                last.then_inc(pT_mm, 1)
            pe.wait_ge(mod_ready, 3)
            for tt in range(TT):
                pe.wait_ge(pT_ready, 2 if tt == 0 else 6)
                for hd in range(ATT_H):
                    for k in range(tt + 1):
                        last = mm(ps[:, 4 + tt, 64 * hd:64 * hd + 64], pT[:, tt + k, hd, :],
                                  z[:, Z_KV, T + 64 * k:T + 64 * k + 64], start=(k == 0), stop=(k == tt))
                last.then_inc(av_mm, 1)
            z_block(8)
            for tt in range(TT):
                pe.wait_ge(ob_ready, tt + 1)
                pe.wait_ge(pT_ready, 6)
                for k in range(4):
                    last = tr(ps[:, 2 + tt, P * k:P * k + P], relu[:, tt, P * k:P * k + P], ident[:, :])
                last.then_inc(br_mm, 1)
            z_block(9)
            ada(3)
            z_block(10)
            z_block(11)
            zf4 = z[:, Z_F:Z_F + 2, :].rearrange("p a n -> p (a n)").rearrange("p (h t) -> p h t", h=HGRN_H)
            zq4 = z[:, Z_Q:Z_Q + 2, :].rearrange("p a n -> p (a n)").rearrange("p (h t) -> p h t", h=HGRN_H)
            pe.wait_ge(mod_ready, 4)
            for n in range(len(HALVES) + 2):
                if n < len(HALVES) + 1:
                    pe.wait_ge(lvl_x, n + 1)
                if n >= 2:
                    pe.wait_ge(lvl_at, n - 1)
                if n == 0:
                    for hd in range(HGRN_H):
                        last = mm(ps[:, 4, P * hd:P * hd + P], level_x[:, 0, hd, 0:P], level_x[:, 0, hd, P:T], start=True, stop=True)
                else:
                    for tt in range(TT):
                        for hd in range(HGRN_H):
                            sl = slice(tt * P, tt * P + P)
                            if n <= len(HALVES):
                                left = right = level_x[:, n % 2, hd, sl]
                            else:
                                left, right = zf4[:, hd, sl], zq4[:, hd, sl]
                            last = mm(ps[:, level_bank(n) + tt, P * hd:P * hd + P], left, right, start=True, stop=True)
                last.then_inc(lvl_mm, 1)
                if n % 2 == 1:
                    z_block(12 + n // 2)
            z_block(16)
            pe.wait_ge(lvl_at, len(HALVES) + 2)
            pe.wait_ge(z_ready, 12)
            for tt in range(TT):
                for hd in range(HGRN_H):
                    vb, vc = Z_V + hd // 2, P * (hd % 2)
                    dst = ps[:, 6 + tt, P * hd:P * hd + P]
                    if tt == 1:
                        mm(dst, aT_off[:, hd, :], z[:, vb, vc:vc + P], start=True, stop=False)
                    last = mm(dst, aT[:, tt, hd, :], z[:, vb, T * tt + vc:T * tt + vc + P], start=(tt == 0), stop=True)
                last.then_inc(o_mm, 1)
            ada(4)
            z_block(17)
            z_block(18)
            ada(5)
            z_block(19)
            for tt in range(TT):
                pe.wait_ge(oa_ready, tt + 1)
                pe.wait_ge(brT_ready, tt + 1)
                for k in range(4):
                    last = tr(ps[:, 2 + tt, P * k:P * k + P], level_x[:, tt, 0:2, :].rearrange("p a t -> p (a t)")[:, P * k:P * k + P], ident[:, :])
                last.then_inc(br_mm, 1)
            z_block(20)
            z_block(21)
            obT = bias[:, 0, :, :].rearrange("p a t -> p (a t)").rearrange("p (k t) -> p k t", k=4)
            oaT = bias[:, 1, :, :].rearrange("p a t -> p (a t)").rearrange("p (k t) -> p k t", k=4)
            pe.wait_ge(brT_ready, 4)
            pe.wait_ge(z_ready, 22)
            u = 0
            for nb in range(2):
                for tt in range(TT):
                    if u >= 2:
                        pe.wait_ge(merged, u - 1)
                    for kind, src, bk in (("pa", oaT, 0), ("pb", obT, 1)):
                        w, full, at = tile_at(kind, nb)
                        pe.wait_ge(full, at)
                        for k in range(4):
                            last = mm(ps[:, 2 * (u % 2) + bk, :], src[:, k, tt * P:(tt + 1) * P], w[:, k, :], start=(k == 0), stop=(k == 3))
                    last.then_inc(proj_mm, 1)
                    u += 1
            for tt in range(TT):
                pe.wait_ge(merged, 3 + tt)
                transposes(h, 4 + 2 * tt, tt, mT_mm)
            for n in range(4):
                w, full, at = tile_at("out", n)
                pe.wait_ge(full, at)
                pe.wait_ge(mT_ready, 4)
                for tt in range(TT):
                    for k in range(KC):
                        last = mm(ps[:, n, T * tt:T * tt + T], hT[:, k, tt * P:(tt + 1) * P], w[:, k, :], start=(k == 0), stop=(k == KC - 1))
                last.then_inc(out_mm, 1)
            for tt in range(TT):
                pe.wait_ge(h2_ready, tt + 1)
                transposes(h, 4 + 2 * tt, tt, h2_mm)
            for tt in range(TT):
                pe.wait_ge(h2T_ready, 2 * tt + 2)
                for k in range(KC):
                    last = mm(ps[:, 2 * tt, NE * tt:NE * tt + NE], hT[:, k, tt * P:(tt + 1) * P], wr[:, k, :], start=(k == 0), stop=(k == KC - 1))
                last.then_inc(rt_mm, 1)
            pe.wait_ge(ld_b, 32)
            for m in range(4):
                last = tr(ps[:, 3, P * m:P * m + P], z[:, 16, P * m:P * m + P], ident[:, :])
            last.then_inc(b1_mm, 1)
            pe.wait_ge(rt_sel, 2)
            mm(ps[:, 1, 0:NE], upper[:, 0, :], route[:, 0, 3, :], start=True, stop=True)
            mm(ps[:, 1, NE:2 * NE], upper[:, 1, :], route[:, 0, 3, :], start=True, stop=False)
            mm(ps[:, 1, NE:2 * NE], upper[:, 0, :], route[:, 1, 3, :], start=False, stop=True)
            for k in range(3):
                for tt in range(TT):
                    last = mm(ps[32 * k:32 * k + 32, 1, 64:65], route[:, tt, 3, :], upper[:, 1, 0:1], start=(tt == 0), stop=(tt == 1))
            last.then_inc(pos_mm, 1)
            pe.wait_ge(flag_ready, 1)
            mm(ps[0:96, 1, 96:97], upper[0:96, 0, 0:96], small[0:96, 41:42], start=True, stop=True).then_inc(flag_mm, 1)
            pe.wait_ge(hot_ready, 1)
            mm(ps[0:1, 1, 128:129], small[0:96, 41:42], upper[0:96, 1, 0:1], start=True, stop=True)
            mm(ps[0:1, 1, 160:176], more_c[:, 1:2], z[0:96, 14, 0:16], start=True, stop=True)
            mm(ps[0:1, 1, 176:192], more_c[:, 0:1], z[0:96, 14, 0:16], start=True, stop=True).then_inc(list_mm, 1)
            pe.wait_ge(h2T_ready, 4)
            for n in range(2):
                mm(ps[:, 4 + n, :], ident[0:NE, :], z[0:NE, 10 + n, :], start=True, stop=True).then_inc(b2_mm, 1)

            pe.wait_ge(parts_ready, 2)
            pe.wait_ge(b1_ready, 1)
            pe.wait_ge(list_ready, 1)
            n_more = pe.value_load(lists_i[0:1, 0:1], min_val=0, max_val=MAX_MORE)
            pe.nop().then_inc(w_free, PARTS)

            def turn_gates(n):
                for tt in range(TT):
                    last = tr(ps[:, 7, P * tt:P * tt + P], pick_g[:, tt, :], ident[:, :])
                last.then_inc(st_mm, 1)

            def gather(n):
                pe.wait_ge(pick_ready, n * 2 + 2)
                for k in range(KC):
                    for tt in range(TT):
                        for part in range(3):
                            last = mm(ps[:, 6, SLOTS * k:SLOTS * k + SLOTS], h_parts[:, tt, part, P * k:P * k + P], pick[:, tt, :],
                                      start=(tt == 0 and part == 0), stop=(tt == 1 and part == 2))
                last.then_inc(gather_mm, 1)

            def into_tokens(g, n):
                if n == 0:
                    pe.wait_ge(ysb_ready, g * 2 + 2)
                    pe.wait_ge(st_ready, g + 1)
                if n >= 2:
                    pe.wait_ge(y_added, g * 4 + (n - 1))
                mm(ps[:, 6 + n % 2, :], st[:, P * (n // 2):P * (n // 2) + P], ysb[:, 512 * (n % 2):512 * (n % 2) + 512],
                   start=True, stop=True).then_inc(sc_mm, 1)

            def body(g):
                def operands(u, stationary):
                    if u in WHOLE:
                        wait_tile(pe, g, u // 2)
                        return [(stationary.bitcast(F32), raw_unit(u))]
                    pe.wait_ge(lo_ready, g * len(SPLIT) + split_count(u))
                    return [(stationary, w_hi[:, u % PARTS, :]), (stationary, w_lo[:, u % PARTS, :])]

                def w1_unit(u):
                    b, k0 = u // 4, 2 * (u % 4)
                    pairs = operands(u, xs[:, k0:k0 + 2, :])
                    for kk in range(2):
                        for n, (x_, w_) in enumerate(pairs):
                            last = mm(ps[:, b % 2, :], x_[:, kk, :], w_[:, 512 * kk:512 * kk + 512],
                                      start=(k0 + kk == 0 and n == 0), stop=(k0 + kk == KC - 1 and n == len(pairs) - 1))
                    last.then_inc(w_free, 1)

                def fold_block(b):
                    pe.wait_ge(hs_ready, g * 4 + (b + 1))
                    if b == 2:
                        pe.wait_ge(t_free, g * 2 + 1)
                    for cch in range(4):
                        last = mm(ps[:, 2 + b % 2, P * cch:P * cch + P], hs[:, b % 2, P * cch:P * cch + P], fold[:, :], start=True, stop=True)
                    last.then_inc(sum_mm, 1)

                def w2_unit(u):
                    fc = u - 16
                    pairs = operands(u, act[:, fc, :])
                    for n, (a_, w_) in enumerate(pairs):
                        for nb in range(2):
                            last = mm(ps[:, 4 + nb, :], a_, w_[:, 512 * nb:512 * nb + 512],
                                      start=(fc == 0 and n == 0), stop=(fc == 7 and n == len(pairs) - 1))
                    last.then_inc(w_free, 1)

                pe.wait_ge(xs_ready, g + 1)
                for u in range(24):
                    if u == 16 or u == 20:
                        pe.wait_ge(act_ready, g * 2 + (u // 4 - 3))
                    if u < 16:
                        w1_unit(u)
                    else:
                        w2_unit(u)
                    if u == 6:
                        into_tokens(g, 0)
                        into_tokens(g, 1)
                    if u == 5:
                        fold_block(0)
                    if u == 9:
                        into_tokens(g, 2)
                        into_tokens(g, 3)
                    if u == 9:
                        fold_block(1)
                    if u == 13:
                        pe.wait_ge(y_added, g * 4 + 4)
                        pe.wait_ge(doubled, g * 4 + 4)
                        turn_gates(g + 1)
                    if u == 14:
                        gather(g + 1)
                    if u == 14:
                        fold_block(2)
                    if u == 16:
                        fold_block(3)

            pe.wait_ge(pickg_ready, 2)
            turn_gates(0)
            gather(0)
            with pe.Fori(0, NE) as i:
                body(i)
            with pe.If(n_more > 0):
                with pe.Fori(0, n_more) as r:
                    body(r + NE)
            for n in range(4):
                into_tokens(n_more + NE, n)


_INS = ["x", "c", "w_ada", "b_ada", "norm_mix_w", "w_in", "hgrn_lb_logits", "hgrn_norm_w", "rel_bias",
        "w_proj_a", "w_proj_b", "w_out", "norm_ffn_w", "w_router", "b_router", "w_mlp1", "b_mlp1",
        "w_mlp2", "b_mlp2", "final_norm_w"]


def constants():
    import math
    import numpy as np

    f = np.float32
    ident = np.eye(128, dtype=f)
    half = np.arange(128) % 64
    fold = (half[:, None] == half[None, :]).astype(f)
    dist = 255 - np.arange(256)
    large = 16 + (np.log(np.maximum(dist, 1).astype(f) / f(16)) / f(math.log(8)) * f(16)).astype(np.int32)
    bucket = np.where(dist < 16, dist, np.minimum(large, 31))
    hot = np.zeros((32, 384), f)
    hot[bucket, np.arange(256)] = 1
    s, t = np.arange(128)[:, None], np.arange(128)[None, :]
    masks = [(s // (2 * m) == t // (2 * m)) & (s % (2 * m) < m) & (t % (2 * m) >= m) for m in HALVES]
    masks = np.stack(masks + [s == t], 1).astype(f).reshape(128, 8 * 128)
    iota = np.broadcast_to(np.arange(256, dtype=f), (128, 256)).copy()
    upper = np.concatenate([(s < t).astype(f), np.ones((128, 128), f)], 1)
    q = np.arange(96)
    more = np.stack([64 * (q // 32 + 1), q % 32, q // 32 + 1, 0 * q], 1).astype(f)
    n = 32 + MAX_MORE + 1
    items = np.zeros((1, 2 * n + 1), f)
    items[0, 1:33] = np.arange(32)
    return {"k_ident": ident, "k_fold": fold, "k_bucket": hot, "k_masks": masks, "k_iota": iota,
            "k_upper": upper, "k_more": more, "k_items": items}


def kernel(**inputs):
    import numpy as np
    import concourse.bacc as bacc
    from concourse.bass_utils import run_bass_kernel_spmd

    nc = bacc.Bacc("TRN2", target_bir_lowering=False, num_devices=1)
    arrays, args = {}, []
    for name, a in [(n, inputs[n]) for n in _INS] + list(constants().items()):
        a = np.ascontiguousarray(a)
        arrays[f"in_{name}_dram"] = a
        args.append(nc.dram_tensor(f"in_{name}_dram", a.shape, mybir.dt.from_np(a.dtype), kind="ExternalInput").ap())
    out = nc.dram_tensor("out_0_dram", (1, 256, 1024), F32, kind="ExternalOutput").ap()
    build(nc, *args, out)
    r = run_bass_kernel_spmd(nc, [arrays], core_ids=[0])
    return r.results[0]["out_0_dram"]
```
